# Optimizing a Trainium2 kernel written in Bass

```python
import numpy as np
import jax
import jax.numpy as jnp
from jax import lax

D_MODEL = 1024
BATCH = 1
SEQ = 256
DEPTH = 2

HEAD_DIM = 64
ROPE_THETA = 10000.0
NORM_EPS = 1e-6
TINY = 1e-30
N_BRANCH = 4

MOBA_HEADS = 8
MOBA_BLOCK = 256
MOBA_TOPK = 3
MOBA_QCHUNK = 8

SWA_HEADS = 8
SWA_KV_HEADS = 2
SWA_WINDOW = 128
SWA_QBLOCK = 128

RET_HEADS = 4
RET_QK_DIM = 64
RET_V_DIM = 128
RET_CHUNK = 128

NSA_HEADS = 8
NSA_KV_HEADS = 2
NSA_CMP_LEN = 32
NSA_CMP_STRIDE = 16
NSA_CMP_HIDDEN = 256
NSA_SLC_BLOCK = 64
NSA_SLC_TOPN = 16
NSA_WINDOW = 512
NSA_QCHUNK = 16
NSA_WIN_QBLOCK = 128

MOBA_W = MOBA_HEADS * HEAD_DIM
SWA_W = SWA_HEADS * HEAD_DIM
SWA_KV_W = SWA_KV_HEADS * HEAD_DIM
RET_QK_W = RET_HEADS * RET_QK_DIM
RET_W = RET_HEADS * RET_V_DIM
NSA_W = NSA_HEADS * HEAD_DIM
NSA_KV_W = NSA_KV_HEADS * HEAD_DIM
BRANCH_WIDTHS = (MOBA_W, SWA_W, RET_W, NSA_W)
D_BRANCH = MOBA_W + SWA_W + RET_W + NSA_W

IN_SPLITS = (
    ('moba_q', MOBA_W), ('moba_k', MOBA_W), ('moba_v', MOBA_W), ('moba_z', MOBA_W),
    ('swa_q', SWA_W), ('swa_k', SWA_KV_W), ('swa_v', SWA_KV_W), ('swa_z', SWA_W),
    ('ret_q', RET_QK_W), ('ret_k', RET_QK_W), ('ret_v', RET_W), ('ret_z', RET_W),
    ('nsa_q', NSA_W), ('nsa_kc', NSA_KV_W), ('nsa_vc', NSA_KV_W),
    ('nsa_ks', NSA_KV_W), ('nsa_vs', NSA_KV_W), ('nsa_kw', NSA_KV_W), ('nsa_vw', NSA_KV_W),
    ('nsa_g', 3 * NSA_HEADS), ('nsa_z', NSA_W),
    ('merge_g', N_BRANCH * D_MODEL),
)
D_IN = sum(w for _, w in IN_SPLITS)

kernel_name = 'hybrid_gated_moba_swa_retention_nsa'

def rms_norm(x, g):
    xf = x.astype(jnp.float32)
    y = xf * lax.rsqrt(jnp.mean(xf * xf, axis=-1, keepdims=True) + NORM_EPS)
    return (y * g.astype(jnp.float32)).astype(x.dtype)

def rope_tables(seq):
    inv = 1.0 / (ROPE_THETA ** (jnp.arange(0, HEAD_DIM, 2, dtype=jnp.float32) / HEAD_DIM))
    ang = jnp.arange(seq, dtype=jnp.float32)[:, None] * inv[None, :]
    return jnp.cos(ang), jnp.sin(ang)

def apply_rope(t, cos, sin):
    half = t.shape[-1] // 2
    t1 = t[..., :half].astype(jnp.float32)
    t2 = t[..., half:].astype(jnp.float32)
    return jnp.concatenate([t1 * cos - t2 * sin, t2 * cos + t1 * sin], axis=-1).astype(t.dtype)

def split_cols(h):
    cols = {}
    off = 0
    for name, width in IN_SPLITS:
        cols[name] = h[..., off:off + width]
        off += width
    return cols

def to_heads(t, n):
    b, s, _ = t.shape
    return t.reshape(b, s, n, -1).transpose(0, 2, 1, 3)

def to_gqa(t, n_kv, n_grp):
    b, s, _ = t.shape
    return t.reshape(b, s, n_kv, n_grp, -1).transpose(0, 2, 3, 1, 4)

def from_heads(o):
    b, h, s, d = o.shape
    return o.transpose(0, 2, 1, 3).reshape(b, s, h * d)

def from_gqa(o):
    b, hk, g, s, d = o.shape
    return o.transpose(0, 3, 1, 2, 4).reshape(b, s, hk * g * d)

def masked_softmax(s, mask, sink=None):
    s = jnp.where(mask, s, -jnp.inf)
    m = jnp.max(s, axis=-1, keepdims=True)
    if sink is not None:
        m = jnp.maximum(m, sink)
    m = jnp.where(jnp.isfinite(m), m, 0.0)
    e = jnp.exp(s - m)
    den = jnp.sum(e, axis=-1, keepdims=True)
    if sink is not None:
        den = den + jnp.exp(sink - m)
    return e / jnp.maximum(den, TINY)

def banded_attention(q, k, v, window, qblock, sink=None):
    b, hk, g, s, dh = q.shape
    scale = dh ** -0.5
    n_pre = -(-(window - 1) // qblock) * qblock
    span = n_pre + qblock
    kp = jnp.pad(k, ((0, 0), (0, 0), (n_pre, 0), (0, 0)))
    vp = jnp.pad(v, ((0, 0), (0, 0), (n_pre, 0), (0, 0)))
    nqb = s // qblock
    qb = q.reshape(b, hk, g, nqb, qblock, dh).transpose(3, 0, 1, 2, 4, 5)

    def one_block(args):
        i, qi = args
        start = i * qblock
        ks = lax.dynamic_slice_in_dim(kp, start, span, axis=2)
        vs = lax.dynamic_slice_in_dim(vp, start, span, axis=2)
        t = start + jnp.arange(qblock)
        p = start - n_pre + jnp.arange(span)
        dist = t[:, None] - p[None, :]
        mask = (dist >= 0) & (dist < window) & (p[None, :] >= 0)
        sc = jnp.einsum('bhgqd,bhkd->bhgqk', qi, ks, preferred_element_type=jnp.float32) * scale
        pr = masked_softmax(sc, mask, sink)
        return jnp.einsum('bhgqk,bhkd->bhgqd', pr.astype(v.dtype), vs)

    out = lax.map(one_block, (jnp.arange(nqb), qb))
    return out.transpose(1, 2, 3, 0, 4, 5).reshape(b, hk, g, s, dh)

def moba_mixer(q, k, v, cos, sin):
    b, s, _ = q.shape
    hq, dh, blk = MOBA_HEADS, HEAD_DIM, MOBA_BLOCK
    scale = dh ** -0.5
    qh = apply_rope(to_heads(q, hq), cos, sin)
    kh = apply_rope(to_heads(k, hq), cos, sin)
    vh = to_heads(v, hq)
    nb = -(-s // blk)
    pad = nb * blk - s
    kb = jnp.pad(kh, ((0, 0), (0, 0), (0, pad), (0, 0))).reshape(b, hq, nb, blk, dh)
    vb = jnp.pad(vh, ((0, 0), (0, 0), (0, pad), (0, 0))).reshape(b, hq, nb, blk, dh)
    t = jnp.arange(s)
    gate = jnp.einsum('bhsd,bhnd->bhsn', qh, jnp.mean(kb, axis=3), preferred_element_type=jnp.float32)
    gate = jnp.where(jnp.arange(nb)[None, :] < (t // blk)[:, None], gate, -jnp.inf)
    n_sel = min(MOBA_TOPK, nb)
    _, sel = lax.top_k(gate, n_sel)
    qc_n = MOBA_QCHUNK
    nqc = s // qc_n
    q_ch = qh.reshape(b, hq, nqc, qc_n, dh).transpose(2, 0, 1, 3, 4)
    sel_ch = sel.reshape(b, hq, nqc, qc_n, n_sel).transpose(2, 0, 1, 3, 4)
    bi = jnp.arange(b)[:, None, None, None]
    hi = jnp.arange(hq)[None, :, None, None]

    def chunk(args):
        ci, qc, ic = args
        tc = ci * qc_n + jnp.arange(qc_n)
        own = (ci * qc_n) // blk
        kg = kb[bi, hi, ic]
        vg = vb[bi, hi, ic]
        ko = lax.dynamic_index_in_dim(kb, own, axis=2, keepdims=False)
        vo = lax.dynamic_index_in_dim(vb, own, axis=2, keepdims=False)
        s_sel = jnp.einsum('bhqd,bhqnkd->bhqnk', qc, kg, preferred_element_type=jnp.float32)
        s_own = jnp.einsum('bhqd,bhkd->bhqk', qc, ko, preferred_element_type=jnp.float32)
        sc = jnp.concatenate([s_sel.reshape(b, hq, qc_n, n_sel * blk), s_own], axis=-1) * scale
        sel_ok = jnp.repeat(jnp.arange(n_sel) < own, blk)
        own_ok = (own * blk + jnp.arange(blk))[None, :] <= tc[:, None]
        mask = jnp.concatenate([jnp.broadcast_to(sel_ok[None, :], (qc_n, n_sel * blk)), own_ok], axis=-1)
        pr = masked_softmax(sc, mask).astype(v.dtype)
        o = jnp.einsum('bhqnk,bhqnkd->bhqd', pr[..., :n_sel * blk].reshape(b, hq, qc_n, n_sel, blk), vg)
        return o + jnp.einsum('bhqk,bhkd->bhqd', pr[..., n_sel * blk:], vo)

    out = lax.map(chunk, (jnp.arange(nqc), q_ch, sel_ch))
    return from_heads(out.transpose(1, 2, 0, 3, 4).reshape(b, hq, s, dh))

def swa_mixer(q, k, v, sink, cos, sin):
    grp = SWA_HEADS // SWA_KV_HEADS
    qh = apply_rope(to_gqa(q, SWA_KV_HEADS, grp), cos, sin)
    kh = apply_rope(to_heads(k, SWA_KV_HEADS), cos, sin)
    vh = to_heads(v, SWA_KV_HEADS)
    sink_logit = sink.astype(jnp.float32).reshape(1, SWA_KV_HEADS, grp, 1, 1)
    return from_gqa(banded_attention(qh, kh, vh, SWA_WINDOW, SWA_QBLOCK, sink_logit))

def retention_mixer(q, k, v, cos, sin):
    b, s, _ = q.shape
    f32 = jnp.float32
    c = RET_CHUNK
    nc = s // c
    qh = apply_rope(to_heads(q, RET_HEADS), cos, sin).astype(f32)
    kh = apply_rope(to_heads(k, RET_HEADS), cos, sin).astype(f32) * (RET_QK_DIM ** -0.5)
    vh = to_heads(v, RET_HEADS).astype(f32)
    log_g = jnp.log(1.0 - 2.0 ** (-5.0 - jnp.arange(RET_HEADS, dtype=f32)))
    idx = jnp.arange(c, dtype=f32)
    diff = idx[:, None] - idx[None, :]
    intra = jnp.where(diff >= 0, jnp.exp(jnp.maximum(diff, 0.0) * log_g[:, None, None]), 0.0)
    q_dec = jnp.exp((idx + 1.0) * log_g[:, None])[None, :, :, None]
    k_dec = jnp.exp((c - 1.0 - idx) * log_g[:, None])[None, :, :, None]
    chunk_dec = jnp.exp(c * log_g)[None, :, None, None]

    def chunks(t):
        return t.reshape(b, RET_HEADS, nc, c, -1).transpose(2, 0, 1, 3, 4)

    def step(state, xs):
        qc, kc, vc = xs
        att = jnp.einsum('bhqd,bhkd->bhqk', qc, kc) * intra
        o = jnp.einsum('bhqk,bhke->bhqe', att, vc) + jnp.einsum('bhqd,bhde->bhqe', qc, state) * q_dec
        state = state * chunk_dec + jnp.einsum('bhkd,bhke->bhde', kc * k_dec, vc)
        return state, o

    state0 = jnp.zeros((b, RET_HEADS, RET_QK_DIM, RET_V_DIM), f32)
    _, o = lax.scan(step, state0, (chunks(qh), chunks(kh), chunks(vh)))
    o = o.transpose(1, 2, 0, 3, 4).reshape(b, RET_HEADS, s, RET_V_DIM)
    mu = jnp.mean(o, axis=-1, keepdims=True)
    var = jnp.mean(jnp.square(o - mu), axis=-1, keepdims=True)
    o = (o - mu) * lax.rsqrt(var + NORM_EPS)
    return from_heads(o).astype(q.dtype)

def nsa_overlap_matrix(n_cmp, n_slc):
    c0 = np.arange(n_cmp)[:, None] * NSA_CMP_STRIDE
    s0 = np.arange(n_slc)[None, :] * NSA_SLC_BLOCK
    ov = np.minimum(c0 + NSA_CMP_LEN, s0 + NSA_SLC_BLOCK) - np.maximum(c0, s0)
    return jnp.asarray(np.clip(ov, 0, None) / NSA_CMP_LEN, dtype=jnp.float32)

def nsa_mixer(q, kc, vc, ks, vs, kw, vw, g, cmp_pos, w_ck1, w_ck2, w_cv1, w_cv2, cos, sin):
    b, s, _ = q.shape
    hk = NSA_KV_HEADS
    grp = NSA_HEADS // NSA_KV_HEADS
    dh = HEAD_DIM
    scale = dh ** -0.5
    t = jnp.arange(s)
    qh = apply_rope(to_gqa(q, hk, grp), cos, sin)

    n_cmp = (s - NSA_CMP_LEN) // NSA_CMP_STRIDE + 1
    blk_idx = jnp.arange(n_cmp)[:, None] * NSA_CMP_STRIDE + jnp.arange(NSA_CMP_LEN)[None, :]
    cmp_end = jnp.arange(n_cmp) * NSA_CMP_STRIDE + NSA_CMP_LEN - 1

    def compress(tok, w1, w2):
        blocks = to_heads(tok, hk)[:, :, blk_idx] + cmp_pos
        flat = blocks.reshape(b, hk, n_cmp, NSA_CMP_LEN * dh)
        return jax.nn.gelu(flat @ w1) @ w2

    k_cmp = apply_rope(compress(kc, w_ck1, w_ck2), cos[cmp_end], sin[cmp_end])
    v_cmp = compress(vc, w_cv1, w_cv2)
    s_c = jnp.einsum('bhgqd,bhnd->bhgqn', qh, k_cmp, preferred_element_type=jnp.float32) * scale
    p_c = masked_softmax(s_c, cmp_end[None, :] <= t[:, None])
    o_cmp = jnp.einsum('bhgqn,bhnd->bhgqd', p_c.astype(v_cmp.dtype), v_cmp)

    n_slc = s // NSA_SLC_BLOCK
    top_n = min(NSA_SLC_TOPN, n_slc)
    imp = jnp.einsum('bhgqn,nj->bhqj', p_c, nsa_overlap_matrix(n_cmp, n_slc))
    q_blk = t // NSA_SLC_BLOCK
    j = jnp.arange(n_slc)[None, :]
    forced = (j == 0) | (j == q_blk[:, None]) | (j == q_blk[:, None] - 1)
    imp = jnp.where(forced, jnp.inf, imp)
    imp = jnp.where(j <= q_blk[:, None], imp, -jnp.inf)
    _, sel = lax.top_k(imp, top_n)
    ksb = apply_rope(to_heads(ks, hk), cos, sin).reshape(b, hk, n_slc, NSA_SLC_BLOCK, dh)
    vsb = to_heads(vs, hk).reshape(b, hk, n_slc, NSA_SLC_BLOCK, dh)
    qc_n = NSA_QCHUNK
    nqc = s // qc_n
    q_ch = qh.reshape(b, hk, grp, nqc, qc_n, dh).transpose(3, 0, 1, 2, 4, 5)
    sel_ch = sel.reshape(b, hk, nqc, qc_n, top_n).transpose(2, 0, 1, 3, 4)
    bi = jnp.arange(b)[:, None, None, None]
    hi = jnp.arange(hk)[None, :, None, None]
    kpos = jnp.arange(NSA_SLC_BLOCK)
    n_keys = top_n * NSA_SLC_BLOCK

    def sel_chunk(args):
        ci, qc, ic = args
        tc = ci * qc_n + jnp.arange(qc_n)
        kg = ksb[bi, hi, ic]
        vg = vsb[bi, hi, ic]
        sc = jnp.einsum('bhgqd,bhqnkd->bhgqnk', qc, kg, preferred_element_type=jnp.float32) * scale
        key_pos = ic[..., None] * NSA_SLC_BLOCK + kpos
        rank_ok = jnp.arange(top_n)[None, :] <= (tc // NSA_SLC_BLOCK)[:, None]
        ok = (key_pos <= tc[None, None, :, None, None]) & rank_ok[None, None, :, :, None]
        pr = masked_softmax(sc.reshape(b, hk, grp, qc_n, n_keys), ok.reshape(b, hk, 1, qc_n, n_keys))
        pr = pr.reshape(b, hk, grp, qc_n, top_n, NSA_SLC_BLOCK).astype(vg.dtype)
        return jnp.einsum('bhgqnk,bhqnkd->bhgqd', pr, vg)

    o_slc = lax.map(sel_chunk, (jnp.arange(nqc), q_ch, sel_ch))
    o_slc = o_slc.transpose(1, 2, 3, 0, 4, 5).reshape(b, hk, grp, s, dh)

    kwh = apply_rope(to_heads(kw, hk), cos, sin)
    o_win = banded_attention(qh, kwh, to_heads(vw, hk), NSA_WINDOW, NSA_WIN_QBLOCK)

    gates = jax.nn.sigmoid(g).reshape(b, s, 3, hk, grp).transpose(2, 0, 3, 4, 1)[..., None]
    o = gates[0] * o_cmp + gates[1] * o_slc + gates[2] * o_win
    return from_gqa(o)

def hybrid_layer(x, cos, sin, norm_g, w_in, w_branch, w_out, swa_sink, cmp_pos, w_ck1, w_ck2, w_cv1, w_cv2):
    b, s, d = x.shape
    h = rms_norm(x, norm_g)
    c = split_cols(h @ w_in)
    silu = jax.nn.silu
    outs = (
        moba_mixer(c['moba_q'], c['moba_k'], c['moba_v'], cos, sin) * silu(c['moba_z']),
        swa_mixer(c['swa_q'], c['swa_k'], c['swa_v'], swa_sink, cos, sin) * silu(c['swa_z']),
        retention_mixer(c['ret_q'], c['ret_k'], c['ret_v'], cos, sin) * silu(c['ret_z']),
        nsa_mixer(c['nsa_q'], c['nsa_kc'], c['nsa_vc'], c['nsa_ks'], c['nsa_vs'], c['nsa_kw'], c['nsa_vw'],
                  c['nsa_g'], cmp_pos, w_ck1, w_ck2, w_cv1, w_cv2, cos, sin) * silu(c['nsa_z']),
    )
    gates = jax.nn.sigmoid(c['merge_g']).reshape(b, s, N_BRANCH, d)
    merged = jnp.zeros_like(x)
    row = 0
    for i in range(N_BRANCH):
        width = BRANCH_WIDTHS[i]
        merged = merged + gates[:, :, i] * (outs[i] @ w_branch[row:row + width])
        row += width
    return x + merged @ w_out

def setup_inputs(seed: int = 0) -> dict:
    key = jax.random.key(seed)
    ks = jax.random.split(key, 12)
    f32 = jnp.float32
    l_dh = NSA_CMP_LEN * HEAD_DIM

    def nrm(k, shape, scale):
        return scale * jax.random.normal(k, shape, f32)

    return {
        'x': nrm(ks[0], (BATCH, SEQ, D_MODEL), 1.0),
        'norm_g': 1.0 + nrm(ks[1], (DEPTH, D_MODEL), 0.02),
        'w_in': nrm(ks[2], (DEPTH, D_MODEL, D_IN), D_MODEL ** -0.5),
        'w_branch': nrm(ks[3], (DEPTH, D_BRANCH, D_MODEL), MOBA_W ** -0.5),
        'w_out': nrm(ks[4], (DEPTH, D_MODEL, D_MODEL), D_MODEL ** -0.5),
        'swa_sink': nrm(ks[5], (DEPTH, SWA_HEADS), 0.5),
        'nsa_cmp_pos': nrm(ks[6], (DEPTH, NSA_CMP_LEN, HEAD_DIM), 0.1),
        'nsa_w_ck1': nrm(ks[7], (DEPTH, l_dh, NSA_CMP_HIDDEN), l_dh ** -0.5),
        'nsa_w_ck2': nrm(ks[8], (DEPTH, NSA_CMP_HIDDEN, HEAD_DIM), NSA_CMP_HIDDEN ** -0.5),
        'nsa_w_cv1': nrm(ks[9], (DEPTH, l_dh, NSA_CMP_HIDDEN), l_dh ** -0.5),
        'nsa_w_cv2': nrm(ks[10], (DEPTH, NSA_CMP_HIDDEN, HEAD_DIM), NSA_CMP_HIDDEN ** -0.5),
        'final_norm_g': 1.0 + nrm(ks[11], (D_MODEL,), 0.02),
    }

def reference(x, norm_g, w_in, w_branch, w_out, swa_sink, nsa_cmp_pos, nsa_w_ck1, nsa_w_ck2,
              nsa_w_cv1, nsa_w_cv2, final_norm_g):
    cos, sin = rope_tables(x.shape[1])
    for l in range(DEPTH):
        x = hybrid_layer(x, cos, sin, norm_g[l], w_in[l], w_branch[l], w_out[l], swa_sink[l],
                         nsa_cmp_pos[l], nsa_w_ck1[l], nsa_w_ck2[l], nsa_w_cv1[l], nsa_w_cv2[l])
    return rms_norm(x, final_norm_g)


_drawn_inputs = setup_inputs


def setup_inputs(seed=0):
    import zlib

    import numpy as np

    out = dict(_drawn_inputs(seed))
    spreads = {}
    factors = {'norm_g': 2.716, 'swa_sink': 8.0, 'nsa_cmp_pos': 4.621, 'final_norm_g': 2.824}
    for name, (base, spread) in spreads.items():
        noise = np.random.default_rng([zlib.crc32(name.encode()), seed]).standard_normal(out[name].shape)
        drawn = base * np.exp(spread * noise) if base else spread * noise
        out[name] = jnp.asarray(drawn.astype(out[name].dtype))
    for name, factor in factors.items():
        out[name] = (out[name] * factor).astype(out[name].dtype)
    return out
```

```python
from contextlib import ExitStack

import concourse.bass as bass
from concourse import mybir

F32 = mybir.dt.float32
F32R = mybir.dt.float32r
BF16 = mybir.dt.bfloat16
ALU = mybir.AluOpType
ACT = mybir.ActivationFunctionType
AX = mybir.AxisListType

P = 128
D = 1024
KD = D // P
SEQ = 256
NT = SEQ // P
LAYERS = 2
HD = 64
HEADS = 8
W = HEADS * HD
CW = 512
UNIT_K = 4
UNIT = UNIT_K * CW
NCMP = 15
EPS = 1e-6
TINY = 1e-30

MQ, MK, MV, MZ = 0, 512, 1024, 1536
SQ, SK, SV, SZ = 2048, 2560, 2688, 2816
RQ, RK, RV, RZ = 3328, 3584, 3840, 4352
NQ, KC, VC, KS, VS, KW, VW = 4864, 5376, 5504, 5632, 5760, 5888, 6016
NG, NZ, MG = 6144, 6168, 6680
D_IN = MG + 4 * D
ZCOL = (MZ, SZ, RZ, NZ)
CHUNKS = MG // CW
TAIL = MG - CHUNKS * CW

U_TAIL, U_CMP, U_MERGE, U_BRANCH, U_OUT, UNITS = 26, 28, 32, 48, 56, 60
N_TAIL, N_MERGE, N_BRANCH, N_OUT, SPLITS = 26, 28, 44, 52, 56

C_ID, C_COS, C_SIN, C_DECAY = 0, 128, 384, 640
C_CADD, C_C01, C_BLK, C_COSK, C_SINK = 2176, 2206, 2236, 2238, 2302
N_CONST = 2366


ONE = 1


class Count:

    def __init__(self):
        self.base, self.n = 0, 0

    def at(self, base):
        self.base, self.n = base, 0

    def next(self):
        self.n += 1
        return self.base + self.n


ACC_ACT, ACC_DVE = 22, 16
DVE_PREP, DVE_TURN = 14, 37
POOL_PREP, POOL_TURN = 9, 21


def hybrid_trunk(nc, x, norm_g, w_in, w_branch, w_out, swa_sink, cmp_pos, w_ck1, w_ck2, w_cv1, w_cv2,
                 final_norm_g, consts, masks, out):
    with ExitStack() as ctx:
        top = [(nc.sbuf_base + 31) // 32 * 32]

        def at(name, shape, dt, offset):
            return nc.alloc_sbuf_tensor_at(name, shape, dt, offset=offset)

        def sb(name, shape, dt=F32):
            size = 2 if dt == BF16 else 4
            for n in shape[1:]:
                size *= n
            t = at(name, shape, dt, top[0])
            top[0] += (size + 31) // 32 * 32
            return t

        def sem(name):
            return ctx.enter_context(nc.semaphore(name))

        x_sb = sb("x_sb", [P, NT, D])
        hT_hi = sb("hT_hi", [P, KD, SEQ], F32R)
        hT_lo = sb("hT_lo", [P, KD, SEQ], F32R)
        raw = sb("raw", [P, 2, UNIT])
        w_hi = sb("w_hi", [P, 2, UNIT], F32R)
        w_lo = sb("w_lo", [P, 2, UNIT], F32R)
        proj_at = top[0]
        proj = sb("proj", [P, NT, MG])
        gates_at = top[0]
        gates = sb("gates", [P, NT, 4 * D])
        merged = gates[:, :, 0:D]
        con = sb("con", [P, N_CONST])
        ident = con[:, C_ID:C_ID + P]
        ident_b = sb("ident_b", [P, P], BF16)
        mask_b = sb("mask_b", [P, 2, 384], BF16)
        small = sb("small", [P, 8])
        neg_half = sb("neg_half", [P, NT])
        sink_in = sb("sink_in", [P, LAYERS * HEADS])
        sink = sb("sink", [P, LAYERS * HEADS, 2])
        nsink = sb("nsink", [P, LAYERS * HEADS, 2])
        nsa_g = sb("nsa_g", [P, NT, 24])
        pos_in = sb("pos_in", [16, P])
        kT_shared = sb("kT_shared", [HD, 3, 2, SEQ])
        kcT = sb("kcT", [HD, 2, NCMP])
        v_blk = sb("v_blk", [2 * NCMP, 2, P])
        tmp_rope = sb("tmp_rope", [P, NT, P])

        roped = sb("roped", [P, 5, NT, P])
        qkT_at = top[0]
        qkT = sb("qkT", [HD, 5, 2, SEQ])
        probs = sb("probs", [P, 2, 384])
        probsT = sb("probsT", [P, 2, 384])
        attT = sb("attT", [P, 384])
        zg = sb("zg", [P, 4, NT, P])
        nsa_sum = sb("nsa_sum", [P, NT, P])
        stat = sb("stat", [P, 4, 12])
        cmp_s = sb("cmp_s", [P, 4, NCMP])
        cmp_st = sb("cmp_st", [P, 4, 4])
        cmp_pT = sb("cmp_pT", [2 * NCMP, SEQ])
        ret_st = sb("ret_st", [P, 20])
        assert top[0] <= nc.sbuf_usable_end, (top[0], nc.sbuf_usable_end)

        g0 = gates_at + 1024 * 4
        g1 = gates_at + 5120 * 4
        h = at("h", [P, NT, D], F32, g0)
        k_shared = at("k_shared", [P, NT, 3, P], F32, g0 + 8192)
        g_row = at("g_row", [P, D], F32, g1)
        mask_f = at("mask_f", [P, 2 * 384], F32, g1 + 4096)
        dup = at("dup", [P, NT, 4, 2, HD], F32, g0)
        pairT = at("pairT", [P, 4, P], F32, g0 + 4096)
        blocksT = at("blocksT", [P, 2, 16, 2 * NCMP], F32, g0 + 6144)
        hid = at("hid", [2 * NCMP, 2 * 256], F32, g1)
        hid2 = at("hid2", [2 * NCMP, 2 * 256], F32, g1 + 2048)
        hid3 = at("hid3", [2 * NCMP, 2 * 256], F32, g1 + 4096)
        gkT = at("gkT", [P, 2, 2 * NCMP], F32, g1 + 6144)
        gvT = at("gvT", [P, 2, 2, 2, NCMP], F32, g1 + 6144 + 256)
        posT = at("posT", [P, 16], F32, g1 + 7168)
        kc_s = at("kc_s", [2 * NCMP, HD], F32, g1 + 7168 + 64)
        kc_t = at("kc_t", [2 * NCMP, HD], F32, g1 + 7168 + 320)
        kc_r = at("kc_r", [2 * NCMP, HD], F32, g1 + 7168 + 576)
        w_c2 = at("w_c2", [P, 2, 2, HD], F32, g1 + 8192)
        spots = [proj_at + 4 * (t * MG + c) for t in range(NT) for c in (0, 512, 1024, 2048, 3328, 3840, 4864, 5376)]
        yT_hi = [at(f"yT_hi{g}", [P, 2, SEQ], F32R, spots[g]) for g in range(8)]
        yT_lo = [at(f"yT_lo{g}", [P, 2, SEQ], F32R, spots[8 + g]) for g in range(8)]
        part = at("part", [P, NT, CW], F32, qkT_at)

        acc = [ctx.enter_context(nc.psum_tensor(f"acc{i}", [P, CW], F32)) for i in range(4)]
        score = [ctx.enter_context(nc.psum_tensor(f"score{i}", [P, CW], F32)) for i in range(2)]
        tbank = ctx.enter_context(nc.psum_tensor("tbank", [P, CW], F32))
        obank = ctx.enter_context(nc.psum_tensor("obank", [P, CW], F32))
        xbank = [score[0], score[1], tbank, obank]

        s_x = sem("s_x")
        s_con = sem("s_con")
        s_mask = sem("s_mask")
        s_sink = sem("s_sink")
        s_g = sem("s_g")
        s_pos = sem("s_pos")
        s_c2 = sem("s_c2")
        s_out = sem("s_out")
        raw_full = [sem("raw_full0"), sem("raw_full1")]
        hi_done = sem("hi_done")
        lo_done = sem("lo_done")
        w_used = sem("w_used")
        cmp_used = sem("cmp_used")
        acc_act = sem("acc_act")
        acc_dve = sem("acc_dve")
        sq_done = sem("sq_done")
        h_done = sem("h_done")
        x_full = sem("x_full")
        x_hi = sem("x_hi")
        x_lo = sem("x_lo")
        setup_done = sem("setup_done")
        dve_step = sem("dve_step")
        pool_step = sem("pool_step")
        rstd_norm = sem("rstd_norm")
        var_norm = sem("var_norm")
        keys_roped = sem("keys_roped")
        keys_T = sem("keys_T")
        keys_out = sem("keys_out")
        dup_done = sem("dup_done")
        dup_T = sem("dup_T")
        blocks_done = sem("blocks_done")
        hid_sb = sem("hid_sb")
        hid_tanh = sem("hid_tanh")
        gelu_done = sem("gelu_done")
        gelu_T = sem("gelu_T")
        gelu_out = sem("gelu_out")
        cmp_kv = sem("cmp_kv")
        cmp_roped = sem("cmp_roped")
        kcT_full = sem("kcT_full")
        cmp_ready = sem("cmp_ready")
        tail_tanh = sem("tail_tanh")
        gates_nsa = sem("gates_nsa")
        q_roped = sem("q_roped")
        tq_done = sem("tq_done")
        t_full = sem("t_full")
        t_free = sem("t_free")
        s_full = sem("s_full")
        max_done = sem("max_done")
        exp_done = sem("exp_done")
        sink_exp = sem("sink_exp")
        s_dve = sem("s_dve")
        att_done = sem("att_done")
        cmp_sub = sem("cmp_sub")
        cmp_exp = sem("cmp_exp")
        cmp_p = sem("cmp_p")
        o_full = sem("o_full")
        o_free = sem("o_free")
        z_tanh = sem("z_tanh")
        z_done = sem("z_done")
        y_done = sem("y_done")
        var_ret = sem("var_ret")
        rstd_ret = sem("rstd_ret")
        part_full = sem("part_full")
        part_added = sem("part_added")
        first_part = sem("first_part")
        y_final = sem("y_final")

        w_in_v = w_in.rearrange("l (h k p) n -> l h p k n", k=UNIT_K, p=P)
        w_br_v = w_branch.rearrange("l (i k p) n -> l i p k n", k=UNIT_K, p=P)
        w_out_v = w_out.rearrange("l (h k p) n -> l h p k n", k=UNIT_K, p=P)
        w_k1_v = w_ck1.rearrange("l (h k p) n -> l h p k n", k=8, p=P)
        w_v1_v = w_cv1.rearrange("l (h k p) n -> l h p k n", k=8, p=P)

        def slot4(buf, u):
            return buf[:, u % 2, :].rearrange("p (k n) -> p k n", k=UNIT_K)

        def slot8(buf, u):
            return buf[:, u % 2, :].rearrange("p (k n) -> p k n", k=8)

        ITEMS = [("ret", 0), ("moba", 0), ("swa", 0), ("cmp", 0), ("slc", 0), ("win", 0),
                 ("moba", 1), ("swa", 1), ("slc", 1), ("win", 1)]
        SOFT = {k: e for e, k in enumerate([1, 2, 4, 5, 6, 7, 8, 9])}
        SOFT_K = list(SOFT)
        S_AT, P_AT, O_AT, SLOTS = 3, 5, 6, 16
        KIND = {"moba": 1, "swa": 3, "slc": 4, "win": 4}
        VCOL = {"moba": MV, "swa": SV, "slc": VS, "win": VW}
        KEYS = {"swa": 0, "slc": 1, "win": 2}
        T_FILLS = 5 + 9

        def settle(eng):
            eng.nop(nofuse=True)

        block = ctx.enter_context(nc.Block())

        @block.sync
        def _(sp):
            sp.dma_start(x_sb[:, :, :], x[0].rearrange("(t p) d -> p t d", p=P)).then_inc(s_x, 16)
            sp.dma_start(con[:, :], consts).then_inc(s_con, 16)
            sp.dma_start(mask_f[:, :], masks).then_inc(s_mask, 16)
            sp.dma_start(sink_in[:, :], swa_sink.rearrange("l h -> (l h)").partition_broadcast(P)).then_inc(s_sink, 16)

            def load(src, dst, u, l):
                sp.dma_start(dst, src).then_inc(raw_full[u % 2], 16)

            with sp.Fori(0, LAYERS) as l:
                sp.wait_ge(x_lo, l * 16 + ONE)
                sp.dma_start(g_row[:, :], norm_g[l].partition_broadcast(P)).then_inc(s_g, 16)
                sp.dma_start(pos_in[:, :], cmp_pos[l].rearrange("(k a) d -> k (a d)", a=2)).then_inc(s_pos, 16)
                with sp.Fori(0, 6) as c:
                    for i in range(4):
                        sp.wait_ge(lo_done, l * SPLITS + c * 4 + (i + 1))
                        load(w_in_v[l, i % 2, :, :, bass.ds(c * 2 * CW + i // 2 * CW, CW)], slot4(raw, i), i, l)
                for i in range(24, 26):
                    sp.wait_ge(lo_done, l * SPLITS + (i + 1))
                    load(w_in_v[l, i % 2, :, :, 12 * CW:13 * CW], slot4(raw, i), i, l)
                for i in range(2):
                    u = U_TAIL + i
                    sp.wait_ge(lo_done, l * SPLITS + (u + 1))
                    load(w_in_v[l, i, :, :, CHUNKS * CW:MG],
                         raw[:, u % 2, 0:UNIT_K * TAIL].rearrange("p (k n) -> p k n", k=UNIT_K), u, l)
                sp.wait_ge(x_lo, l * 16 + (4 + ONE))
                for i, w2 in enumerate((w_ck2, w_cv2)):
                    sp.dma_start(w_c2[:, i, :, :], w2[l].rearrange("(k p) n -> p k n", p=P)).then_inc(s_c2, 16)
                for i in range(4):
                    u = U_CMP + i
                    if i < 2:
                        sp.wait_ge(lo_done, l * SPLITS + (u + 1))
                    else:
                        sp.wait_ge(cmp_used, l * 4 + (i - 1))
                    load((w_k1_v, w_v1_v)[i // 2][l, i % 2], slot8(raw, u), u, l)
                sp.wait_ge(cmp_used, l * 4 + 4)
                settle(sp)
                with sp.Fori(0, 4) as j:
                    for i in range(4):
                        sp.wait_ge(lo_done, l * SPLITS + j * 4 + (N_MERGE + i + 1))
                        load(w_in_v[l, i % 2, :, :, bass.ds(j * 2 * CW + (MG + i // 2 * CW), CW)], slot4(raw, i), i, l)
                for v in range(8):
                    sp.wait_ge(lo_done, l * SPLITS + (N_BRANCH + v + 1))
                    c, i = divmod(v, 4)
                    load(w_br_v[l, i, :, :, c * CW:(c + 1) * CW], slot4(raw, v), v, l)
                for v in range(4):
                    sp.wait_ge(lo_done, l * SPLITS + (N_OUT + v + 1))
                    kh, c = divmod(v, 2)
                    load(w_out_v[l, kh, :, :, c * CW:(c + 1) * CW], slot4(raw, v), v, l)
            sp.wait_ge(x_lo, LAYERS * 16 + ONE)
            sp.dma_start(g_row[:, :], final_norm_g.partition_broadcast(P)).then_inc(s_g, 16)
            sp.wait_ge(y_final, 1)
            sp.dma_start(out[0].rearrange("(t p) d -> p t d", p=P), h[:, :, :]).then_inc(s_out, 16)
            sp.wait_ge(s_out, 16)

        @block.gpsimd
        def _(pool):
            steps = Count()

            def rotate(dst, src):
                cos = con[:, C_COS:C_COS + 2 * P].rearrange("p (t n) -> p t n", t=NT)
                sin = con[:, C_SIN:C_SIN + 2 * P].rearrange("p (t a f n) -> p t a f n", t=NT, a=2, f=2)
                s = src.rearrange("p t (a f n) -> p t a f n", a=2, f=2)
                m = tmp_rope[:, :, :].rearrange("p t (a f n) -> p t a f n", a=2, f=2)
                nc.gpsimd.tensor_tensor(m[:, :, :, 0], s[:, :, :, 1], sin[:, :, :, 0], ALU.mult).then_inc(pool_step, 1)
                steps.next()
                nc.gpsimd.tensor_tensor(m[:, :, :, 1], s[:, :, :, 0], sin[:, :, :, 1], ALU.mult).then_inc(pool_step, 1)
                pool.wait_ge(pool_step, steps.next())
                settle(pool)
                nc.gpsimd.tensor_tensor(dst, src, cos, ALU.mult).then_inc(pool_step, 1)
                pool.wait_ge(pool_step, steps.next())
                return nc.gpsimd.tensor_tensor(dst, dst, tmp_rope[:, :, :], ALU.add)

            def norm_rstd(i):
                pool.wait_ge(var_norm, i + 1)
                nc.gpsimd.tensor_tensor(small[:, 4:6], small[:, 2:4], neg_half[:, :], ALU.pow).then_inc(rstd_norm, 1)

            pool.sem_inc(part_added, ONE)
            nc.gpsimd.memset(neg_half[:, :], -0.5).then_inc(pool_step, 1)
            pool.wait_ge(pool_step, 1)
            pool.wait_ge(s_con, 16)
            per = POOL_PREP + 4 * POOL_TURN
            with pool.Fori(0, LAYERS) as l:
                norm_rstd(l)
                steps.at(l * per + 1)
                pool.wait_ge(acc_act, l * ACC_ACT + (2 + 12))
                pool.wait_ge(acc_dve, l * ACC_DVE + (2 + 12))
                for i, col in enumerate((SK, KS, KW)):
                    rotate(k_shared[:, :, i, :], proj[:, :, col:col + P]).then_inc(keys_roped, 1)
                    pool.wait_ge(keys_roped, l * 3 + (i + 1))
                settle(pool)
                assert steps.n == POOL_PREP, steps.n
                with pool.Fori(0, 4) as j:
                    steps.at(l * per + j * POOL_TURN + (1 + POOL_PREP))
                    pool.wait_ge(acc_act, l * ACC_ACT + (2 + 14))
                    pool.wait_ge(acc_dve, l * ACC_DVE + (2 + 14))
                    pool.wait_ge(tq_done, l * 4 + j + ONE)
                    rotate(roped[:, 1, :, :], proj[:, :, bass.ds(j * P + MQ, P)]).then_inc(q_roped, 1)
                    pool.wait_ge(q_roped, (l * 4 + j) * 5 + 1)
                    rotate(roped[:, 2, :, :], proj[:, :, bass.ds(j * P + MK, P)]).then_inc(q_roped, 1)
                    pool.wait_ge(q_roped, (l * 4 + j) * 5 + 2)
                    rotate(roped[:, 3, :, :], proj[:, :, bass.ds(j * P + SQ, P)]).then_inc(q_roped, 1)
                    pool.wait_ge(q_roped, (l * 4 + j) * 5 + 3)
                    rotate(roped[:, 4, :, :], proj[:, :, bass.ds(j * P + NQ, P)]).then_inc(q_roped, 1)
                    pool.wait_ge(q_roped, (l * 4 + j) * 5 + 4)
                    for f, col in ((0, RQ), (1, RK)):
                        nc.gpsimd.tensor_copy(roped[:, 0, :, f * HD:(f + 1) * HD],
                                              proj[:, :, bass.ds(j * HD + col, HD)]).then_inc(pool_step, 1)
                        v = steps.next()
                    pool.wait_ge(pool_step, v)
                    rotate(roped[:, 0, :, :], roped[:, 0, :, :]).then_inc(q_roped, 1)
                    pool.wait_ge(q_roped, (l * 4 + j) * 5 + 5)
                    for n, b in enumerate((2, 0, 1, 3)):
                        pool.wait_ge(z_tanh, (l * 4 + j) * 4 + n + 1)
                        settle(pool)
                        nc.gpsimd.tensor_scalar(zg[:, b, :, :], zg[:, b, :, :], 1.0, 0.25, ALU.add,
                                                ALU.mult).then_inc(pool_step, 1)
                        pool.wait_ge(pool_step, steps.next())
                        nc.gpsimd.tensor_tensor(zg[:, b, :, :], zg[:, b, :, :], proj[:, :, bass.ds(j * P + ZCOL[b], P)],
                                                ALU.mult).then_inc(z_done, 1)
                        if n == 1:
                            pool.wait_ge(var_ret, l * 4 + j + 1)
                            nc.gpsimd.tensor_tensor(ret_st[:, 18:20], ret_st[:, 16:18], neg_half[:, :], ALU.pow
                                                    ).then_inc(rstd_ret, 1)
                    assert steps.n == POOL_TURN, steps.n
                for v in range(8):
                    c, i = divmod(v, 4)
                    if i == 0:
                        continue
                    m = c * 6 + (i - 1) * 2
                    if i == 1:
                        pool.wait_ge(first_part, l * 4 + c * 2 + 2)
                    for t in range(NT):
                        pool.wait_ge(part_full, l * 12 + (m + t + 1))
                        if i > 1:
                            pool.wait_ge(part_added, l * 12 + (m + t - 1 + ONE))
                        nc.gpsimd.tensor_tensor(merged[:, t, c * CW:(c + 1) * CW], merged[:, t, c * CW:(c + 1) * CW],
                                                part[:, t, :], ALU.add).then_inc(part_added, 1)
            norm_rstd(LAYERS)

        @block.scalar
        def _(act):
            def split_hi(n, u, l, cols=UNIT):
                act.wait_ge(raw_full[u[1]], (l * (UNITS // 2) + u[0]) * 16 + 16)
                act.wait_ge(w_used, l * SPLITS + (n[0] + 1))
                nc.scalar.activation(w_hi[:, n[1], 0:cols], raw[:, u[1], 0:cols], ACT.Copy).then_inc(hi_done, 1)

            def ahead(n, cols=UNIT, l=None):
                u = n if n < N_MERGE else n + 4
                split_hi((n, n % 2), (u // 2, u % 2), l, cols)

            def xgroup_hi(g, dst, l):
                act.wait_ge(x_full, l * 16 + (g + 1))
                nc.scalar.activation(dst, xbank[g % 4][:, :], ACT.Copy).then_inc(x_hi, 1)

            def squares(count):
                act.wait_ge(x_lo, count * 16 + ONE)
                for t in range(NT):
                    nc.scalar.activation(h[:, t, :], x_sb[:, t, :], ACT.Square,
                                         accum_out=small[:, t:t + 1]).then_inc(sq_done, 1)

            act.wait_ge(s_x, 16)
            act.sem_inc(acc_act, 2)
            for first in (t_free, exp_done):
                act.sem_inc(first, ONE)
            with act.Fori(0, LAYERS) as l:
                act.wait_ge(acc_dve, l * ACC_DVE + 2)
                squares(l)
                ahead(0, l=l)
                ahead(1, l=l)
                for g in range(4):
                    xgroup_hi(g, hT_hi[:, 2 * g:2 * g + 2, :], l)
                with act.Fori(0, 6) as c:
                    for i in range(2):
                        for m in range(2):
                            n = c * 4 + (2 * i + m + 2)
                            split_hi((n, m), (c * 2 + (i + 1), m), l)
                        act.wait_ge(w_used, l * SPLITS + c * 4 + (2 * i + 2 + 2))
                        nc.scalar.activation(proj[:, 0, bass.ds(c * 2 * CW + i * CW, CW)], acc[2 * i][:, :],
                                             ACT.Copy).then_inc(acc_act, 1)
                for n in (N_TAIL, N_TAIL + 1):
                    ahead(n, UNIT_K * TAIL, l=l)
                act.wait_ge(w_used, l * SPLITS + (26 + 2))
                nc.scalar.activation(proj[:, 0, 12 * CW:13 * CW], acc[0][:, :], ACT.Copy).then_inc(acc_act, 1)
                act.wait_ge(w_used, l * SPLITS + (28 + 2))
                nc.scalar.activation(proj[:, 0, 13 * CW:MG], acc[2][:, 0:TAIL], ACT.Copy).then_inc(acc_act, 1)
                act.wait_ge(acc_act, l * ACC_ACT + (2 + 14))
                act.wait_ge(acc_dve, l * ACC_DVE + (2 + 14))
                nc.scalar.activation(nsa_g[:, :, :], proj[:, :, NG:NG + 24], ACT.Tanh, scale=0.5).then_inc(tail_tanh, 1)
                for i in range(3):
                    act.wait_ge(keys_T, l * 3 + (i + 1))
                    nc.scalar.activation(kT_shared[:, i, :, :], xbank[i][0:HD, :], ACT.Copy).then_inc(keys_out, 1)
                act.wait_ge(hid_sb, l + 1)
                nc.scalar.activation(hid3[:, :], hid2[:, :], ACT.Tanh, scale=0.7978845608028654).then_inc(hid_tanh, 1)
                ahead(N_MERGE, l=l)
                with act.Fori(0, 4) as j:
                    turn = l * 4 + j

                    def t_out(f, dst, src, scale=1.0):
                        act.wait_ge(t_full, turn * T_FILLS + (f + 1 + ONE))
                        nc.scalar.activation(dst, src, ACT.Copy, scale=scale).then_inc(t_free, 1)

                    def gate_out(i):
                        act.wait_ge(w_used, l * SPLITS + j * 4 + (N_MERGE + 2 * i + 2 + 2))
                        for t in range(NT):
                            ins = nc.scalar.activation(gates[:, t, bass.ds(j * 2 * CW + i * CW, CW)],
                                                       acc[2 * i + t][:, :], ACT.Tanh, scale=0.5)
                        ins.then_inc(acc_act, 1)

                    for s in range(SLOTS + 1):
                        if s % 4 == 0 and s < SLOTS:
                            i = s // 4 + 1
                            split_hi((j * 4 + (N_MERGE + i), i % 2), (j * 2 + (U_MERGE + i) // 2, i % 2), l)
                        if s < 5:
                            if s == 0:
                                act.wait_ge(t_full, turn * T_FILLS + (1 + ONE))
                                nc.scalar.activation(qkT[:, 0, 0, :], tbank[0:HD, 0:SEQ], ACT.Copy, scale=0.125)
                                nc.scalar.activation(qkT[:, 0, 1, :], tbank[0:HD, SEQ:2 * SEQ],
                                                     ACT.Copy).then_inc(t_free, 1)
                            else:
                                t_out(s, qkT[:, s, :, :], tbank[0:HD, :], 1.0 if s == 2 else 0.125)
                        if s == 2:
                            act.wait_ge(y_done, turn + ONE)
                            for b in (2, 0, 1, 3):
                                nc.scalar.activation(zg[:, b, :, :], proj[:, :, bass.ds(j * P + ZCOL[b], P)],
                                                     ACT.Tanh, scale=0.5).then_inc(z_tanh, 1)
                        k = s - S_AT
                        if k in SOFT:
                            e = SOFT[k]
                            act.wait_ge(max_done, turn * 8 + (e + 1))
                            act.wait_ge(t_full, turn * T_FILLS + ((SOFT_K[e - 2] + 5 if e > 1 else 0) + ONE))
                            for t, (a, b) in enumerate(((0, P), (P, 384))):
                                ins = nc.scalar.activation(probs[:, e % 2, a:b], score[k % 2][:, a:b], ACT.Exp,
                                                           bias=stat[:, e % 4, t:t + 1],
                                                           accum_out=stat[:, e % 4, 2 + t:3 + t])
                            ins.then_inc(exp_done, 1)
                            if ITEMS[k][0] == "swa":
                                nc.scalar.activation(stat[:, e % 4, 6:8], stat[:, e % 4, 4:6],
                                                     ACT.Exp).then_inc(sink_exp, 1)
                        elif 0 <= k < 10 and ITEMS[k][0] == "cmp":
                            act.wait_ge(cmp_sub, turn + 1)
                            nc.scalar.activation(cmp_s[:, :, :], cmp_s[:, :, :], ACT.Exp).then_inc(cmp_exp, 1)
                        k = s - P_AT
                        if 1 <= k < 10:
                            if k in SOFT:
                                t_out(4 + k, probsT[:, SOFT[k] % 2, :], tbank[:, 0:384])
                            else:
                                t_out(4 + k, cmp_pT[:, :], tbank[0:2 * NCMP, 0:SEQ])
                        if s == 8:
                            gate_out(0)
                        if s == SLOTS:
                            gate_out(1)
                for g in range(4):
                    xgroup_hi(4 + g, yT_hi[g][:, :, :], l)
                for v in range(8):
                    ahead(N_BRANCH + v + 1, l=l)
                    if v < 2:
                        for g in (4 + 2 * v, 5 + 2 * v):
                            xgroup_hi(4 + g, yT_hi[g][:, :, :], l)
                    if v == 5:
                        for g in range(2):
                            xgroup_hi(12 + g, hT_hi[:, 2 * g:2 * g + 2, :], l)
                ahead(N_OUT + 1, l=l)
                for g in range(2, 4):
                    xgroup_hi(12 + g, hT_hi[:, 2 * g:2 * g + 2, :], l)
                ahead(N_OUT + 2, l=l)
                ahead(N_OUT + 3, l=l)
            act.wait_ge(acc_dve, LAYERS * ACC_DVE + 2)
            squares(LAYERS)

        @block.vector
        def _(dve):
            steps = Count()

            def chain(ins):
                ins.then_inc(dve_step, 1)
                return steps.next()

            def split_lo(parity, done, cols=UNIT):
                dve.wait_ge(hi_done, done)
                nc.vector.tensor_tensor(w_lo[:, parity, 0:cols], raw[:, parity, 0:cols],
                                        w_hi[:, parity, 0:cols].bitcast(F32), ALU.subtract).then_inc(lo_done, 1)

            def xgroup_lo(g, hi, lo, l):
                dve.wait_ge(x_hi, l * 16 + (g + 1))
                bank = xbank[g % 4][:, :].rearrange("p (k n) -> p k n", k=2)
                nc.vector.tensor_tensor(lo, bank, hi.bitcast(F32), ALU.subtract).then_inc(x_lo, 1)

            def normalise(i):
                dve.wait_ge(acc_dve, i * ACC_DVE + 2)
                dve.wait_ge(sq_done, i * 2 + 2)
                nc.vector.tensor_scalar(small[:, 2:4], small[:, 0:2], 1.0 / D, EPS, ALU.mult,
                                        ALU.add).then_inc(var_norm, 1)
                dve.wait_ge(rstd_norm, i + 1)
                dve.wait_ge(s_g, i * 16 + 16)
                for t in range(NT):
                    ins = nc.vector.scalar_tensor_tensor(h[:, t, :], x_sb[:, t, :], small[:, 4 + t:5 + t],
                                                         g_row[:, :], ALU.mult, ALU.mult)
                return ins

            dve.sem_inc(lo_done, 2)
            for first in (x_lo, y_done, o_free):
                dve.sem_inc(first, ONE)
            dve.sem_inc(acc_dve, 2)
            dve.wait_ge(s_con, 16)
            nc.vector.tensor_copy(ident_b[:, :], ident)
            dve.wait_ge(s_mask, 16)
            nc.vector.tensor_copy(mask_b[:, :, :], mask_f[:, :].rearrange("p (m n) -> p m n", m=2)).then_inc(setup_done, 1)
            dve.wait_ge(s_sink, 16)
            for i in range(2):
                nc.vector.tensor_copy(sink[:, :, i], sink_in[:, :])
                ins = nc.vector.tensor_scalar(nsink[:, :, i], sink_in[:, :], -1.0, None, ALU.mult)
            ins.then_inc(setup_done, 1)
            dve.wait_ge(setup_done, 2)

            per = DVE_PREP + 4 * DVE_TURN
            with dve.Fori(0, LAYERS) as l:
                normalise(l).then_inc(h_done, 1)
                for n in range(2):
                    split_lo(n, l * SPLITS + n + 1)
                for g in range(4):
                    xgroup_lo(g, hT_hi[:, 2 * g:2 * g + 2, :], hT_lo[:, 2 * g:2 * g + 2, :], l)
                with dve.Fori(0, 6) as c:
                    for i in range(2):
                        for m in range(2):
                            split_lo(m, l * SPLITS + c * 4 + (2 * i + m + 3))
                        dve.wait_ge(w_used, l * SPLITS + c * 4 + (2 * i + 2 + 2))
                        nc.vector.tensor_copy(proj[:, 1, bass.ds(c * 2 * CW + i * CW, CW)],
                                              acc[2 * i + 1][:, :]).then_inc(acc_dve, 1)
                for n in (N_TAIL, N_TAIL + 1):
                    split_lo(n % 2, l * SPLITS + n + 1, UNIT_K * TAIL)
                dve.wait_ge(w_used, l * SPLITS + (26 + 2))
                nc.vector.tensor_copy(proj[:, 1, 12 * CW:13 * CW], acc[1][:, :]).then_inc(acc_dve, 1)
                steps.at(l * per)
                dve.wait_ge(acc_act, l * ACC_ACT + (2 + 12))
                dve.wait_ge(acc_dve, l * ACC_DVE + (2 + 12))
                for a in range(2):
                    for t in range(NT):
                        ins = nc.vector.tensor_copy(dup[:, t, :, a, :],
                                                    proj[:, t, KC:KC + 2 * P].rearrange("p (s n) -> p s n", n=HD))
                ins.then_inc(dup_done, 1)
                dve.wait_ge(w_used, l * SPLITS + (28 + 2))
                nc.vector.tensor_copy(proj[:, 1, 13 * CW:MG], acc[3][:, 0:TAIL]).then_inc(acc_dve, 1)
                for t, bank in enumerate((obank, tbank)):
                    dve.wait_ge(dup_T, l * 3 + (t + 1))
                    for odd in range(2):
                        rows = slice(odd * HD, (odd + 1) * HD)
                        v = chain(nc.vector.tensor_copy(
                            pairT[rows, :, t * HD:(t + 1) * HD],
                            bank[rows, :].rearrange("p (s n two) -> p s n two", s=4, two=2)[:, :, :, odd]))
                dve.wait_ge(dup_T, l * 3 + 3)
                v = chain(nc.vector.tensor_copy(posT[:, :], score[1][:, 0:16]))
                dve.wait_ge(dve_step, v)
                for s in range(2):
                    for half in range(2):
                        src = pairT[:, 2 * s:2 * s + 2, :].rearrange("p v (n k) -> p k v n", k=8)[:, :, :, half:half + NCMP]
                        dst = blocksT[:, s, half * 8:half * 8 + 8, :].rearrange("p k (v n) -> p k v n", v=2)
                        pos = posT[:, half * 8:half * 8 + 8].unsqueeze(2).unsqueeze(3).to_broadcast([P, 8, 2, NCMP])
                        ins = nc.vector.tensor_tensor(dst, src, pos, ALU.add)
                ins.then_inc(blocks_done, 1)
                dve.wait_ge(cmp_used, l * 4 + 4)
                v = chain(nc.vector.tensor_copy(hid[:, :], score[0][0:2 * NCMP, :]))
                dve.wait_ge(dve_step, v)
                v = chain(nc.vector.tensor_tensor(hid2[:, :], hid[:, :], hid[:, :], ALU.mult))
                dve.wait_ge(dve_step, v)
                v = chain(nc.vector.tensor_scalar(hid2[:, :], hid2[:, :], 0.044715, 1.0, ALU.mult, ALU.add))
                dve.wait_ge(dve_step, v)
                nc.vector.tensor_tensor(hid2[:, :], hid2[:, :], hid[:, :], ALU.mult).then_inc(hid_sb, 1)
                dve.wait_ge(hid_tanh, l + 1)
                nc.vector.scalar_tensor_tensor(hid2[:, :], hid3[:, :], 1.0, hid[:, :], ALU.add,
                                               ALU.mult).then_inc(gelu_done, 1)
                dve.wait_ge(gelu_T, l + 1)
                gT = obank[:, :].rearrange("p (f n) -> p f n", f=4)
                nc.vector.tensor_copy(gkT[:, :, :], gT[:, 0:2, 0:2 * NCMP])
                for a in range(2):
                    ins = nc.vector.tensor_copy(gvT[:, :, :, a, :],
                                                gT[:, 2:4, 0:2 * NCMP].rearrange("p f (v n) -> p f v n", v=2))
                ins.then_inc(gelu_out, 1)
                dve.wait_ge(tail_tanh, l + 1)
                nc.vector.tensor_scalar(nsa_g[:, :, :], nsa_g[:, :, :], 1.0, 0.5, ALU.add, ALU.mult).then_inc(gates_nsa, 1)
                dve.wait_ge(cmp_kv, l + 1)
                v = chain(nc.vector.tensor_scalar(kc_s[:, :], score[0][0:2 * NCMP, 0:HD], 0.5, None, ALU.mult))
                for kv in range(2):
                    blk = con[0:2 * NCMP, C_BLK:C_BLK + 2].unsqueeze(2).to_broadcast([2 * NCMP, 2, HD])
                    val = score[1][0:2 * NCMP, kv * HD:(kv + 1) * HD].unsqueeze(1).to_broadcast([2 * NCMP, 2, HD])
                    last = chain(nc.vector.tensor_tensor(v_blk[:, kv, :].rearrange("p (a n) -> p a n", a=2), val, blk,
                                                         ALU.mult))
                dve.wait_ge(dve_step, v)
                sin = con[0:2 * NCMP, C_SINK:C_SINK + HD]
                chain(nc.vector.tensor_tensor(kc_t[:, 0:32], kc_s[:, 32:64], sin[:, 0:32], ALU.mult))
                chain(nc.vector.tensor_tensor(kc_t[:, 32:64], kc_s[:, 0:32], sin[:, 32:64], ALU.mult))
                v = chain(nc.vector.tensor_tensor(kc_r[:, :], kc_s[:, :], con[0:2 * NCMP, C_COSK:C_COSK + HD], ALU.mult))
                dve.wait_ge(dve_step, v)
                nc.vector.tensor_tensor(kc_r[:, :], kc_r[:, :], kc_t[:, :], ALU.add).then_inc(cmp_roped, 1)
                dve.wait_ge(kcT_full, l + 1)
                nc.vector.tensor_copy(kcT[:, :, :], tbank[0:HD, 0:2 * NCMP].rearrange("p (v n) -> p v n", v=2)
                                      ).then_inc(cmp_ready, 1)
                prep_n = steps.n
                split_lo(0, l * SPLITS + N_MERGE + 1)
                with dve.Fori(0, 4) as j:
                    turn = l * 4 + j
                    steps.at(l * per + j * DVE_TURN + DVE_PREP)

                    def scores_in(k):
                        kind, a = ITEMS[k]
                        bank = score[k % 2]
                        dve.wait_ge(s_full, turn * 10 + (k + 1))
                        if kind == "ret":
                            dve.wait_ge(o_full, turn * 10 + ONE)
                            nc.vector.tensor_tensor(attT[:, :], bank[:, 0:384],
                                                    con[:, bass.ds(j * 384 + C_DECAY, 384)], ALU.mult
                                                    ).then_inc(s_dve, 1)
                            return
                        if kind == "cmp":
                            sc = bank[:, 0:64].rearrange("p (t a n) -> p t a n", t=NT, a=2)[:, :, :, 0:NCMP]
                            cs = cmp_s[:, :, :].rearrange("p (t a) n -> p t a n", t=NT)

                            def per_tile(col):
                                return con[:, col:col + 2 * NCMP].rearrange("p (t n) -> p t n", t=NT).unsqueeze(2
                                    ).to_broadcast([P, NT, 2, NCMP])
                            nc.vector.tensor_tensor(cs, sc, per_tile(C_CADD), ALU.add).then_inc(s_dve, 1)
                            dve.wait_ge(s_dve, turn * 2 + 2)
                            v = chain(nc.vector.tensor_reduce(cmp_st[:, :, 0], cmp_s[:, :, :], AX.X, ALU.max))
                            dve.wait_ge(dve_step, v)
                            nc.vector.tensor_tensor(cmp_s[:, :, :], cmp_s[:, :, :],
                                                    cmp_st[:, :, 0:1].to_broadcast([P, 4, NCMP]), ALU.subtract
                                                    ).then_inc(cmp_sub, 1)
                            dve.wait_ge(cmp_exp, turn + 1)
                            nc.vector.tensor_tensor(cs, cs, per_tile(C_C01), ALU.mult).then_inc(cmp_p, 1)
                            dve.wait_ge(cmp_p, turn + 1)
                            v = chain(nc.vector.tensor_reduce(cmp_st[:, :, 1], cmp_s[:, :, :], AX.X, ALU.add))
                            dve.wait_ge(dve_step, v)
                            v = chain(nc.vector.tensor_scalar(cmp_st[:, :, 2], cmp_st[:, :, 1], TINY, None, ALU.max))
                            dve.wait_ge(dve_step, v)
                            v = chain(nc.vector.reciprocal(cmp_st[:, :, 3], cmp_st[:, :, 2]))
                            dve.wait_ge(dve_step, v)
                            chain(nc.vector.tensor_tensor(
                                cmp_st[:, :, 2].rearrange("p (t a) -> p t a", t=NT),
                                cmp_st[:, :, 3].rearrange("p (t a) -> p t a", t=NT),
                                nsa_g[:, :, bass.ds(j * 2, 2)], ALU.mult))
                            return
                        e = SOFT[k]
                        st = stat[:, e % 4, :]
                        n_max = chain(nc.vector.tensor_reduce(st[:, 0:1], bank[:, 0:P], AX.X, ALU.max, negate=True))
                        if kind != "swa":
                            nc.vector.tensor_reduce(st[:, 1:2], bank[:, P:384], AX.X, ALU.max, negate=True
                                                    ).then_inc(max_done, 1)
                            return
                        v = chain(nc.vector.tensor_reduce(st[:, 1:2], bank[:, P:384], AX.X, ALU.max, negate=True))
                        dve.wait_ge(dve_step, v)
                        v = chain(nc.vector.tensor_tensor(st[:, 0:2], st[:, 0:2],
                                                          nsink[:, bass.ds(l * HEADS + j * 2 + a, 1), :].squeeze(1),
                                                          ALU.min))
                        dve.wait_ge(dve_step, v)
                        nc.vector.tensor_tensor(st[:, 4:6], st[:, 0:2],
                                                sink[:, bass.ds(l * HEADS + j * 2 + a, 1), :].squeeze(1), ALU.add
                                                ).then_inc(max_done, 1)

                    def outputs_in(k):
                        kind, a = ITEMS[k]
                        o = obank[:, 0:2 * P].rearrange("p (t n) -> p t n", t=NT)
                        hcols = slice(a * HD, (a + 1) * HD)
                        if kind == "ret":
                            dve.wait_ge(o_full, turn * 10 + (k + 1 + ONE))
                            for t in range(NT):
                                v = chain(nc.vector.bn_stats(ret_st[:, 6 * t:6 * t + 6], o[:, t, :]))
                            dve.wait_ge(dve_step, v)
                            settle(dve)
                            for t in range(NT):
                                v = chain(nc.vector.bn_aggr(ret_st[:, 12 + 2 * t:14 + 2 * t], ret_st[:, 6 * t:6 * t + 6]))
                            dve.wait_ge(dve_step, v)
                            nc.vector.tensor_scalar(ret_st[:, 16:18],
                                                    ret_st[:, 12:16].rearrange("p (t m) -> p t m", m=2)[:, :, 1],
                                                    EPS, None, ALU.add).then_inc(var_ret, 1)
                            dve.wait_ge(rstd_ret, turn + 1)
                            dve.wait_ge(z_done, turn * 4 + 1)
                            for t in range(NT):
                                ins = nc.vector.tensor_scalar(nsa_sum[:, t, :], o[:, t, :], ret_st[:, 12 + 2 * t:13 + 2 * t],
                                                              ret_st[:, 18 + t:19 + t], ALU.subtract, ALU.mult)
                            ins.then_inc(o_free, 1)
                            dve.wait_ge(o_free, turn * 10 + (k + 1 + ONE))
                            chain(nc.vector.tensor_tensor(proj[:, :, bass.ds(j * P + RZ, P)], nsa_sum[:, :, :],
                                                          zg[:, 2, :, :], ALU.mult))
                            return
                        if kind == "cmp":
                            dve.wait_ge(dve_step, steps.base + steps.n)
                            dve.wait_ge(o_full, turn * 10 + (k + 1 + ONE))
                            nc.vector.tensor_tensor(
                                nsa_sum[:, :, :].rearrange("p t (a n) -> p (t a) n", a=2),
                                obank[:, 0:2 * P].rearrange("p (t n) -> p t n", n=HD),
                                cmp_st[:, :, 2:3].to_broadcast([P, 4, HD]), ALU.mult).then_inc(o_free, 1)
                            return
                        e = SOFT[k]
                        st = stat[:, e % 4, :]
                        dve.wait_ge(exp_done, turn * 8 + (e + 1 + ONE))
                        if kind == "swa":
                            dve.wait_ge(sink_exp, turn * 2 + (a + 1))
                            v = chain(nc.vector.tensor_tensor(st[:, 2:4], st[:, 2:4], st[:, 6:8], ALU.add))
                            dve.wait_ge(dve_step, v)
                        v = chain(nc.vector.reciprocal(st[:, 8:10], st[:, 2:4]))
                        dve.wait_ge(dve_step, v)
                        if kind in ("moba", "swa"):
                            b = 0 if kind == "moba" else 1
                            dve.wait_ge(z_done, turn * 4 + (b + 2))
                            dve.wait_ge(o_full, turn * 10 + (k + 1 + ONE))
                            for t in range(NT):
                                ins = nc.vector.scalar_tensor_tensor(
                                    proj[:, t, bass.ds(j * P + (ZCOL[b] + a * HD), HD)], o[:, t, 0:HD], st[:, 8 + t:9 + t],
                                    zg[:, b, t, hcols], ALU.mult, ALU.mult)
                            ins.then_inc(o_free, 1)
                            return
                        g = 1 if kind == "slc" else 2
                        v = chain(nc.vector.tensor_tensor(st[:, 10:12], st[:, 8:10],
                                                          nsa_g[:, :, bass.ds(j * 2 + (g * HEADS + a), 1)].squeeze(2),
                                                          ALU.mult))
                        dve.wait_ge(dve_step, v)
                        dve.wait_ge(o_full, turn * 10 + (k + 1 + ONE))
                        dve.wait_ge(o_free, turn * 10 + (k + ONE))
                        for t in range(NT):
                            ins = nc.vector.scalar_tensor_tensor(nsa_sum[:, t, hcols], o[:, t, 0:HD], st[:, 10 + t:11 + t],
                                                                 nsa_sum[:, t, hcols], ALU.mult, ALU.add)
                        ins.then_inc(o_free, 1)
                        if kind == "win":
                            dve.wait_ge(o_free, turn * 10 + (k + 1 + ONE))
                            dve.wait_ge(z_done, turn * 4 + 4)
                            ins = nc.vector.tensor_tensor(proj[:, :, bass.ds(j * P + (NZ + a * HD), HD)],
                                                          nsa_sum[:, :, hcols], zg[:, 3, :, hcols], ALU.mult)
                            if a == 1:
                                ins.then_inc(y_done, 1)
                            else:
                                chain(ins)

                    for s in range(SLOTS):
                        if s % 4 == 0:
                            i = s // 4 + 1
                            split_lo(i % 2, l * SPLITS + j * 4 + (N_MERGE + i + 1))
                        if 0 <= s - S_AT < 10:
                            scores_in(s - S_AT)
                        if 0 <= s - O_AT < 10:
                            outputs_in(s - O_AT)
                    turn_n = steps.n
                assert (prep_n, turn_n) == (DVE_PREP, DVE_TURN), (prep_n, turn_n)
                for g in range(4):
                    xgroup_lo(4 + g, yT_hi[g][:, :, :], yT_lo[g][:, :, :], l)
                for v in range(8):
                    c, i = divmod(v, 4)
                    split_lo((v + 1) % 2, l * SPLITS + N_BRANCH + v + 2)
                    if v < 2:
                        for g in (4 + 2 * v, 5 + 2 * v):
                            xgroup_lo(4 + g, yT_hi[g][:, :, :], yT_lo[g][:, :, :], l)
                    dve.wait_ge(w_used, l * SPLITS + (N_BRANCH + v + 1 + 2))
                    if i == 0:
                        dve.wait_ge(acc_act, l * ACC_ACT + (22 + 2))
                    for t in range(NT):
                        gate = gates[:, t, i * D + c * CW:i * D + (c + 1) * CW]
                        if i == 0:
                            ins = nc.vector.scalar_tensor_tensor(gate, gate, 1.0, acc[(v % 2) * 2 + t][:, :], ALU.add,
                                                                 ALU.mult)
                            ins.then_inc(first_part, 1)
                        else:
                            m = c * 6 + (i - 1) * 2 + t
                            dve.wait_ge(part_added, l * 12 + (max(m - 1, 0) + ONE))
                            nc.vector.scalar_tensor_tensor(part[:, t, :], gate, 1.0, acc[(v % 2) * 2 + t][:, :],
                                                           ALU.add, ALU.mult).then_inc(part_full, 1)
                    if v == 5:
                        for g in range(2):
                            xgroup_lo(12 + g, hT_hi[:, 2 * g:2 * g + 2, :], hT_lo[:, 2 * g:2 * g + 2, :], l)
                split_lo(1, l * SPLITS + N_OUT + 2)
                for g in range(2, 4):
                    xgroup_lo(12 + g, hT_hi[:, 2 * g:2 * g + 2, :], hT_lo[:, 2 * g:2 * g + 2, :], l)
                split_lo(0, l * SPLITS + N_OUT + 3)
                split_lo(1, l * SPLITS + N_OUT + 4)
                for c in range(2):
                    dve.wait_ge(w_used, l * SPLITS + (N_OUT + 2 + c + 1 + 2))
                    for t in range(NT):
                        cols = slice(c * CW, (c + 1) * CW)
                        ins = nc.vector.tensor_tensor(x_sb[:, t, cols], x_sb[:, t, cols], acc[2 * c + t][:, :], ALU.add)
                    ins.then_inc(acc_dve, 1)
            normalise(LAYERS).then_inc(y_final, 1)

        @block.tensor
        def _(pe):
            def steps_of(hi, lo, k, unit, uk, banks, first, last, cols=CW):
                wide = cols * UNIT_K
                wh = w_hi[:, unit, 0:wide].rearrange("p (k n) -> p k n", k=UNIT_K)[:, uk, :]
                wl = w_lo[:, unit, 0:wide].rearrange("p (k n) -> p k n", k=UNIT_K)[:, uk, :]
                for t in range(NT):
                    o = acc[banks + t][:, 0:cols]
                    a, b = hi[:, k, t * P:(t + 1) * P], lo[:, k, t * P:(t + 1) * P]
                    nc.tensor.matmul(o, a, wl, start=first, stop=False)
                    nc.tensor.matmul(o, a, wh, start=False, stop=False)
                    ins = nc.tensor.matmul(o, b, wh, start=False, stop=last)
                return ins

            def unit_of(kh, unit, banks, done, cols=CW):
                pe.wait_ge(lo_done, done)
                for uk in range(UNIT_K):
                    ins = steps_of(hT_hi, hT_lo, kh * UNIT_K + uk, unit, uk, banks, kh == 0 and uk == 0,
                                   kh == 1 and uk == UNIT_K - 1, cols)
                ins.then_inc(w_used, 1)

            def transposes(g, src):
                for k in range(2):
                    for t in range(NT):
                        ins = nc.tensor.transpose(xbank[g % 4][:, k * SEQ + t * P:k * SEQ + (t + 1) * P],
                                                  src(t, k), ident)
                ins.then_inc(x_full, 1)

            pe.sem_inc(w_used, 2)
            for first in (tq_done, t_full, o_full):
                pe.sem_inc(first, ONE)
            pe.wait_ge(s_con, 16)
            pe.wait_ge(setup_done, 2)
            with pe.Fori(0, LAYERS) as l:
                pe.wait_ge(h_done, l + 1)
                pe.wait_ge(x_lo, l * 16 + ONE)
                for g in range(4):
                    transposes(g, lambda t, k: h[:, t, (2 * g + k) * P:(2 * g + k + 1) * P])
                pe.wait_ge(x_lo, l * 16 + (4 + ONE))
                settle(pe)
                with pe.Fori(0, 6) as c:
                    for i in range(2):
                        pe.wait_ge(acc_act, l * ACC_ACT + c * 2 + (i + 1))
                        pe.wait_ge(acc_dve, l * ACC_DVE + c * 2 + (i + 1))
                        for kh in range(2):
                            unit_of(kh, kh, 2 * i, l * SPLITS + c * 4 + (2 * i + kh + 1 + 2))
                pe.wait_ge(acc_act, l * ACC_ACT + 13)
                pe.wait_ge(acc_dve, l * ACC_DVE + 13)
                for kh in range(2):
                    unit_of(kh, kh, 0, l * SPLITS + 24 + kh + 1 + 2)
                pe.wait_ge(acc_act, l * ACC_ACT + 14)
                pe.wait_ge(acc_dve, l * ACC_DVE + 14)
                for kh in range(2):
                    unit_of(kh, kh, 2, l * SPLITS + N_TAIL + kh + 1 + 2, TAIL)
                pe.wait_ge(keys_roped, l * 3 + 3)
                settle(pe)
                for i in range(3):
                    for kv in range(2):
                        for t in range(NT):
                            ins = nc.tensor.transpose(xbank[i][0:HD, kv * SEQ + t * P:kv * SEQ + (t + 1) * P],
                                                      k_shared[:, t, i, kv * HD:(kv + 1) * HD], ident)
                    ins.then_inc(keys_T, 1)
                pe.wait_ge(dup_done, l + 1)
                for t, bank in enumerate((obank, tbank)):
                    if t:
                        pe.wait_ge(keys_out, l * 3 + 3)
                    for s in range(4):
                        ins = nc.tensor.transpose(bank[:, s * P:(s + 1) * P],
                                                  dup[:, t, s, :, :].rearrange("p a n -> p (a n)"), ident)
                    ins.then_inc(dup_T, 1)
                pe.wait_ge(s_pos, l * 16 + 16)
                settle(pe)
                nc.tensor.transpose(score[1][:, 0:16], pos_in[:, :], ident[0:16, 0:16]).then_inc(dup_T, 1)
                pe.wait_ge(blocks_done, l + 1)
                for i in range(4):
                    u = U_CMP + i
                    pe.wait_ge(raw_full[u % 2], (l * (UNITS // 2) + u // 2) * 16 + 16)
                    for k in range(8):
                        ins = nc.tensor.matmul(score[0][0:2 * NCMP, i // 2 * 256:i // 2 * 256 + 256],
                                               blocksT[:, i // 2, (i % 2) * 8 + k, :], slot8(raw, u)[:, k, :],
                                               start=(i % 2 == 0 and k == 0), stop=(i % 2 == 1 and k == 7))
                    ins.then_inc(cmp_used, 1)
                pe.wait_ge(gelu_done, l + 1)
                settle(pe)
                for f in range(4):
                    ins = nc.tensor.transpose(obank[:, f * P:f * P + 2 * NCMP], hid2[:, f * P:(f + 1) * P],
                                              ident[0:2 * NCMP, 0:2 * NCMP])
                ins.then_inc(gelu_T, 1)
                pe.wait_ge(gelu_out, l + 1)
                pe.wait_ge(s_c2, l * 32 + 32)
                for f in range(2):
                    nc.tensor.matmul(score[0][0:2 * NCMP, 0:HD], gkT[:, f, :], w_c2[:, 0, f, :], start=(f == 0),
                                     stop=(f == 1))
                for kv in range(2):
                    for f in range(2):
                        ins = nc.tensor.matmul(score[1][0:2 * NCMP, kv * HD:(kv + 1) * HD],
                                               gvT[:, f, kv, :, :].rearrange("p a n -> p (a n)"), w_c2[:, 1, f, :],
                                               start=(f == 0), stop=(f == 1))
                ins.then_inc(cmp_kv, 1)
                pe.wait_ge(cmp_roped, l + 1)
                settle(pe)
                nc.tensor.transpose(tbank[0:HD, 0:2 * NCMP], kc_r[:, :], ident[0:2 * NCMP, 0:2 * NCMP]).then_inc(kcT_full, 1)
                pe.wait_ge(cmp_ready, l + 1)
                pe.wait_ge(gates_nsa, l + 1)
                settle(pe)
                with pe.Fori(0, 4) as j:
                    turn = l * 4 + j

                    def heads_T(f):
                        pe.wait_ge(t_free, turn * T_FILLS + (f + ONE))
                        settle(pe)
                        for a in range(2):
                            for t in range(NT):
                                ins = nc.tensor.transpose(tbank[0:HD, a * SEQ + t * P:a * SEQ + (t + 1) * P],
                                                          roped[:, f, t, a * HD:(a + 1) * HD], ident)
                        ins.then_inc(t_full, 1)

                    def scores_of(k):
                        kind, a = ITEMS[k]
                        bank = score[k % 2]
                        if k < 2:
                            pe.wait_ge(exp_done, turn * 8 + ONE)
                        elif k - 2 in SOFT:
                            pe.wait_ge(exp_done, turn * 8 + (SOFT[k - 2] + 1 + ONE))
                        else:
                            pe.wait_ge(s_dve, turn * 2 + (1 if k == 2 else 2))
                        if kind == "ret":
                            pe.wait_ge(t_free, turn * T_FILLS + (1 + ONE))
                            nc.tensor.matmul(bank[:, 0:SEQ], qkT[:, 0, 1, 0:P], qkT[:, 0, 0, :], start=True, stop=True)
                            nc.tensor.matmul(bank[:, SEQ:384], qkT[:, 0, 1, P:SEQ], qkT[:, 0, 0, P:SEQ], start=True,
                                             stop=True).then_inc(s_full, 1)
                            return
                        if kind == "cmp":
                            pe.wait_ge(t_free, turn * T_FILLS + (5 + ONE))
                            for t in range(NT):
                                for b in range(2):
                                    o = (t * 2 + b) * 16
                                    ins = nc.tensor.matmul(bank[:, o:o + NCMP], qkT[:, 4, b, t * P:(t + 1) * P],
                                                           kcT[:, bass.ds(j // 2, 1), :].squeeze(1), start=True, stop=True)
                            ins.then_inc(s_full, 1)
                            return
                        pe.wait_ge(t_free, turn * T_FILLS + ((3 if kind == "moba" else KIND[kind] + 1) + ONE))
                        ins = nc.tensor.matmul(bank[:, 0:384], ident_b[:, :], mask_b[:, int(kind == "swa"), :],
                                               start=True, stop=False)
                        if k == 1:
                            ins.then_inc(tq_done, 1)
                        for t, (c0, c1, n) in enumerate(((0, P, P), (P, 384, SEQ))):
                            keys = qkT[:, 2, a, 0:n] if kind == "moba" else \
                                kT_shared[:, KEYS[kind], bass.ds(j // 2, 1), 0:n].squeeze(1)
                            ins = nc.tensor.matmul(bank[:, c0:c1], qkT[:, KIND[kind], a, t * P:(t + 1) * P], keys,
                                                   start=False, stop=(t == 1))
                        ins.then_inc(s_full, 1)

                    def probs_T(k):
                        pe.wait_ge(t_free, turn * T_FILLS + (4 + k + ONE))
                        if k in SOFT:
                            e = SOFT[k]
                            pe.wait_ge(exp_done, turn * 8 + (e + 1 + ONE))
                            for i in range(3):
                                ins = nc.tensor.transpose(tbank[:, i * P:(i + 1) * P], probs[:, e % 2, i * P:(i + 1) * P],
                                                          ident)
                            ins.then_inc(t_full, 1)
                            return
                        pe.wait_ge(cmp_p, turn + 1)
                        for t in range(NT):
                            ins = nc.tensor.transpose(tbank[0:2 * NCMP, t * P:(t + 1) * P],
                                                      cmp_s[:, 2 * t:2 * t + 2, :].rearrange("p a n -> p (a n)"), ident)
                        ins.then_inc(t_full, 1)

                    def outputs_of(k):
                        kind, a = ITEMS[k]
                        pe.wait_ge(o_free, turn * 10 + (k + ONE))
                        if kind == "cmp":
                            pe.wait_ge(t_free, turn * T_FILLS + (5 + k + ONE))
                            for t in range(NT):
                                ins = nc.tensor.matmul(obank[:, t * P:(t + 1) * P], cmp_pT[:, t * P:(t + 1) * P],
                                                       v_blk[:, bass.ds(j // 2, 1), :].squeeze(1), start=True, stop=True)
                            ins.then_inc(o_full, 1)
                            return
                        if kind == "ret":
                            pe.wait_ge(s_dve, turn * 2 + 1)
                            left, n = attT[:, :], P
                            vcol = bass.ds(j * P + RV, P)
                        else:
                            pe.wait_ge(t_free, turn * T_FILLS + (5 + k + ONE))
                            left, n = probsT[:, SOFT[k] % 2, :], HD
                            vcol = bass.ds(j * P + (MV + a * HD), HD) if kind == "moba" else \
                                bass.ds(j // 2 * HD + VCOL[kind], HD)
                        nc.tensor.matmul(obank[:, 0:n], left[:, 0:P], proj[:, 0, vcol], start=True, stop=True)
                        nc.tensor.matmul(obank[:, P:P + n], left[:, P:2 * P], proj[:, 0, vcol], start=True, stop=False)
                        nc.tensor.matmul(obank[:, P:P + n], left[:, 2 * P:3 * P], proj[:, 1, vcol], start=False,
                                         stop=True).then_inc(o_full, 1)

                    for s in range(SLOTS):
                        i, uk = divmod(s, UNIT_K)
                        if s % 8 == 0:
                            pe.wait_ge(acc_act, l * ACC_ACT + j * 2 + (14 + s // 8 + 1))
                            pe.wait_ge(acc_dve, l * ACC_DVE + (2 + 14))
                        if uk == 0:
                            pe.wait_ge(lo_done, l * SPLITS + j * 4 + (N_MERGE + i + 1 + 2))
                        ins = steps_of(hT_hi, hT_lo, s % 8, i % 2, uk, 2 * (s // 8), s % 8 == 0, s % 8 == 7)
                        if uk == UNIT_K - 1:
                            ins.then_inc(w_used, 1)
                        if s == 0:
                            pe.wait_ge(q_roped, turn * 5 + 5)
                        if s < 5:
                            heads_T(s)
                        if 0 <= s - S_AT < 10:
                            scores_of(s - S_AT)
                        if 1 <= s - P_AT < 10:
                            probs_T(s - P_AT)
                        if 0 <= s - O_AT < 10:
                            outputs_of(s - O_AT)
                def outputs_T(g):
                    b, pair = divmod(g, 2)
                    if g >= 4:
                        pe.wait_ge(x_lo, l * 16 + (g + 1 + ONE))
                    transposes(4 + g, lambda t, k: proj[:, t, ZCOL[b] + (2 * pair + k) * P:ZCOL[b] + (2 * pair + k + 1) * P])

                def merged_T(g):
                    pe.wait_ge(x_lo, l * 16 + (12 + ONE))
                    transposes(12 + g, lambda t, k: merged[:, t, (2 * g + k) * P:(2 * g + k + 1) * P])

                pe.wait_ge(y_done, l * 4 + (4 + ONE))
                pe.wait_ge(t_free, l * 4 * T_FILLS + (4 * T_FILLS + ONE))
                for g in range(4):
                    outputs_T(g)
                for v in range(8):
                    c, i = divmod(v, 4)
                    pe.wait_ge(x_lo, l * 16 + (4 + min(2 * v + 2, 8) + ONE))
                    if v < 2:
                        pe.wait_ge(acc_act, l * ACC_ACT + (23 + v))
                    elif (v - 2) % 4 == 0:
                        pe.wait_ge(first_part, l * 4 + ((v - 2) // 4 * 2 + 2))
                    else:
                        pe.wait_ge(part_full, l * 12 + ((v - 2) // 4 * 6 + (v - 2) % 4 * 2))
                    pe.wait_ge(lo_done, l * SPLITS + (N_BRANCH + v + 1 + 2))
                    for uk in range(UNIT_K):
                        g = 2 * i + uk // 2
                        ins = steps_of(yT_hi[g], yT_lo[g], uk % 2, v % 2, uk, (v % 2) * 2, uk == 0, uk == UNIT_K - 1)
                    ins.then_inc(w_used, 1)
                    if v < 2:
                        outputs_T(4 + 2 * v)
                        outputs_T(5 + 2 * v)
                    if v == 4:
                        pe.wait_ge(part_added, l * 12 + (6 + ONE))
                        merged_T(0)
                        merged_T(1)
                pe.wait_ge(part_added, l * 12 + (12 + ONE))
                merged_T(2)
                merged_T(3)
                for v in range(4):
                    kh, c = divmod(v, 2)
                    pe.wait_ge(x_lo, l * 16 + ((14 if kh == 0 else 16) + ONE))
                    pe.wait_ge(lo_done, l * SPLITS + (N_OUT + v + 1 + 2))
                    for uk in range(UNIT_K):
                        k = kh * UNIT_K + uk
                        ins = steps_of(hT_hi, hT_lo, k, v % 2, uk, 2 * c, k == 0, k == KD - 1)
                    ins.then_inc(w_used, 1)


_INS = ["x", "norm_g", "w_in", "w_branch", "w_out", "swa_sink", "nsa_cmp_pos", "nsa_w_ck1", "nsa_w_ck2",
        "nsa_w_cv1", "nsa_w_cv2", "final_norm_g"]


def constant_arrays():
    import numpy as np
    f = np.float32
    inv = (f(1.0) / f(10000.0) ** (np.arange(0, HD, 2, dtype=f) / f(HD))).astype(f)
    ang = np.arange(SEQ, dtype=f)[:, None] * inv[None, :]
    cos, sin = np.cos(ang).astype(f), np.sin(ang).astype(f)
    cos2, sin2 = np.concatenate([cos, cos], 1), np.concatenate([-sin, sin], 1)
    c = np.zeros((P, N_CONST), f)
    c[:, C_ID:C_ID + P] = np.eye(P, dtype=f)
    for t in range(NT):
        for a in range(2):
            o = t * P + a * HD
            c[:, C_COS + o:C_COS + o + HD] = cos2[t * P:(t + 1) * P]
            c[:, C_SIN + o:C_SIN + o + HD] = sin2[t * P:(t + 1) * P]
    row = np.arange(P)
    for h in range(4):
        log_g = np.log(f(1.0) - f(2.0) ** f(-5.0 - h)).astype(f)
        for i, (k0, q0, n) in enumerate(((0, 0, 2 * P), (P, P, P))):
            diff = (q0 + np.arange(n))[None, :] - (k0 + row)[:, None]
            o = C_DECAY + h * 384 + i * 2 * P
            c[:, o:o + n] = np.where(diff >= 0, np.exp(np.maximum(diff, 0).astype(f) * log_g), 0.0)
    end = np.arange(NCMP) * 16 + 31
    for t in range(NT):
        ok = end[None, :] <= (t * P + row)[:, None]
        c[:, C_CADD + t * NCMP:C_CADD + (t + 1) * NCMP] = np.where(ok, 0.0, -1e30)
        c[:, C_C01 + t * NCMP:C_C01 + (t + 1) * NCMP] = ok
    for a in range(2):
        c[a * NCMP:(a + 1) * NCMP, C_BLK + a] = 0.5
        c[a * NCMP:(a + 1) * NCMP, C_COSK:C_COSK + HD] = cos2[end]
        c[a * NCMP:(a + 1) * NCMP, C_SINK:C_SINK + HD] = sin2[end]
    m = np.zeros((P, 2, 384), f)
    for i, (q0, k0) in enumerate(((0, 0), (P, 0), (P, P))):
        dist = (q0 + row)[:, None] - (k0 + row)[None, :]
        m[:, 0, i * P:(i + 1) * P] = np.where(dist >= 0, 0.0, -1e30)
        m[:, 1, i * P:(i + 1) * P] = np.where((dist >= 0) & (dist < 128), 0.0, -1e30)
    return c, m.reshape(P, 768)


def kernel(**inputs):
    import numpy as np
    import concourse.bacc as bacc
    from concourse.bass_utils import run_bass_kernel_spmd

    nc = bacc.Bacc("TRN2", target_bir_lowering=False, num_devices=1)
    consts, masks = constant_arrays()
    arrays, args = {}, []
    for name, a in [(n, np.ascontiguousarray(inputs[n])) for n in _INS] + [("consts", consts), ("masks", masks)]:
        arrays[f"in_{name}_dram"] = a
        args.append(nc.dram_tensor(f"in_{name}_dram", a.shape, mybir.dt.from_np(a.dtype), kind="ExternalInput").ap())
    args.append(nc.dram_tensor("out_dram", (1, SEQ, D), F32, kind="ExternalOutput").ap())
    hybrid_trunk(nc, *args)
    r = run_bass_kernel_spmd(nc, [arrays], core_ids=[0])
    return r.results[0]["out_dram"]
```

```python
from contextlib import ExitStack

import concourse.bass as bass
from concourse import mybir

F32 = mybir.dt.float32
F32R = mybir.dt.float32r
BF16 = mybir.dt.bfloat16
ALU = mybir.AluOpType
ACT = mybir.ActivationFunctionType
AX = mybir.AxisListType

P = 128
D = 1024
KD = D // P
SEQ = 256
NT = SEQ // P
LAYERS = 2
HD = 64
HEADS = 8
W = HEADS * HD
CW = 512
UNIT_K = 4
UNIT = UNIT_K * CW
NCMP = 15
EPS = 1e-6
TINY = 1e-30

MQ, MK, MV, MZ = 0, 512, 1024, 1536
SQ, SK, SV, SZ = 2048, 2560, 2688, 2816
RQ, RK, RV, RZ = 3328, 3584, 3840, 4352
NQ, KC, VC, KS, VS, KW, VW = 4864, 5376, 5504, 5632, 5760, 5888, 6016
NG, NZ, MG = 6144, 6168, 6680
D_IN = MG + 4 * D
ZCOL = (MZ, SZ, RZ, NZ)
CHUNKS = MG // CW
TAIL = MG - CHUNKS * CW

LOOPED = 8
LATE = ((9, 10), (10, 11), (11, 9), (12, 12))

C_UNIT = (23, 24, 27, 28)
U_MERGE, UNITS = 30, 58
N_MERGE, N_BRANCH, N_OUT, SPLITS = 26, 42, 50, 54
WHOLE = SPLITS - 16


def raw_unit(n):
    return n + sum(u <= n + i for i, u in enumerate(C_UNIT))


C_ID, C_COS, C_SIN, C_DECAY = 0, 128, 384, 640
C_CADD, C_C01, C_BLK, C_COSK, C_SINK = 2176, 2206, 2236, 2238, 2302
N_CONST = 2366


ONE = 1


class Count:

    def __init__(self):
        self.base, self.n = 0, 0

    def at(self, base):
        self.base, self.n = base, 0

    def next(self):
        self.n += 1
        return self.base + self.n


ACC_ACT, ACC_DVE = 22, 16
DVE_PREP, DVE_TURN = 16, 39
POOL_PREP, POOL_TURN = 9, 21


def hybrid_trunk(nc, x, norm_g, w_in, w_branch, w_out, swa_sink, cmp_pos, w_ck1, w_ck2, w_cv1, w_cv2,
                 final_norm_g, consts, masks, out):
    with ExitStack() as ctx:
        top = [(nc.sbuf_base + 31) // 32 * 32]

        def at(name, shape, dt, offset):
            return nc.alloc_sbuf_tensor_at(name, shape, dt, offset=offset)

        def sb(name, shape, dt=F32):
            size = 2 if dt == BF16 else 4
            for n in shape[1:]:
                size *= n
            t = at(name, shape, dt, top[0])
            top[0] += (size + 31) // 32 * 32
            return t

        def sem(name):
            return ctx.enter_context(nc.semaphore(name))

        x_sb = sb("x_sb", [P, NT, D])
        hT_hi = sb("hT_hi", [P, KD, SEQ], F32R)
        hT_lo = sb("hT_lo", [P, KD, SEQ], F32R)
        raw = sb("raw", [P, 2, UNIT])
        w_hi = sb("w_hi", [P, 2, UNIT], F32R)
        w_lo = sb("w_lo", [P, 2, UNIT], F32R)
        proj_at = top[0]
        proj = sb("proj", [P, NT, MG])
        gates_at = top[0]
        gates = sb("gates", [P, NT, 4 * D])
        merged = gates[:, :, 0:D]
        con = sb("con", [P, N_CONST])
        ident = con[:, C_ID:C_ID + P]
        ident_b = sb("ident_b", [P, P], BF16)
        mask_b = sb("mask_b", [P, 2, 384], BF16)
        small = sb("small", [P, 8])
        g_col = sb("g_col", [P, LAYERS * KD])
        g_now = sb("g_now", [P, KD])
        act_warm = sb("act_warm", [P, 1])
        g_in = sb("g_in", [LAYERS * KD, P])
        neg_half = sb("neg_half", [P, NT])
        sink_in = sb("sink_in", [P, LAYERS * HEADS])
        sink = sb("sink", [P, LAYERS * HEADS, 2])
        nsink = sb("nsink", [P, LAYERS * HEADS, 2])
        nsa_g = sb("nsa_g", [P, NT, 24])
        pos_in = sb("pos_in", [16, P])
        kT_shared = sb("kT_shared", [HD, 3, 2, SEQ])
        kcT = sb("kcT", [HD, 2, NCMP])
        v_blk = sb("v_blk", [2 * NCMP, 2, P])
        tmp_rope = sb("tmp_rope", [P, NT, P])

        roped = sb("roped", [P, 5, NT, P])
        qkT_at = top[0]
        qkT = sb("qkT", [HD, 5, 2, SEQ])
        probs = sb("probs", [P, 2, 384])
        probsT = sb("probsT", [P, 2, 384])
        attT = sb("attT", [P, 384])
        zg = sb("zg", [P, 4, NT, P])
        nsa_sum = sb("nsa_sum", [P, NT, P])
        stat = sb("stat", [P, 4, 12])
        cmp_s = sb("cmp_s", [P, 4, NCMP])
        cmp_st = sb("cmp_st", [P, 4, 4])
        cmp_pT = sb("cmp_pT", [2 * NCMP, SEQ])
        ret_st = sb("ret_st", [P, 20])
        assert top[0] <= nc.sbuf_usable_end, (top[0], nc.sbuf_usable_end)

        g0 = gates_at + 1024 * 4
        g1 = gates_at + 5120 * 4
        h = at("h", [P, NT, D], F32, g0)
        k_shared = at("k_shared", [P, NT, 3, P], F32, g1 + 9216)
        g_row = at("g_row", [P, D], F32, g1)
        mask_f = at("mask_f", [P, 2 * 384], F32, g1 + 4096)
        dup = at("dup", [P, NT, 4, 2, HD], F32, g0)
        pairT = at("pairT", [P, 4, P], F32, g0 + 4096)
        blocksT = at("blocksT", [P, 2, 16, 2 * NCMP], F32, g0 + 6144)
        hid = at("hid", [2 * NCMP, 2 * 256], F32, g1)
        hid2 = at("hid2", [2 * NCMP, 2 * 256], F32, g1 + 2048)
        hid3 = at("hid3", [2 * NCMP, 2 * 256], F32, g1 + 4096)
        gkT = at("gkT", [P, 2, 2 * NCMP], F32, g1 + 6144)
        gvT = at("gvT", [P, 2, 2, 2, NCMP], F32, g1 + 6144 + 256)
        posT = at("posT", [P, 16], F32, g1 + 7168)
        kc_s = at("kc_s", [2 * NCMP, HD], F32, g1 + 7168 + 64)
        kc_t = at("kc_t", [2 * NCMP, HD], F32, g1 + 7168 + 320)
        kc_r = at("kc_r", [2 * NCMP, HD], F32, g1 + 7168 + 576)
        w_c2 = at("w_c2", [P, 2, 2, HD], F32, g1 + 8192)
        spots = [proj_at + 4 * (t * MG + c) for t in range(NT) for c in (0, 512, 1024, 2048, 3328, 3840, 4864, 5376)]
        yT_hi = [at(f"yT_hi{g}", [P, 2, SEQ], F32R, spots[g]) for g in range(8)]
        yT_lo = [at(f"yT_lo{g}", [P, 2, SEQ], F32R, spots[8 + g]) for g in range(8)]
        part = at("part", [P, NT, CW], F32, qkT_at)
        t_raw = at("t_raw", [P, KD, TAIL], F32, qkT_at)
        t_hl = at("t_hl", [P, KD * 2 * TAIL + P - 2 * TAIL], F32R, qkT_at + 768)
        t_parts = t_hl[:, 0:KD * 2 * TAIL].rearrange("p (k s n) -> p k s n", k=KD, s=2)
        t_sum = at("t_sum", [2 * TAIL, SEQ], F32, qkT_at + 2688)
        t_cols = at("t_cols", [P, NT, TAIL], F32, qkT_at + 3712)

        acc = [ctx.enter_context(nc.psum_tensor(f"acc{i}", [P, CW], F32)) for i in range(4)]
        score = [ctx.enter_context(nc.psum_tensor(f"score{i}", [P, CW], F32)) for i in range(2)]
        tbank = ctx.enter_context(nc.psum_tensor("tbank", [P, CW], F32))
        obank = ctx.enter_context(nc.psum_tensor("obank", [P, CW], F32))
        xbank = [score[0], score[1], tbank, obank]

        s_x = [sem("s_x0"), sem("s_x1")]
        s_con = sem("s_con")
        s_mask = sem("s_mask")
        s_id = sem("s_id")
        s_g = sem("s_g")
        s_g_row = sem("s_g_row")
        s_tail = sem("s_tail")
        s_pos = sem("s_pos")
        s_c2 = sem("s_c2")
        s_out = sem("s_out")
        raw_full = [sem("raw_full0"), sem("raw_full1")]
        hi_done = sem("hi_done")
        hi_piece = sem("hi_piece")
        lo_done = sem("lo_done")
        w_used = sem("w_used")
        cmp_used = sem("cmp_used")
        acc_act = sem("acc_act")
        acc_dve = sem("acc_dve")
        sq_done = sem("sq_done")
        g_T = sem("g_T")
        g_ready = sem("g_ready")
        half_rstd = sem("half_rstd")
        hi_first = sem("hi_first")
        lo_first = sem("lo_first")
        tail_hi = sem("tail_hi")
        tail_lo = sem("tail_lo")
        tail_done = sem("tail_done")
        tail_T = sem("tail_T")
        x_full = sem("x_full")
        x_hi = sem("x_hi")
        x_lo = sem("x_lo")
        setup_done = sem("setup_done")
        dve_step = sem("dve_step")
        pool_step = sem("pool_step")
        rstd_norm = sem("rstd_norm")
        var_norm = sem("var_norm")
        keys_roped = sem("keys_roped")
        keys_T = sem("keys_T")
        keys_out = sem("keys_out")
        dup_done = sem("dup_done")
        dup_T = sem("dup_T")
        blocks_done = sem("blocks_done")
        hid_sb = sem("hid_sb")
        hid_tanh = sem("hid_tanh")
        gelu_done = sem("gelu_done")
        gelu_T = sem("gelu_T")
        gelu_out = sem("gelu_out")
        cmp_kv = sem("cmp_kv")
        cmp_roped = sem("cmp_roped")
        kcT_full = sem("kcT_full")
        cmp_ready = sem("cmp_ready")
        tail_tanh = sem("tail_tanh")
        gates_nsa = sem("gates_nsa")
        q_roped = sem("q_roped")
        tq_done = sem("tq_done")
        t_full = sem("t_full")
        t_free = sem("t_free")
        s_full = sem("s_full")
        max_done = sem("max_done")
        exp_done = sem("exp_done")
        sink_exp = sem("sink_exp")
        s_dve = sem("s_dve")
        att_done = sem("att_done")
        cmp_sub = sem("cmp_sub")
        cmp_exp = sem("cmp_exp")
        cmp_p = sem("cmp_p")
        o_full = sem("o_full")
        o_free = sem("o_free")
        z_tanh = sem("z_tanh")
        z_done = sem("z_done")
        y_done = sem("y_done")
        var_ret = sem("var_ret")
        rstd_ret = sem("rstd_ret")
        part_full = sem("part_full")
        part_added = sem("part_added")
        first_part = sem("first_part")
        y_final = sem("y_final")

        w_in_v = w_in.rearrange("l (h k p) n -> l h p k n", k=UNIT_K, p=P)
        w_br_v = w_branch.rearrange("l (i k p) n -> l i p k n", k=UNIT_K, p=P)
        w_out_v = w_out.rearrange("l (h k p) n -> l h p k n", k=UNIT_K, p=P)
        w_k1_v = w_ck1.rearrange("l (h k p) n -> l h p k n", k=8, p=P)
        w_v1_v = w_cv1.rearrange("l (h k p) n -> l h p k n", k=8, p=P)

        def slot4(buf, u):
            return buf[:, u % 2, :].rearrange("p (k n) -> p k n", k=UNIT_K)

        def slot8(buf, u):
            return buf[:, u % 2, :].rearrange("p (k n) -> p k n", k=8)

        ITEMS = [("ret", 0), ("moba", 0), ("swa", 0), ("cmp", 0), ("slc", 0), ("win", 0),
                 ("moba", 1), ("swa", 1), ("slc", 1), ("win", 1)]
        SOFT = {k: e for e, k in enumerate([1, 2, 4, 5, 6, 7, 8, 9])}
        SOFT_K = list(SOFT)
        S_AT, P_AT, O_AT, SLOTS = 3, 5, 6, 16
        PIECES = ((0, 1), (2, 3), (), ())
        KIND = {"moba": 1, "swa": 3, "slc": 4, "win": 4}
        VCOL = {"moba": MV, "swa": SV, "slc": VS, "win": VW}
        KEYS = {"swa": 0, "slc": 1, "win": 2}
        T_FILLS = 5 + 9

        def settle(eng):
            eng.nop(nofuse=True)

        block = ctx.enter_context(nc.Block())

        @block.sync
        def _(sp):
            sp.dma_start(ident, consts[:, C_ID:C_ID + P]).then_inc(s_id, 16)
            sp.dma_start(g_in[:, :], norm_g.rearrange("l (k p) -> (l k) p", p=P)).then_inc(s_g, 16)
            for half in range(2):
                cols = slice(half * CW, (half + 1) * CW)
                sp.dma_start(x_sb[:, :, cols], x[0].rearrange("(t p) d -> p t d", p=P)[:, :, cols]).then_inc(s_x[half], 16)

            def load(src, dst, u):
                sp.dma_start(dst, src).then_inc(raw_full[u % 2], 16)

            with sp.Fori(0, LAYERS) as l:
                for i in range(2):
                    sp.wait_ge(lo_done, l * SPLITS + (i + 1))
                    load(w_in_v[l, i, :, :, 0:CW], slot4(raw, i), i)
                sp.dma_start(pos_in[:, :], cmp_pos[l].rearrange("(k a) d -> k (a d)", a=2)).then_inc(s_pos, 16)
                with sp.Fori(0, LOOPED // 2) as c:
                    for i in range(4):
                        sp.wait_ge(lo_done, l * SPLITS + c * 4 + (i + 3))
                        load(w_in_v[l, i % 2, :, :, bass.ds(c * 2 * CW + (i // 2 + 1) * CW, CW)], slot4(raw, i), i)
                sp.wait_ge(x_lo, l * 16 + (4 + ONE))
                sp.dma_start(t_raw[:, :, :], w_in[l].rearrange("(k p) n -> p k n", p=P)[:, :, CHUNKS * CW:MG]
                             ).then_inc(s_tail, 16)
                for i, w2 in enumerate((w_ck2, w_cv2)):
                    sp.dma_start(w_c2[:, i, :, :], w2[l].rearrange("(k p) n -> p k n", p=P)).then_inc(s_c2, 16)
                for u in range(18, U_MERGE):
                    if u - 2 in C_UNIT:
                        sp.wait_ge(cmp_used, l * 4 + (C_UNIT.index(u - 2) + 1))
                    else:
                        sp.wait_ge(lo_done, l * SPLITS + (u - 2 - sum(v < u - 2 for v in C_UNIT) + 1 + 2))
                    if u in C_UNIT:
                        i = C_UNIT.index(u)
                        load((w_k1_v, w_v1_v)[i // 2][l, i % 2], slot8(raw, u), u)
                    else:
                        n = u - sum(v < u for v in C_UNIT)
                        chunk = LATE[n // 2 - 9][1]
                        load(w_in_v[l, n % 2, :, :, chunk * CW:(chunk + 1) * CW], slot4(raw, u), u)
                sp.wait_ge(cmp_used, l * 4 + 4)
                settle(sp)
                with sp.Fori(0, 4) as j:
                    for i in range(4):
                        sp.wait_ge(lo_done, l * SPLITS + j * 4 + (N_MERGE + i + 1))
                        load(w_in_v[l, i % 2, :, :, bass.ds(j * 2 * CW + (MG + i // 2 * CW), CW)], slot4(raw, i), i)
                for v in range(8):
                    sp.wait_ge(lo_done, l * SPLITS + (N_BRANCH + v + 1))
                    c, i = divmod(v, 4)
                    load(w_br_v[l, i, :, :, c * CW:(c + 1) * CW], slot4(raw, v), v)
                for v in range(4):
                    sp.wait_ge(lo_done, l * SPLITS + (N_OUT + v + 1))
                    kh, c = divmod(v, 2)
                    load(w_out_v[l, kh, :, :, c * CW:(c + 1) * CW], slot4(raw, v), v)
            sp.wait_ge(x_lo, LAYERS * 16 + ONE)
            sp.dma_start(g_row[:, :], final_norm_g.partition_broadcast(P)).then_inc(s_g_row, 16)
            for t in range(NT):
                sp.wait_ge(y_final, t + 1)
                sp.dma_start(out[0, t * P:(t + 1) * P, :], h[:, t, :]).then_inc(s_out, 16)
            sp.wait_ge(s_out, NT * 16)

        @block.gpsimd
        def _(pool):
            steps = Count()

            def rotate(dst, src):
                cos = con[:, C_COS:C_COS + 2 * P].rearrange("p (t n) -> p t n", t=NT)
                sin = con[:, C_SIN:C_SIN + 2 * P].rearrange("p (t a f n) -> p t a f n", t=NT, a=2, f=2)
                s = src.rearrange("p t (a f n) -> p t a f n", a=2, f=2)
                m = tmp_rope[:, :, :].rearrange("p t (a f n) -> p t a f n", a=2, f=2)
                nc.gpsimd.tensor_tensor(m[:, :, :, 0], s[:, :, :, 1], sin[:, :, :, 0], ALU.mult).then_inc(pool_step, 1)
                steps.next()
                nc.gpsimd.tensor_tensor(m[:, :, :, 1], s[:, :, :, 0], sin[:, :, :, 1], ALU.mult).then_inc(pool_step, 1)
                pool.wait_ge(pool_step, steps.next())
                settle(pool)
                nc.gpsimd.tensor_tensor(dst, src, cos, ALU.mult).then_inc(pool_step, 1)
                pool.wait_ge(pool_step, steps.next())
                return nc.gpsimd.tensor_tensor(dst, dst, tmp_rope[:, :, :], ALU.add)

            def norm_rstd(i):
                pool.wait_ge(var_norm, i + 1)
                nc.gpsimd.tensor_tensor(small[:, 4:6], small[:, 2:4], neg_half[:, :], ALU.pow).then_inc(rstd_norm, 1)

            pool.sem_inc(part_added, ONE)
            pool.wait_ge(raw_full[0], 16)
            pool.dma_start(mask_f[:, :], masks).then_inc(s_mask, 16)
            pool.dma_start(sink_in[:, :], swa_sink.rearrange("l h -> (l h)").partition_broadcast(P)).then_inc(s_mask, 16)
            nc.gpsimd.memset(neg_half[:, :], -0.5).then_inc(pool_step, 1)
            pool.wait_ge(s_id, 16)
            nc.gpsimd.tensor_copy(ident_b[:, :], ident)
            pool.wait_ge(s_mask, 32)
            nc.gpsimd.tensor_copy(mask_b[:, :, :], mask_f[:, :].rearrange("p (m n) -> p m n", m=2))
            for i in range(2):
                nc.gpsimd.tensor_copy(sink[:, :, i], sink_in[:, :])
                ins = nc.gpsimd.tensor_scalar(nsink[:, :, i], sink_in[:, :], -1.0, None, ALU.mult)
            ins.then_inc(setup_done, 1)
            pool.dma_start(con[:, P:N_CONST], consts[:, P:N_CONST]).then_inc(s_con, 16)
            pool.wait_ge(setup_done, 1)
            pool.wait_ge(pool_step, 1)
            per = POOL_PREP + 4 * POOL_TURN
            with pool.Fori(0, LAYERS) as l:
                norm_rstd(l)
                pool.wait_ge(s_con, 16)
                steps.at(l * per + 1)
                pool.wait_ge(acc_act, l * ACC_ACT + (2 + 11))
                pool.wait_ge(acc_dve, l * ACC_DVE + (2 + 11))
                for i, col in enumerate((SK, KS, KW)):
                    rotate(k_shared[:, :, i, :], proj[:, :, col:col + P]).then_inc(keys_roped, 1)
                    pool.wait_ge(keys_roped, l * 3 + (i + 1))
                settle(pool)
                assert steps.n == POOL_PREP, steps.n
                with pool.Fori(0, 4) as j:
                    steps.at(l * per + j * POOL_TURN + (1 + POOL_PREP))
                    pool.wait_ge(acc_act, l * ACC_ACT + (2 + 13))
                    pool.wait_ge(acc_dve, l * ACC_DVE + (2 + 12))
                    pool.wait_ge(tq_done, l * 4 + j + ONE)
                    rotate(roped[:, 1, :, :], proj[:, :, bass.ds(j * P + MQ, P)]).then_inc(q_roped, 1)
                    pool.wait_ge(q_roped, (l * 4 + j) * 5 + 1)
                    rotate(roped[:, 2, :, :], proj[:, :, bass.ds(j * P + MK, P)]).then_inc(q_roped, 1)
                    pool.wait_ge(q_roped, (l * 4 + j) * 5 + 2)
                    rotate(roped[:, 3, :, :], proj[:, :, bass.ds(j * P + SQ, P)]).then_inc(q_roped, 1)
                    pool.wait_ge(q_roped, (l * 4 + j) * 5 + 3)
                    rotate(roped[:, 4, :, :], proj[:, :, bass.ds(j * P + NQ, P)]).then_inc(q_roped, 1)
                    pool.wait_ge(q_roped, (l * 4 + j) * 5 + 4)
                    for f, col in ((0, RQ), (1, RK)):
                        nc.gpsimd.tensor_copy(roped[:, 0, :, f * HD:(f + 1) * HD],
                                              proj[:, :, bass.ds(j * HD + col, HD)]).then_inc(pool_step, 1)
                        v = steps.next()
                    pool.wait_ge(pool_step, v)
                    rotate(roped[:, 0, :, :], roped[:, 0, :, :]).then_inc(q_roped, 1)
                    pool.wait_ge(q_roped, (l * 4 + j) * 5 + 5)
                    for n, b in enumerate((2, 0, 1, 3)):
                        pool.wait_ge(z_tanh, (l * 4 + j) * 4 + n + 1)
                        settle(pool)
                        nc.gpsimd.tensor_scalar(zg[:, b, :, :], zg[:, b, :, :], 1.0, 0.25, ALU.add,
                                                ALU.mult).then_inc(pool_step, 1)
                        pool.wait_ge(pool_step, steps.next())
                        nc.gpsimd.tensor_tensor(zg[:, b, :, :], zg[:, b, :, :], proj[:, :, bass.ds(j * P + ZCOL[b], P)],
                                                ALU.mult).then_inc(z_done, 1)
                        if n == 1:
                            pool.wait_ge(var_ret, l * 4 + j + 1)
                            nc.gpsimd.tensor_tensor(ret_st[:, 18:20], ret_st[:, 16:18], neg_half[:, :], ALU.pow
                                                    ).then_inc(rstd_ret, 1)
                    assert steps.n == POOL_TURN, steps.n
                for v in range(8):
                    c, i = divmod(v, 4)
                    if i == 0:
                        continue
                    m = c * 6 + (i - 1) * 2
                    if i == 1:
                        pool.wait_ge(first_part, l * 4 + c * 2 + 2)
                    for t in range(NT):
                        pool.wait_ge(part_full, l * 12 + (m + t + 1))
                        if i > 1:
                            pool.wait_ge(part_added, l * 12 + (m + t - 1 + ONE))
                        nc.gpsimd.tensor_tensor(merged[:, t, c * CW:(c + 1) * CW], merged[:, t, c * CW:(c + 1) * CW],
                                                part[:, t, :], ALU.add).then_inc(part_added, 1)
            norm_rstd(LAYERS)

        @block.scalar
        def _(act):
            def split_hi(n, u, l):
                act.wait_ge(raw_full[u[1]], (l * (UNITS // 2) + u[0]) * 16 + 16)
                act.wait_ge(w_used, l * SPLITS + n[0] + 1)
                nc.scalar.activation(w_hi[:, n[1], :], raw[:, u[1], :], ACT.Copy).then_inc(hi_done, 1)

            def ahead(n, l):
                u = raw_unit(n)
                split_hi((n, n % 2), (u // 2, u % 2), l)

            def xgroup_hi(g, dst, l):
                act.wait_ge(x_full, l * 16 + (g + 1))
                nc.scalar.activation(dst, xbank[g % 4][:, :], ACT.Copy).then_inc(x_hi, 1)

            def squares(count):
                act.wait_ge(acc_dve, count * ACC_DVE + 2)
                for t in range(NT):
                    nc.scalar.activation(h[:, t, :], x_sb[:, t, :], ACT.Square,
                                         accum_out=small[:, t:t + 1]).then_inc(sq_done, 1)

            def columns_out(count, bank, cols):
                act.wait_ge(w_used, count)
                nc.scalar.activation(proj[:, 0, cols], acc[bank][:, :], ACT.Copy, scale=small[:, 4:5]).then_inc(acc_act, 1)

            act.sem_inc(acc_act, 2)
            for first in (t_free, exp_done):
                act.sem_inc(first, ONE)
            act.wait_ge(s_id, 16)
            nc.scalar.activation(act_warm[:, :], ident[:, 0:1], ACT.Tanh)
            act.wait_ge(s_x[0], 16)
            act.wait_ge(s_x[1], 16)
            with act.Fori(0, LAYERS) as l:
                def xgain_hi(g):
                    act.wait_ge(x_full, l * 16 + (g + 1))
                    for k in range(2):
                        ins = nc.scalar.activation(hT_hi[:, 2 * g + k, :], xbank[g][:, k * SEQ:(k + 1) * SEQ], ACT.Copy,
                                                   scale=g_now[:, 2 * g + k:2 * g + k + 1])
                    ins.then_inc(x_hi, 1)

                act.wait_ge(g_ready, l + 1)
                for n in range(2):
                    for m in range(UNIT_K):
                        if n == 0 and m % 2 == 0:
                            xgain_hi(m // 2)
                        if m == 0:
                            if n == 1:
                                xgain_hi(2)
                                xgain_hi(3)
                            act.wait_ge(raw_full[n], l * (UNITS // 2 * 16) + 16)
                            act.wait_ge(w_used, l * SPLITS + (n + 1))
                        cols = slice(m * CW, (m + 1) * CW)
                        nc.scalar.activation(w_hi[:, n, cols], raw[:, n, cols], ACT.Copy
                                             ).then_inc(hi_first if m < UNIT_K - 1 else hi_done, 1)
                squares(l)
                ahead(2, l)
                ahead(3, l)
                act.wait_ge(rstd_norm, l + 1)
                columns_out(l * SPLITS + (2 + 2), 0, slice(0, CW))
                with act.Fori(0, LOOPED // 2) as c:
                    for i in range(2):
                        for m in range(2):
                            n = c * 4 + (2 * i + m + 4)
                            split_hi((n, m), (c * 2 + (i + 2), m), l)
                        columns_out(l * SPLITS + c * 4 + (2 * i + 4 + 2), 2 - 2 * i,
                                    bass.ds(c * 2 * CW + (i + 1) * CW, CW))
                act.wait_ge(s_tail, l * 16 + 16)
                nc.scalar.activation(t_parts[:, :, 0, :], t_raw[:, :, :], ACT.Copy)
                nc.scalar.activation(t_hl[:, KD * 2 * TAIL:], t_raw[:, :, :].rearrange("p k n -> p (k n)")[:, 0:P - 2 * TAIL],
                                     ACT.Copy).then_inc(tail_hi, 1)
                for q, chunk in LATE:
                    for n in (2 * q + 2, 2 * q + 3):
                        if n < N_MERGE and n != 23:
                            ahead(n, l)
                    if q == 12:
                        for i in range(3):
                            act.wait_ge(keys_T, l * 3 + (i + 1))
                            nc.scalar.activation(kT_shared[:, i, :, :], xbank[i + 1][0:HD, :], ACT.Copy).then_inc(keys_out, 1)
                        act.wait_ge(hid_sb, l + 1)
                        nc.scalar.activation(hid3[:, :], hid2[:, :], ACT.Tanh, scale=0.7978845608028654).then_inc(hid_tanh, 1)
                        ahead(N_MERGE, l)
                    columns_out(l * SPLITS + (2 * q + 2 + 2), 2 * (q % 2), slice(chunk * CW, (chunk + 1) * CW))
                    if q == 10:
                        act.wait_ge(tail_done, l + 1)
                        nc.scalar.activation(t_sum[:, :], acc[2][0:2 * TAIL, 0:SEQ], ACT.Copy).then_inc(acc_act, 1)
                        ahead(23, l)
                act.wait_ge(acc_act, l * ACC_ACT + (2 + 14))
                act.wait_ge(acc_dve, l * ACC_DVE + (2 + 14))
                nc.scalar.activation(nsa_g[:, :, :], proj[:, :, NG:NG + 24], ACT.Tanh, scale=0.5).then_inc(tail_tanh, 1)
                act.wait_ge(half_rstd, l + 1)
                with act.Fori(0, 4) as j:
                    turn = l * 4 + j

                    def t_out(f, dst, src, scale=1.0):
                        act.wait_ge(t_full, turn * T_FILLS + (f + 1 + ONE))
                        nc.scalar.activation(dst, src, ACT.Copy, scale=scale).then_inc(t_free, 1)

                    def gate_out(i):
                        act.wait_ge(w_used, l * SPLITS + j * 4 + (N_MERGE + 2 * i + 2 + 2))
                        for t in range(NT):
                            ins = nc.scalar.activation(gates[:, t, bass.ds(j * 2 * CW + i * CW, CW)],
                                                       acc[2 * i + t][:, :], ACT.Tanh, scale=small[:, 6 + t:7 + t])
                        ins.then_inc(acc_act, 1)

                    for s in range(SLOTS + 1):
                        i = s // 4 + 1
                        if s % 4 == 0 and s < SLOTS:
                            act.wait_ge(raw_full[i % 2], (l * (UNITS // 2) + j * 2 + (U_MERGE + i) // 2) * 16 + 16)
                            act.wait_ge(w_used, l * SPLITS + j * 4 + (N_MERGE + i + 1))
                        for m in (PIECES[s % 4] if s < SLOTS else ()):
                            nc.scalar.activation(w_hi[:, i % 2, m * CW:(m + 1) * CW], raw[:, i % 2, m * CW:(m + 1) * CW],
                                                 ACT.Copy).then_inc(hi_piece, 1)
                        if s < 5:
                            if s == 0:
                                act.wait_ge(t_full, turn * T_FILLS + (1 + ONE))
                                nc.scalar.activation(qkT[:, 0, 0, :], tbank[0:HD, 0:SEQ], ACT.Copy, scale=0.125)
                                nc.scalar.activation(qkT[:, 0, 1, :], tbank[0:HD, SEQ:2 * SEQ],
                                                     ACT.Copy).then_inc(t_free, 1)
                            else:
                                t_out(s, qkT[:, s, :, :], tbank[0:HD, :], 1.0 if s == 2 else 0.125)
                        if s == 2:
                            act.wait_ge(y_done, turn + ONE)
                            for b in (2, 0, 1, 3):
                                nc.scalar.activation(zg[:, b, :, :], proj[:, :, bass.ds(j * P + ZCOL[b], P)],
                                                     ACT.Tanh, scale=0.5).then_inc(z_tanh, 1)
                        k = s - S_AT
                        if k in SOFT:
                            e = SOFT[k]
                            act.wait_ge(max_done, turn * 8 + (e + 1))
                            act.wait_ge(t_full, turn * T_FILLS + ((SOFT_K[e - 2] + 5 if e > 1 else 0) + ONE))
                            for t, (a, b) in enumerate(((0, P), (P, 384))):
                                ins = nc.scalar.activation(probs[:, e % 2, a:b], score[k % 2][:, a:b], ACT.Exp,
                                                           bias=stat[:, e % 4, t:t + 1],
                                                           accum_out=stat[:, e % 4, 2 + t:3 + t])
                            ins.then_inc(exp_done, 1)
                            if ITEMS[k][0] == "swa":
                                nc.scalar.activation(stat[:, e % 4, 6:8], stat[:, e % 4, 4:6],
                                                     ACT.Exp).then_inc(sink_exp, 1)
                        elif 0 <= k < 10 and ITEMS[k][0] == "cmp":
                            act.wait_ge(cmp_sub, turn + 1)
                            nc.scalar.activation(cmp_s[:, :, :], cmp_s[:, :, :], ACT.Exp).then_inc(cmp_exp, 1)
                        k = s - P_AT
                        if 1 <= k < 10:
                            if k in SOFT:
                                t_out(4 + k, probsT[:, SOFT[k] % 2, :], tbank[:, 0:384])
                            else:
                                t_out(4 + k, cmp_pT[:, :], tbank[0:2 * NCMP, 0:SEQ])
                        if s == 8:
                            gate_out(0)
                        if s == SLOTS:
                            gate_out(1)
                for g in range(4):
                    xgroup_hi(4 + g, yT_hi[g][:, :, :], l)
                for v in range(8):
                    ahead(N_BRANCH + v + 1, l)
                    if v < 2:
                        for g in (4 + 2 * v, 5 + 2 * v):
                            xgroup_hi(4 + g, yT_hi[g][:, :, :], l)
                    if v == 5:
                        for g in range(2):
                            xgroup_hi(12 + g, hT_hi[:, 2 * g:2 * g + 2, :], l)
                ahead(N_OUT + 1, l)
                for g in range(2, 4):
                    xgroup_hi(12 + g, hT_hi[:, 2 * g:2 * g + 2, :], l)
                ahead(N_OUT + 2, l)
                ahead(N_OUT + 3, l)
            squares(LAYERS)

        @block.vector
        def _(dve):
            steps = Count()

            def chain(ins):
                ins.then_inc(dve_step, 1)
                return steps.next()

            def split_lo(parity, done, cols=UNIT):
                dve.wait_ge(hi_done, done)
                nc.vector.tensor_tensor(w_lo[:, parity, 0:cols], raw[:, parity, 0:cols],
                                        w_hi[:, parity, 0:cols].bitcast(F32), ALU.subtract).then_inc(lo_done, 1)

            def xgroup_lo(g, hi, lo, l):
                dve.wait_ge(x_hi, l * 16 + (g + 1))
                bank = xbank[g % 4][:, :].rearrange("p (k n) -> p k n", k=2)
                nc.vector.tensor_tensor(lo, bank, hi.bitcast(F32), ALU.subtract).then_inc(x_lo, 1)

            def mean_square(i):
                dve.wait_ge(sq_done, i * 2 + 2)
                nc.vector.tensor_scalar(small[:, 2:4], small[:, 0:2], 1.0 / D, EPS, ALU.mult,
                                        ALU.add).then_inc(var_norm, 1)
                dve.wait_ge(rstd_norm, i + 1)

            def columns_out(count, bank, cols):
                dve.wait_ge(w_used, count)
                nc.vector.tensor_scalar(proj[:, 1, cols], acc[bank][:, :], small[:, 5:6], None, ALU.mult).then_inc(acc_dve, 1)

            dve.sem_inc(lo_done, 2)
            for first in (x_lo, y_done, o_free):
                dve.sem_inc(first, ONE)
            dve.sem_inc(acc_dve, 2)
            dve.wait_ge(g_T, 1)
            nc.vector.tensor_copy(g_col[:, :], score[0][:, 0:LAYERS * KD]).then_inc(dve_step, 1)
            dve.wait_ge(dve_step, 1)
            per = DVE_PREP + 4 * DVE_TURN
            with dve.Fori(0, LAYERS) as l:
                nc.vector.tensor_copy(g_now[:, :], g_col[:, bass.ds(l * KD, KD)]).then_inc(g_ready, 1)
                dve.wait_ge(g_ready, l + 1)

                def xgain_lo(g):
                    dve.wait_ge(x_hi, l * 16 + (g + 1))
                    for k in range(2 * g, 2 * g + 2):
                        ins = nc.vector.scalar_tensor_tensor(hT_lo[:, k, :], xbank[g][:, k % 2 * SEQ:(k % 2 + 1) * SEQ],
                                                             g_now[:, k:k + 1], hT_hi[:, k, :].bitcast(F32), ALU.mult,
                                                             ALU.subtract)
                    ins.then_inc(x_lo, 1)

                for n in range(2):
                    for m in range(UNIT_K):
                        if n == 0 and m % 2 == 0:
                            xgain_lo(m // 2)
                        if n == 1 and m == 0:
                            xgain_lo(2)
                            xgain_lo(3)
                        if m < UNIT_K - 1:
                            dve.wait_ge(hi_first, l * 6 + (n * 3 + m + 1))
                        else:
                            dve.wait_ge(hi_done, l * WHOLE + (n + 1))
                        cols = slice(m * CW, (m + 1) * CW)
                        nc.vector.tensor_tensor(w_lo[:, n, cols], raw[:, n, cols], w_hi[:, n, cols].bitcast(F32),
                                                ALU.subtract).then_inc(lo_first if m < UNIT_K - 1 else lo_done, 1)
                mean_square(l)
                nc.vector.tensor_scalar(small[:, 6:8], small[:, 4:6], 0.5, None, ALU.mult).then_inc(half_rstd, 1)
                for n in (2, 3):
                    split_lo(n % 2, l * WHOLE + (n + 1))
                columns_out(l * SPLITS + (2 + 2), 1, slice(0, CW))
                with dve.Fori(0, LOOPED // 2) as c:
                    for i in range(2):
                        for m in range(2):
                            split_lo(m, l * WHOLE + c * 4 + (2 * i + m + 5))
                        columns_out(l * SPLITS + c * 4 + (2 * i + 4 + 2), 3 - 2 * i, bass.ds(c * 2 * CW + (i + 1) * CW, CW))

                def late(q):
                    for n in (2 * q + 2, 2 * q + 3):
                        if n < N_MERGE:
                            split_lo(n % 2, l * WHOLE + (n + 1))
                    chunk = LATE[q - 9][1]
                    columns_out(l * SPLITS + (2 * q + 2 + 2), 2 * (q % 2) + 1, slice(chunk * CW, (chunk + 1) * CW))

                late(9)
                dve.wait_ge(tail_hi, l + 1)
                nc.vector.tensor_tensor(t_parts[:, :, 1, :], t_raw[:, :, :], t_parts[:, :, 0, :].bitcast(F32),
                                        ALU.subtract).then_inc(tail_lo, 1)
                steps.at(l * per + 1)
                dve.wait_ge(s_con, 16)
                dve.wait_ge(acc_act, l * ACC_ACT + (2 + 10))
                dve.wait_ge(acc_dve, l * ACC_DVE + (2 + 10))
                for a in range(2):
                    for t in range(NT):
                        ins = nc.vector.tensor_copy(dup[:, t, :, a, :],
                                                    proj[:, t, KC:KC + 2 * P].rearrange("p (s n) -> p s n", n=HD))
                ins.then_inc(dup_done, 1)
                split_lo(0, l * WHOLE + (22 + 1))
                for t, bank in enumerate((obank, tbank)):
                    dve.wait_ge(dup_T, l * 3 + (t + 1))
                    for odd in range(2):
                        rows = slice(odd * HD, (odd + 1) * HD)
                        v = chain(nc.vector.tensor_copy(
                            pairT[rows, :, t * HD:(t + 1) * HD],
                            bank[rows, :].rearrange("p (s n two) -> p s n two", s=4, two=2)[:, :, :, odd]))
                dve.wait_ge(dup_T, l * 3 + 3)
                v = chain(nc.vector.tensor_copy(posT[:, :], score[1][:, 0:16]))
                dve.wait_ge(dve_step, v)
                for s in range(2):
                    for half in range(2):
                        src = pairT[:, 2 * s:2 * s + 2, :].rearrange("p v (n k) -> p k v n", k=8)[:, :, :, half:half + NCMP]
                        dst = blocksT[:, s, half * 8:half * 8 + 8, :].rearrange("p k (v n) -> p k v n", v=2)
                        pos = posT[:, half * 8:half * 8 + 8].unsqueeze(2).unsqueeze(3).to_broadcast([P, 8, 2, NCMP])
                        ins = nc.vector.tensor_tensor(dst, src, pos, ALU.add)
                ins.then_inc(blocks_done, 1)
                columns_out(l * SPLITS + (22 + 2), 1, slice(11 * CW, 12 * CW))
                split_lo(1, l * WHOLE + (23 + 1))
                split_lo(0, l * WHOLE + (24 + 1))
                columns_out(l * SPLITS + (24 + 2), 3, slice(9 * CW, 10 * CW))
                split_lo(1, l * WHOLE + (25 + 1))
                dve.wait_ge(cmp_used, l * 4 + 4)
                v = chain(nc.vector.tensor_copy(hid[:, :], score[0][0:2 * NCMP, :]))
                dve.wait_ge(dve_step, v)
                v = chain(nc.vector.tensor_tensor(hid2[:, :], hid[:, :], hid[:, :], ALU.mult))
                dve.wait_ge(dve_step, v)
                v = chain(nc.vector.tensor_scalar(hid2[:, :], hid2[:, :], 0.044715, 1.0, ALU.mult, ALU.add))
                dve.wait_ge(dve_step, v)
                nc.vector.tensor_tensor(hid2[:, :], hid2[:, :], hid[:, :], ALU.mult).then_inc(hid_sb, 1)
                dve.wait_ge(hid_tanh, l + 1)
                nc.vector.scalar_tensor_tensor(hid2[:, :], hid3[:, :], 1.0, hid[:, :], ALU.add,
                                               ALU.mult).then_inc(gelu_done, 1)
                dve.wait_ge(gelu_T, l + 1)
                gT = obank[:, :].rearrange("p (f n) -> p f n", f=4)
                nc.vector.tensor_copy(gkT[:, :, :], gT[:, 0:2, 0:2 * NCMP])
                for a in range(2):
                    ins = nc.vector.tensor_copy(gvT[:, :, :, a, :],
                                                gT[:, 2:4, 0:2 * NCMP].rearrange("p f (v n) -> p f v n", v=2))
                ins.then_inc(gelu_out, 1)
                columns_out(l * SPLITS + (26 + 2), 1, slice(12 * CW, 13 * CW))
                dve.wait_ge(cmp_kv, l + 1)
                v = chain(nc.vector.tensor_scalar(kc_s[:, :], score[0][0:2 * NCMP, 0:HD], 0.5, None, ALU.mult))
                for kv in range(2):
                    blk = con[0:2 * NCMP, C_BLK:C_BLK + 2].unsqueeze(2).to_broadcast([2 * NCMP, 2, HD])
                    val = score[1][0:2 * NCMP, kv * HD:(kv + 1) * HD].unsqueeze(1).to_broadcast([2 * NCMP, 2, HD])
                    last = chain(nc.vector.tensor_tensor(v_blk[:, kv, :].rearrange("p (a n) -> p a n", a=2), val, blk,
                                                         ALU.mult))
                dve.wait_ge(dve_step, v)
                sin = con[0:2 * NCMP, C_SINK:C_SINK + HD]
                chain(nc.vector.tensor_tensor(kc_t[:, 0:32], kc_s[:, 32:64], sin[:, 0:32], ALU.mult))
                chain(nc.vector.tensor_tensor(kc_t[:, 32:64], kc_s[:, 0:32], sin[:, 32:64], ALU.mult))
                v = chain(nc.vector.tensor_tensor(kc_r[:, :], kc_s[:, :], con[0:2 * NCMP, C_COSK:C_COSK + HD], ALU.mult))
                dve.wait_ge(dve_step, v)
                nc.vector.tensor_tensor(kc_r[:, :], kc_r[:, :], kc_t[:, :], ALU.add).then_inc(cmp_roped, 1)
                split_lo(0, l * WHOLE + (N_MERGE + 1))
                dve.wait_ge(tail_T, l + 1)
                parts = acc[3][:, 0:NT * 2 * TAIL].rearrange("p (t s n) -> p t s n", t=NT, s=2)
                v = chain(nc.vector.tensor_copy(t_cols[:, :, :], parts[:, :, 0, :]))
                dve.wait_ge(dve_step, v)
                v = chain(nc.vector.tensor_tensor(t_cols[:, :, :], t_cols[:, :, :], parts[:, :, 1, :], ALU.add))
                dve.wait_ge(dve_step, v)
                for t in range(NT):
                    ins = nc.vector.tensor_scalar(proj[:, t, CHUNKS * CW:MG], t_cols[:, t, :], small[:, 4 + t:5 + t], None,
                                                  ALU.mult)
                ins.then_inc(acc_dve, 1)
                dve.wait_ge(tail_tanh, l + 1)
                nc.vector.tensor_scalar(nsa_g[:, :, :], nsa_g[:, :, :], 1.0, 0.5, ALU.add, ALU.mult).then_inc(gates_nsa, 1)
                dve.wait_ge(kcT_full, l + 1)
                nc.vector.tensor_copy(kcT[:, :, :], score[1][0:HD, 0:2 * NCMP].rearrange("p (v n) -> p v n", v=2)
                                      ).then_inc(cmp_ready, 1)
                prep_n = steps.n
                dve.wait_ge(setup_done, 1)
                with dve.Fori(0, 4) as j:
                    turn = l * 4 + j
                    steps.at(l * per + j * DVE_TURN + (1 + DVE_PREP))

                    def per_tile(col):
                        return con[:, col:col + 2 * NCMP].rearrange("p (t n) -> p t n", t=NT).unsqueeze(2
                            ).to_broadcast([P, NT, 2, NCMP])

                    def cmp_rest():
                        cs = cmp_s[:, :, :].rearrange("p (t a) n -> p t a n", t=NT)
                        dve.wait_ge(cmp_exp, turn + 1)
                        nc.vector.tensor_tensor(cs, cs, per_tile(C_C01), ALU.mult).then_inc(cmp_p, 1)
                        dve.wait_ge(cmp_p, turn + 1)
                        v = chain(nc.vector.tensor_reduce(cmp_st[:, :, 1], cmp_s[:, :, :], AX.X, ALU.add))
                        dve.wait_ge(dve_step, v)
                        v = chain(nc.vector.tensor_scalar(cmp_st[:, :, 2], cmp_st[:, :, 1], TINY, None, ALU.max))
                        dve.wait_ge(dve_step, v)
                        v = chain(nc.vector.reciprocal(cmp_st[:, :, 3], cmp_st[:, :, 2]))
                        dve.wait_ge(dve_step, v)
                        chain(nc.vector.tensor_tensor(
                            cmp_st[:, :, 2].rearrange("p (t a) -> p t a", t=NT),
                            cmp_st[:, :, 3].rearrange("p (t a) -> p t a", t=NT),
                            nsa_g[:, :, bass.ds(j * 2, 2)], ALU.mult))

                    def ret_rest():
                        dve.wait_ge(rstd_ret, turn + 1)
                        for t in range(NT):
                            v = chain(nc.vector.tensor_scalar(nsa_sum[:, t, :], nsa_sum[:, t, :],
                                                              ret_st[:, 12 + 2 * t:13 + 2 * t],
                                                              ret_st[:, 18 + t:19 + t], ALU.subtract, ALU.mult))
                        dve.wait_ge(dve_step, v)
                        dve.wait_ge(z_done, turn * 4 + 1)
                        chain(nc.vector.tensor_tensor(proj[:, :, bass.ds(j * P + RZ, P)], nsa_sum[:, :, :],
                                                      zg[:, 2, :, :], ALU.mult))

                    def scores_in(k):
                        kind, a = ITEMS[k]
                        bank = score[k % 2]
                        dve.wait_ge(s_full, turn * 10 + (k + 1))
                        if kind == "ret":
                            dve.wait_ge(o_full, turn * 10 + ONE)
                            nc.vector.tensor_tensor(attT[:, :], bank[:, 0:384],
                                                    con[:, bass.ds(j * 384 + C_DECAY, 384)], ALU.mult
                                                    ).then_inc(s_dve, 1)
                            return
                        if kind == "cmp":
                            sc = bank[:, 0:64].rearrange("p (t a n) -> p t a n", t=NT, a=2)[:, :, :, 0:NCMP]
                            cs = cmp_s[:, :, :].rearrange("p (t a) n -> p t a n", t=NT)
                            nc.vector.tensor_tensor(cs, sc, per_tile(C_CADD), ALU.add).then_inc(s_dve, 1)
                            dve.wait_ge(s_dve, turn * 2 + 2)
                            v = chain(nc.vector.tensor_reduce(cmp_st[:, :, 0], cmp_s[:, :, :], AX.X, ALU.max))
                            dve.wait_ge(dve_step, v)
                            nc.vector.tensor_tensor(cmp_s[:, :, :], cmp_s[:, :, :],
                                                    cmp_st[:, :, 0:1].to_broadcast([P, 4, NCMP]), ALU.subtract
                                                    ).then_inc(cmp_sub, 1)
                            return
                        e = SOFT[k]
                        st = stat[:, e % 4, :]
                        n_max = chain(nc.vector.tensor_reduce(st[:, 0:1], bank[:, 0:P], AX.X, ALU.max, negate=True))
                        if kind != "swa":
                            nc.vector.tensor_reduce(st[:, 1:2], bank[:, P:384], AX.X, ALU.max, negate=True
                                                    ).then_inc(max_done, 1)
                            return
                        v = chain(nc.vector.tensor_reduce(st[:, 1:2], bank[:, P:384], AX.X, ALU.max, negate=True))
                        dve.wait_ge(dve_step, v)
                        v = chain(nc.vector.tensor_tensor(st[:, 0:2], st[:, 0:2],
                                                          nsink[:, bass.ds(l * HEADS + j * 2 + a, 1), :].squeeze(1),
                                                          ALU.min))
                        dve.wait_ge(dve_step, v)
                        nc.vector.tensor_tensor(st[:, 4:6], st[:, 0:2],
                                                sink[:, bass.ds(l * HEADS + j * 2 + a, 1), :].squeeze(1), ALU.add
                                                ).then_inc(max_done, 1)

                    def outputs_in(k):
                        kind, a = ITEMS[k]
                        o = obank[:, 0:2 * P].rearrange("p (t n) -> p t n", t=NT)
                        hcols = slice(a * HD, (a + 1) * HD)
                        if kind == "ret":
                            dve.wait_ge(o_full, turn * 10 + (k + 1 + ONE))
                            nc.vector.tensor_copy(nsa_sum[:, :, :], o).then_inc(o_free, 1)
                            dve.wait_ge(o_free, turn * 10 + (k + 1 + ONE))
                            for t in range(NT):
                                v = chain(nc.vector.bn_stats(ret_st[:, 6 * t:6 * t + 6], nsa_sum[:, t, :]))
                            dve.wait_ge(dve_step, v)
                            settle(dve)
                            for t in range(NT):
                                v = chain(nc.vector.bn_aggr(ret_st[:, 12 + 2 * t:14 + 2 * t], ret_st[:, 6 * t:6 * t + 6]))
                            dve.wait_ge(dve_step, v)
                            nc.vector.tensor_scalar(ret_st[:, 16:18],
                                                    ret_st[:, 12:16].rearrange("p (t m) -> p t m", m=2)[:, :, 1],
                                                    EPS, None, ALU.add).then_inc(var_ret, 1)
                            return
                        if kind == "cmp":
                            dve.wait_ge(dve_step, steps.base + steps.n)
                            dve.wait_ge(o_full, turn * 10 + (k + 1 + ONE))
                            nc.vector.tensor_tensor(
                                nsa_sum[:, :, :].rearrange("p t (a n) -> p (t a) n", a=2),
                                obank[:, 0:2 * P].rearrange("p (t n) -> p t n", n=HD),
                                cmp_st[:, :, 2:3].to_broadcast([P, 4, HD]), ALU.mult).then_inc(o_free, 1)
                            return
                        e = SOFT[k]
                        st = stat[:, e % 4, :]
                        dve.wait_ge(exp_done, turn * 8 + (e + 1 + ONE))
                        if kind == "swa":
                            dve.wait_ge(sink_exp, turn * 2 + (a + 1))
                            v = chain(nc.vector.tensor_tensor(st[:, 2:4], st[:, 2:4], st[:, 6:8], ALU.add))
                            dve.wait_ge(dve_step, v)
                        v = chain(nc.vector.reciprocal(st[:, 8:10], st[:, 2:4]))
                        dve.wait_ge(dve_step, v)
                        if kind in ("moba", "swa"):
                            b = 0 if kind == "moba" else 1
                            dve.wait_ge(z_done, turn * 4 + (b + 2))
                            dve.wait_ge(o_full, turn * 10 + (k + 1 + ONE))
                            for t in range(NT):
                                ins = nc.vector.scalar_tensor_tensor(
                                    proj[:, t, bass.ds(j * P + (ZCOL[b] + a * HD), HD)], o[:, t, 0:HD], st[:, 8 + t:9 + t],
                                    zg[:, b, t, hcols], ALU.mult, ALU.mult)
                            ins.then_inc(o_free, 1)
                            return
                        g = 1 if kind == "slc" else 2
                        v = chain(nc.vector.tensor_tensor(st[:, 10:12], st[:, 8:10],
                                                          nsa_g[:, :, bass.ds(j * 2 + (g * HEADS + a), 1)].squeeze(2),
                                                          ALU.mult))
                        dve.wait_ge(dve_step, v)
                        dve.wait_ge(o_full, turn * 10 + (k + 1 + ONE))
                        dve.wait_ge(o_free, turn * 10 + (k + ONE))
                        for t in range(NT):
                            ins = nc.vector.scalar_tensor_tensor(nsa_sum[:, t, hcols], o[:, t, 0:HD], st[:, 10 + t:11 + t],
                                                                 nsa_sum[:, t, hcols], ALU.mult, ALU.add)
                        ins.then_inc(o_free, 1)
                        if kind == "win":
                            dve.wait_ge(o_free, turn * 10 + (k + 1 + ONE))
                            dve.wait_ge(z_done, turn * 4 + 4)
                            ins = nc.vector.tensor_tensor(proj[:, :, bass.ds(j * P + (NZ + a * HD), HD)],
                                                          nsa_sum[:, :, hcols], zg[:, 3, :, hcols], ALU.mult)
                            if a == 1:
                                ins.then_inc(y_done, 1)
                            else:
                                chain(ins)

                    for s in range(SLOTS):
                        if 0 <= s - S_AT < 10:
                            scores_in(s - S_AT)
                        if 0 <= s - O_AT < 10:
                            outputs_in(s - O_AT)
                        if s == S_AT + 3:
                            cmp_rest()
                        if s == O_AT + 1:
                            ret_rest()
                        i = s // 4 + 1
                        for m in PIECES[s % 4]:
                            dve.wait_ge(hi_piece, turn * SLOTS + (i - 1) * 4 + m + 1)
                            cols = slice(m * CW, (m + 1) * CW)
                            ins = nc.vector.tensor_tensor(w_lo[:, i % 2, cols], raw[:, i % 2, cols],
                                                          w_hi[:, i % 2, cols].bitcast(F32), ALU.subtract)
                            if m == UNIT_K - 1:
                                ins.then_inc(lo_done, 1)
                    turn_n = steps.n
                assert (prep_n, turn_n) == (DVE_PREP, DVE_TURN), (prep_n, turn_n)
                for g in range(4):
                    xgroup_lo(4 + g, yT_hi[g][:, :, :], yT_lo[g][:, :, :], l)
                for v in range(8):
                    c, i = divmod(v, 4)
                    split_lo((v + 1) % 2, l * WHOLE + (N_BRANCH + v + 2 - 16))
                    if v < 2:
                        for g in (4 + 2 * v, 5 + 2 * v):
                            xgroup_lo(4 + g, yT_hi[g][:, :, :], yT_lo[g][:, :, :], l)
                    dve.wait_ge(w_used, l * SPLITS + (N_BRANCH + v + 1 + 2))
                    if i == 0:
                        dve.wait_ge(acc_act, l * ACC_ACT + (22 + 2))
                    for t in range(NT):
                        gate = gates[:, t, i * D + c * CW:i * D + (c + 1) * CW]
                        if i == 0:
                            ins = nc.vector.scalar_tensor_tensor(gate, gate, 1.0, acc[(v % 2) * 2 + t][:, :], ALU.add,
                                                                 ALU.mult)
                            ins.then_inc(first_part, 1)
                        else:
                            m = c * 6 + (i - 1) * 2 + t
                            dve.wait_ge(part_added, l * 12 + (max(m - 1, 0) + ONE))
                            nc.vector.scalar_tensor_tensor(part[:, t, :], gate, 1.0, acc[(v % 2) * 2 + t][:, :],
                                                           ALU.add, ALU.mult).then_inc(part_full, 1)
                    if v == 5:
                        for g in range(2):
                            xgroup_lo(12 + g, hT_hi[:, 2 * g:2 * g + 2, :], hT_lo[:, 2 * g:2 * g + 2, :], l)
                split_lo(1, l * WHOLE + (N_OUT + 2 - 16))
                for g in range(2, 4):
                    xgroup_lo(12 + g, hT_hi[:, 2 * g:2 * g + 2, :], hT_lo[:, 2 * g:2 * g + 2, :], l)
                split_lo(0, l * WHOLE + (N_OUT + 3 - 16))
                split_lo(1, l * WHOLE + (N_OUT + 4 - 16))
                for c in range(2):
                    dve.wait_ge(w_used, l * SPLITS + (N_OUT + 2 + c + 1 + 2))
                    for t in range(NT):
                        cols = slice(c * CW, (c + 1) * CW)
                        ins = nc.vector.tensor_tensor(x_sb[:, t, cols], x_sb[:, t, cols], acc[2 * c + t][:, :], ALU.add)
                    ins.then_inc(acc_dve, 1)
            mean_square(LAYERS)
            dve.wait_ge(s_g_row, 16)
            for t in range(NT):
                nc.vector.scalar_tensor_tensor(h[:, t, :], x_sb[:, t, :], small[:, 4 + t:5 + t], g_row[:, :], ALU.mult,
                                               ALU.mult).then_inc(y_final, 1)

        @block.tensor
        def _(pe):
            def steps_of(hi, lo, k, unit, uk, banks, first, last, cols=CW):
                wide = cols * UNIT_K
                wh = w_hi[:, unit, 0:wide].rearrange("p (k n) -> p k n", k=UNIT_K)[:, uk, :]
                wl = w_lo[:, unit, 0:wide].rearrange("p (k n) -> p k n", k=UNIT_K)[:, uk, :]
                for t in range(NT):
                    o = acc[banks + t][:, 0:cols]
                    a, b = hi[:, k, t * P:(t + 1) * P], lo[:, k, t * P:(t + 1) * P]
                    nc.tensor.matmul(o, a, wl, start=first, stop=False)
                    nc.tensor.matmul(o, a, wh, start=False, stop=False)
                    ins = nc.tensor.matmul(o, b, wh, start=False, stop=last)
                return ins

            def unit_of(kh, unit, banks, done, cols=CW):
                pe.wait_ge(lo_done, done)
                for uk in range(UNIT_K):
                    ins = steps_of(hT_hi, hT_lo, kh * UNIT_K + uk, unit, uk, banks, kh == 0 and uk == 0,
                                   kh == 1 and uk == UNIT_K - 1, cols)
                ins.then_inc(w_used, 1)

            def transposes(g, src):
                for k in range(2):
                    for t in range(NT):
                        ins = nc.tensor.transpose(xbank[g % 4][:, k * SEQ + t * P:k * SEQ + (t + 1) * P],
                                                  src(t, k), ident)
                ins.then_inc(x_full, 1)

            pe.sem_inc(w_used, 2)
            for first in (tq_done, t_full, o_full):
                pe.sem_inc(first, ONE)
            pe.wait_ge(s_id, 16)
            pe.wait_ge(s_g, 16)
            nc.tensor.transpose(score[0][:, 0:LAYERS * KD], g_in[:, :], ident[0:LAYERS * KD, 0:LAYERS * KD]).then_inc(g_T, 1)
            pe.wait_ge(g_ready, 1)
            pe.wait_ge(s_x[0], 16)
            pe.wait_ge(s_x[1], 16)
            with pe.Fori(0, LAYERS) as l:
                pe.wait_ge(x_lo, l * 16 + ONE)
                for g in range(4):
                    pe.wait_ge(acc_dve, l * ACC_DVE + (1 + g // 2))
                    transposes(g, lambda t, k: x_sb[:, t, (2 * g + k) * P:(2 * g + k + 1) * P])

                def wait_banks(q):
                    pe.wait_ge(acc_act, l * ACC_ACT + (q + 1))
                    pe.wait_ge(acc_dve, l * ACC_DVE + (q + 1))

                wait_banks(0)
                for n in range(2):
                    for uk in range(UNIT_K):
                        if uk < UNIT_K - 1:
                            pe.wait_ge(lo_first, l * 6 + (n * 3 + uk + 1))
                        else:
                            pe.wait_ge(lo_done, l * SPLITS + (n + 1 + 2))
                        if uk % 2 == 0:
                            pe.wait_ge(x_lo, l * 16 + (2 * n + uk // 2 + 1 + ONE))
                        ins = steps_of(hT_hi, hT_lo, n * UNIT_K + uk, n, uk, 0, n == 0 and uk == 0,
                                       n == 1 and uk == UNIT_K - 1)
                    ins.then_inc(w_used, 1)
                settle(pe)
                with pe.Fori(0, LOOPED // 2) as c:
                    for i in range(2):
                        pe.wait_ge(acc_act, l * ACC_ACT + c * 2 + (i + 2))
                        pe.wait_ge(acc_dve, l * ACC_DVE + c * 2 + (i + 2))
                        for kh in range(2):
                            unit_of(kh, kh, 2 - 2 * i, l * SPLITS + c * 4 + (2 * i + kh + 2 + 1 + 2))

                def late(n):
                    if n % 2 == 0:
                        wait_banks(n // 2)
                    unit_of(n % 2, n % 2, 2 * (n // 2 % 2), l * SPLITS + (n + 1 + 2))

                def hidden(i):
                    u = C_UNIT[i]
                    pe.wait_ge(raw_full[u % 2], (l * (UNITS // 2) + u // 2) * 16 + 16)
                    for k in range(8):
                        ins = nc.tensor.matmul(score[0][0:2 * NCMP, i // 2 * 256:i // 2 * 256 + 256],
                                               blocksT[:, i // 2, (i % 2) * 8 + k, :], slot8(raw, u)[:, k, :],
                                               start=(i % 2 == 0 and k == 0), stop=(i % 2 == 1 and k == 7))
                    ins.then_inc(cmp_used, 1)

                late(18)
                late(19)
                late(20)
                pe.wait_ge(dup_done, l + 1)
                for t, bank in enumerate((obank, tbank)):
                    for s in range(4):
                        ins = nc.tensor.transpose(bank[:, s * P:(s + 1) * P],
                                                  dup[:, t, s, :, :].rearrange("p a n -> p (a n)"), ident)
                    ins.then_inc(dup_T, 1)
                pe.wait_ge(s_pos, l * 16 + 16)
                settle(pe)
                nc.tensor.transpose(score[1][:, 0:16], pos_in[:, :], ident[0:16, 0:16]).then_inc(dup_T, 1)
                late(21)
                pe.wait_ge(acc_act, l * ACC_ACT + (2 + 10))
                pe.wait_ge(acc_dve, l * ACC_DVE + (2 + 10))
                pe.wait_ge(tail_lo, l + 1)
                for k in range(KD):
                    weights = t_hl[:, k * 2 * TAIL:k * 2 * TAIL + P]
                    nc.tensor.matmul(acc[2][:, 0:SEQ], weights, hT_hi[:, k, :], start=(k == 0), stop=False)
                    ins = nc.tensor.matmul(acc[2][:, 0:SEQ], weights, hT_lo[:, k, :], start=False, stop=(k == KD - 1))
                ins.then_inc(tail_done, 1)
                pe.wait_ge(blocks_done, l + 1)
                hidden(0)
                pe.wait_ge(acc_act, l * ACC_ACT + (2 + 12))
                late(22)
                hidden(1)
                late(23)
                hidden(2)
                pe.wait_ge(keys_roped, l * 3 + 3)
                settle(pe)
                for i in range(3):
                    for kv in range(2):
                        for t in range(NT):
                            ins = nc.tensor.transpose(xbank[i + 1][0:HD, kv * SEQ + t * P:kv * SEQ + (t + 1) * P],
                                                      k_shared[:, t, i, kv * HD:(kv + 1) * HD], ident)
                    ins.then_inc(keys_T, 1)
                late(24)
                hidden(3)
                late(25)
                pe.wait_ge(keys_out, l * 3 + 3)
                pe.wait_ge(gelu_done, l + 1)
                settle(pe)
                for f in range(4):
                    ins = nc.tensor.transpose(obank[:, f * P:f * P + 2 * NCMP], hid2[:, f * P:(f + 1) * P],
                                              ident[0:2 * NCMP, 0:2 * NCMP])
                ins.then_inc(gelu_T, 1)
                pe.wait_ge(gelu_out, l + 1)
                pe.wait_ge(s_c2, l * 32 + 32)
                for f in range(2):
                    nc.tensor.matmul(score[0][0:2 * NCMP, 0:HD], gkT[:, f, :], w_c2[:, 0, f, :], start=(f == 0),
                                     stop=(f == 1))
                for kv in range(2):
                    for f in range(2):
                        ins = nc.tensor.matmul(score[1][0:2 * NCMP, kv * HD:(kv + 1) * HD],
                                               gvT[:, f, kv, :, :].rearrange("p a n -> p (a n)"), w_c2[:, 1, f, :],
                                               start=(f == 0), stop=(f == 1))
                ins.then_inc(cmp_kv, 1)
                pe.wait_ge(acc_act, l * ACC_ACT + (2 + 13))
                pe.wait_ge(acc_dve, l * ACC_DVE + (2 + 12))
                settle(pe)
                for t in range(NT):
                    ins = nc.tensor.transpose(acc[3][:, t * 2 * TAIL:(t + 1) * 2 * TAIL], t_sum[:, t * P:(t + 1) * P],
                                              ident[0:2 * TAIL, 0:2 * TAIL])
                ins.then_inc(tail_T, 1)
                pe.wait_ge(cmp_roped, l + 1)
                settle(pe)
                nc.tensor.transpose(score[1][0:HD, 0:2 * NCMP], kc_r[:, :], ident[0:2 * NCMP, 0:2 * NCMP]).then_inc(kcT_full, 1)
                pe.wait_ge(acc_act, l * ACC_ACT + (2 + 14))
                pe.wait_ge(setup_done, 1)
                settle(pe)
                with pe.Fori(0, 4) as j:
                    turn = l * 4 + j

                    def heads_T(f):
                        pe.wait_ge(t_free, turn * T_FILLS + (f + ONE))
                        settle(pe)
                        for a in range(2):
                            for t in range(NT):
                                ins = nc.tensor.transpose(tbank[0:HD, a * SEQ + t * P:a * SEQ + (t + 1) * P],
                                                          roped[:, f, t, a * HD:(a + 1) * HD], ident)
                        ins.then_inc(t_full, 1)

                    def scores_of(k):
                        kind, a = ITEMS[k]
                        bank = score[k % 2]
                        if k < 2:
                            pe.wait_ge(exp_done, turn * 8 + ONE)
                            if k == 1:
                                pe.wait_ge(cmp_ready, l + 1)
                        elif k - 2 in SOFT:
                            pe.wait_ge(exp_done, turn * 8 + (SOFT[k - 2] + 1 + ONE))
                        else:
                            pe.wait_ge(s_dve, turn * 2 + (1 if k == 2 else 2))
                        if kind == "ret":
                            pe.wait_ge(t_free, turn * T_FILLS + (1 + ONE))
                            nc.tensor.matmul(bank[:, 0:SEQ], qkT[:, 0, 1, 0:P], qkT[:, 0, 0, :], start=True, stop=True)
                            nc.tensor.matmul(bank[:, SEQ:384], qkT[:, 0, 1, P:SEQ], qkT[:, 0, 0, P:SEQ], start=True,
                                             stop=True).then_inc(s_full, 1)
                            return
                        if kind == "cmp":
                            pe.wait_ge(t_free, turn * T_FILLS + (5 + ONE))
                            for t in range(NT):
                                for b in range(2):
                                    o = (t * 2 + b) * 16
                                    ins = nc.tensor.matmul(bank[:, o:o + NCMP], qkT[:, 4, b, t * P:(t + 1) * P],
                                                           kcT[:, bass.ds(j // 2, 1), :].squeeze(1), start=True, stop=True)
                            ins.then_inc(s_full, 1)
                            return
                        pe.wait_ge(t_free, turn * T_FILLS + ((3 if kind == "moba" else KIND[kind] + 1) + ONE))
                        ins = nc.tensor.matmul(bank[:, 0:384], ident_b[:, :], mask_b[:, int(kind == "swa"), :],
                                               start=True, stop=False)
                        if k == 1:
                            ins.then_inc(tq_done, 1)
                        for t, (c0, c1, n) in enumerate(((0, P, P), (P, 384, SEQ))):
                            keys = qkT[:, 2, a, 0:n] if kind == "moba" else \
                                kT_shared[:, KEYS[kind], bass.ds(j // 2, 1), 0:n].squeeze(1)
                            ins = nc.tensor.matmul(bank[:, c0:c1], qkT[:, KIND[kind], a, t * P:(t + 1) * P], keys,
                                                   start=False, stop=(t == 1))
                        ins.then_inc(s_full, 1)

                    def probs_T(k):
                        pe.wait_ge(t_free, turn * T_FILLS + (4 + k + ONE))
                        if k in SOFT:
                            e = SOFT[k]
                            pe.wait_ge(exp_done, turn * 8 + (e + 1 + ONE))
                            for i in range(3):
                                ins = nc.tensor.transpose(tbank[:, i * P:(i + 1) * P], probs[:, e % 2, i * P:(i + 1) * P],
                                                          ident)
                            ins.then_inc(t_full, 1)
                            return
                        pe.wait_ge(cmp_p, turn + 1)
                        for t in range(NT):
                            ins = nc.tensor.transpose(tbank[0:2 * NCMP, t * P:(t + 1) * P],
                                                      cmp_s[:, 2 * t:2 * t + 2, :].rearrange("p a n -> p (a n)"), ident)
                        ins.then_inc(t_full, 1)

                    def outputs_of(k):
                        kind, a = ITEMS[k]
                        pe.wait_ge(o_free, turn * 10 + (k + ONE))
                        if kind == "cmp":
                            pe.wait_ge(t_free, turn * T_FILLS + (5 + k + ONE))
                            for t in range(NT):
                                ins = nc.tensor.matmul(obank[:, t * P:(t + 1) * P], cmp_pT[:, t * P:(t + 1) * P],
                                                       v_blk[:, bass.ds(j // 2, 1), :].squeeze(1), start=True, stop=True)
                            ins.then_inc(o_full, 1)
                            return
                        if kind == "ret":
                            pe.wait_ge(s_dve, turn * 2 + 1)
                            left, n = attT[:, :], P
                            vcol = bass.ds(j * P + RV, P)
                        else:
                            pe.wait_ge(t_free, turn * T_FILLS + (5 + k + ONE))
                            left, n = probsT[:, SOFT[k] % 2, :], HD
                            vcol = bass.ds(j * P + (MV + a * HD), HD) if kind == "moba" else \
                                bass.ds(j // 2 * HD + VCOL[kind], HD)
                        nc.tensor.matmul(obank[:, 0:n], left[:, 0:P], proj[:, 0, vcol], start=True, stop=True)
                        nc.tensor.matmul(obank[:, P:P + n], left[:, P:2 * P], proj[:, 0, vcol], start=True, stop=False)
                        nc.tensor.matmul(obank[:, P:P + n], left[:, 2 * P:3 * P], proj[:, 1, vcol], start=False,
                                         stop=True).then_inc(o_full, 1)

                    for s in range(SLOTS):
                        i, uk = divmod(s, UNIT_K)
                        if s % 8 == 0:
                            pe.wait_ge(acc_act, l * ACC_ACT + j * 2 + (14 + s // 8 + 1))
                            pe.wait_ge(acc_dve, l * ACC_DVE + (2 + 13 + s // 8))
                        if uk == 0:
                            pe.wait_ge(lo_done, l * SPLITS + j * 4 + (N_MERGE + i + 1 + 2))
                        ins = steps_of(hT_hi, hT_lo, s % 8, i % 2, uk, 2 * (s // 8), s % 8 == 0, s % 8 == 7)
                        if uk == UNIT_K - 1:
                            ins.then_inc(w_used, 1)
                        if s == 0:
                            pe.wait_ge(q_roped, turn * 5 + 5)
                        if s < 5:
                            heads_T(s)
                        if 0 <= s - S_AT < 10:
                            scores_of(s - S_AT)
                        if 1 <= s - P_AT < 10:
                            probs_T(s - P_AT)
                        if 0 <= s - O_AT < 10:
                            outputs_of(s - O_AT)
                def outputs_T(g):
                    b, pair = divmod(g, 2)
                    if g >= 4:
                        pe.wait_ge(x_lo, l * 16 + (g + 1 + ONE))
                    transposes(4 + g, lambda t, k: proj[:, t, ZCOL[b] + (2 * pair + k) * P:ZCOL[b] + (2 * pair + k + 1) * P])

                def merged_T(g):
                    pe.wait_ge(x_lo, l * 16 + (12 + ONE))
                    transposes(12 + g, lambda t, k: merged[:, t, (2 * g + k) * P:(2 * g + k + 1) * P])

                pe.wait_ge(y_done, l * 4 + (4 + ONE))
                pe.wait_ge(t_free, l * 4 * T_FILLS + (4 * T_FILLS + ONE))
                for g in range(4):
                    outputs_T(g)
                for v in range(8):
                    c, i = divmod(v, 4)
                    pe.wait_ge(x_lo, l * 16 + (4 + min(2 * v + 2, 8) + ONE))
                    if v < 2:
                        pe.wait_ge(acc_act, l * ACC_ACT + (23 + v))
                    elif (v - 2) % 4 == 0:
                        pe.wait_ge(first_part, l * 4 + ((v - 2) // 4 * 2 + 2))
                    else:
                        pe.wait_ge(part_full, l * 12 + ((v - 2) // 4 * 6 + (v - 2) % 4 * 2))
                    pe.wait_ge(lo_done, l * SPLITS + (N_BRANCH + v + 1 + 2))
                    for uk in range(UNIT_K):
                        g = 2 * i + uk // 2
                        ins = steps_of(yT_hi[g], yT_lo[g], uk % 2, v % 2, uk, (v % 2) * 2, uk == 0, uk == UNIT_K - 1)
                    ins.then_inc(w_used, 1)
                    if v < 2:
                        outputs_T(4 + 2 * v)
                        outputs_T(5 + 2 * v)
                    if v == 4:
                        pe.wait_ge(part_added, l * 12 + (6 + ONE))
                        merged_T(0)
                        merged_T(1)
                for v in range(4):
                    kh, c = divmod(v, 2)
                    pe.wait_ge(x_lo, l * 16 + ((14 if kh == 0 else 16) + ONE))
                    pe.wait_ge(lo_done, l * SPLITS + (N_OUT + v + 1 + 2))
                    for uk in range(UNIT_K):
                        k = kh * UNIT_K + uk
                        ins = steps_of(hT_hi, hT_lo, k, v % 2, uk, 2 * c, k == 0, k == KD - 1)
                    ins.then_inc(w_used, 1)
                    if v == 0:
                        pe.wait_ge(part_added, l * 12 + (12 + ONE))
                        merged_T(2)
                        merged_T(3)


_INS = ["x", "norm_g", "w_in", "w_branch", "w_out", "swa_sink", "nsa_cmp_pos", "nsa_w_ck1", "nsa_w_ck2",
        "nsa_w_cv1", "nsa_w_cv2", "final_norm_g"]


def constant_arrays():
    import numpy as np
    f = np.float32
    inv = (f(1.0) / f(10000.0) ** (np.arange(0, HD, 2, dtype=f) / f(HD))).astype(f)
    ang = np.arange(SEQ, dtype=f)[:, None] * inv[None, :]
    cos, sin = np.cos(ang).astype(f), np.sin(ang).astype(f)
    cos2, sin2 = np.concatenate([cos, cos], 1), np.concatenate([-sin, sin], 1)
    c = np.zeros((P, N_CONST), f)
    c[:, C_ID:C_ID + P] = np.eye(P, dtype=f)
    for t in range(NT):
        for a in range(2):
            o = t * P + a * HD
            c[:, C_COS + o:C_COS + o + HD] = cos2[t * P:(t + 1) * P]
            c[:, C_SIN + o:C_SIN + o + HD] = sin2[t * P:(t + 1) * P]
    row = np.arange(P)
    for h in range(4):
        log_g = np.log(f(1.0) - f(2.0) ** f(-5.0 - h)).astype(f)
        for i, (k0, q0, n) in enumerate(((0, 0, 2 * P), (P, P, P))):
            diff = (q0 + np.arange(n))[None, :] - (k0 + row)[:, None]
            o = C_DECAY + h * 384 + i * 2 * P
            c[:, o:o + n] = np.where(diff >= 0, np.exp(np.maximum(diff, 0).astype(f) * log_g), 0.0)
    end = np.arange(NCMP) * 16 + 31
    for t in range(NT):
        ok = end[None, :] <= (t * P + row)[:, None]
        c[:, C_CADD + t * NCMP:C_CADD + (t + 1) * NCMP] = np.where(ok, 0.0, -1e30)
        c[:, C_C01 + t * NCMP:C_C01 + (t + 1) * NCMP] = ok
    for a in range(2):
        c[a * NCMP:(a + 1) * NCMP, C_BLK + a] = 0.5
        c[a * NCMP:(a + 1) * NCMP, C_COSK:C_COSK + HD] = cos2[end]
        c[a * NCMP:(a + 1) * NCMP, C_SINK:C_SINK + HD] = sin2[end]
    m = np.zeros((P, 2, 384), f)
    for i, (q0, k0) in enumerate(((0, 0), (P, 0), (P, P))):
        dist = (q0 + row)[:, None] - (k0 + row)[None, :]
        m[:, 0, i * P:(i + 1) * P] = np.where(dist >= 0, 0.0, -1e30)
        m[:, 1, i * P:(i + 1) * P] = np.where((dist >= 0) & (dist < 128), 0.0, -1e30)
    return c, m.reshape(P, 768)


def kernel(**inputs):
    import numpy as np
    import concourse.bacc as bacc
    from concourse.bass_utils import run_bass_kernel_spmd

    nc = bacc.Bacc("TRN2", target_bir_lowering=False, num_devices=1)
    consts, masks = constant_arrays()
    arrays, args = {}, []
    for name, a in [(n, np.ascontiguousarray(inputs[n])) for n in _INS] + [("consts", consts), ("masks", masks)]:
        arrays[f"in_{name}_dram"] = a
        args.append(nc.dram_tensor(f"in_{name}_dram", a.shape, mybir.dt.from_np(a.dtype), kind="ExternalInput").ap())
    args.append(nc.dram_tensor("out_dram", (1, SEQ, D), F32, kind="ExternalOutput").ap())
    hybrid_trunk(nc, *args)
    r = run_bass_kernel_spmd(nc, [arrays], core_ids=[0])
    return r.results[0]["out_dram"]
```

```python
from contextlib import ExitStack

import concourse.bass as bass
from concourse import mybir

F32 = mybir.dt.float32
F32R = mybir.dt.float32r
BF16 = mybir.dt.bfloat16
ALU = mybir.AluOpType
ACT = mybir.ActivationFunctionType
AX = mybir.AxisListType

P = 128
D = 1024
KD = D // P
SEQ = 256
NT = SEQ // P
LAYERS = 2
HD = 64
HEADS = 8
W = HEADS * HD
CW = 512
UNIT_K = 4
UNIT = UNIT_K * CW
NCMP = 15
EPS = 1e-6
TINY = 1e-30

MQ, MK, MV, MZ = 0, 512, 1024, 1536
SQ, SK, SV, SZ = 2048, 2560, 2688, 2816
RQ, RK, RV, RZ = 3328, 3584, 3840, 4352
NQ, KC, VC, KS, VS, KW, VW = 4864, 5376, 5504, 5632, 5760, 5888, 6016
NG, NZ, MG = 6144, 6168, 6680
D_IN = MG + 4 * D
ZCOL = (MZ, SZ, RZ, NZ)
CHUNKS = MG // CW
TAIL = MG - CHUNKS * CW

FIRST, LOOPED = 10, 8
LATE = ((9, 8), (10, 11), (11, 9), (12, 12))

LATE_UNITS = ((8, 0), (8, 1), (11, 0), (None, 0), (11, 1), (None, 1),
              (9, 0), (None, 2), (9, 1), (None, 3), (12, 0), (12, 1))
N_LATE = 2 * (1 + LOOPED)
N_MERGE = N_LATE + len(LATE_UNITS)
MIX_UNITS = 16
N_BRANCH = N_MERGE + MIX_UNITS
N_OUT = N_BRANCH + 8
UNITS = N_OUT + 4
WHOLE = UNITS - MIX_UNITS
QUARTERED = (0, 1, 2, 3) + tuple(range(N_LATE + 2, N_MERGE + 1))


def late_unit(chunk, part):
    return N_LATE + LATE_UNITS.index((chunk, part))


C_ID, C_COS, C_SIN, C_DECAY = 0, 128, 384, 640
C_CADD, C_C01, C_BLK, C_COSK, C_SINK = 2176, 2206, 2236, 2238, 2302
N_CONST = 2366


ONE = 1


class Count:

    def __init__(self):
        self.base, self.n = 0, 0

    def at(self, base):
        self.base, self.n = base, 0

    def next(self):
        self.n += 1
        return self.base + self.n


ACC_ACT, ACC_DVE = 22, 16
DVE_PREP, DVE_TURN = 22, 39
POOL_PREP, POOL_TURN = 9, 21


def hybrid_trunk(nc, x, norm_g, w_in, w_branch, w_out, swa_sink, cmp_pos, w_ck1, w_ck2, w_cv1, w_cv2,
                 final_norm_g, consts, masks, out):
    with ExitStack() as ctx:
        top = [(nc.sbuf_base + 31) // 32 * 32]

        def at(name, shape, dt, offset):
            return nc.alloc_sbuf_tensor_at(name, shape, dt, offset=offset)

        def sb(name, shape, dt=F32):
            size = 2 if dt == BF16 else 4
            for n in shape[1:]:
                size *= n
            t = at(name, shape, dt, top[0])
            top[0] += (size + 31) // 32 * 32
            return t

        def sem(name):
            return ctx.enter_context(nc.semaphore(name))

        x_sb = sb("x_sb", [P, NT, D])
        hT_hi = sb("hT_hi", [P, KD, SEQ], F32R)
        hT_lo = sb("hT_lo", [P, KD, SEQ], F32R)
        raw = sb("raw", [P, 2, UNIT])
        w_hi = sb("w_hi", [P, 2, UNIT], F32R)
        w_lo = sb("w_lo", [P, 2, UNIT], F32R)
        proj_at = top[0]
        proj = sb("proj", [P, NT, MG])
        gates_at = top[0]
        gates = sb("gates", [P, NT, 4 * D])
        merged = gates[:, :, 0:D]
        con = sb("con", [P, N_CONST])
        ident = con[:, C_ID:C_ID + P]
        ident_b = sb("ident_b", [P, P], BF16)
        mask_b = sb("mask_b", [P, 2, 384], BF16)
        small = sb("small", [P, 8])
        g_col = sb("g_col", [P, LAYERS * KD])
        g_now = sb("g_now", [P, KD])
        act_warm = sb("act_warm", [P, 1])
        g_in = sb("g_in", [LAYERS * KD, P])
        neg_half = sb("neg_half", [P, NT])
        sink_in = sb("sink_in", [P, LAYERS * HEADS])
        sink = sb("sink", [P, LAYERS * HEADS, 2])
        nsink = sb("nsink", [P, LAYERS * HEADS, 2])
        nsa_g = sb("nsa_g", [P, NT, 24])
        pos_in = sb("pos_in", [16, P])
        kT_shared = sb("kT_shared", [HD, 3, 2, SEQ])
        kcT = sb("kcT", [HD, 2, NCMP])
        v_blk = sb("v_blk", [2 * NCMP, 2, P])
        tmp_rope = sb("tmp_rope", [P, NT, P])

        roped = sb("roped", [P, 5, NT, P])
        qkT_at = top[0]
        qkT = sb("qkT", [HD, 5, 2, SEQ])
        probs = sb("probs", [P, 2, 384])
        probsT = sb("probsT", [P, 2, 384])
        attT = sb("attT", [P, 384])
        zg = sb("zg", [P, 4, NT, P])
        nsa_sum = sb("nsa_sum", [P, NT, P])
        stat = sb("stat", [P, 4, 12])
        cmp_s = sb("cmp_s", [P, 4, NCMP])
        cmp_st = sb("cmp_st", [P, 4, 4])
        cmp_pT = sb("cmp_pT", [2 * NCMP, SEQ])
        ret_st = sb("ret_st", [P, 20])
        assert top[0] <= nc.sbuf_usable_end, (top[0], nc.sbuf_usable_end)

        g0 = gates_at + 1024 * 4
        g1 = gates_at + 5120 * 4
        h = at("h", [P, NT, D], F32, g0)
        k_shared = at("k_shared", [P, NT, 3, P], F32, g1 + 9216)
        g_row = at("g_row", [P, D], F32, g1)
        mask_f = at("mask_f", [P, 2 * 384], F32, g1 + 4096)
        dup = at("dup", [P, NT, 4, 2, HD], F32, g0)
        pairT = at("pairT", [P, 4, P], F32, g0 + 8448)
        b_parts = at("b_parts", [P, 33 * 64], F32R, g0)
        blocksT = at("blocksT", [P, 32, 2 * NCMP], F32, g1)
        hid = at("hid", [2 * NCMP, 2 * 256], F32, g1)
        hid2 = at("hid2", [2 * NCMP, 2 * 256], F32, g1 + 2048)
        hid3 = at("hid3", [2 * NCMP, 2 * 256], F32, g1 + 4096)
        gkT = at("gkT", [P, 2, 2 * NCMP], F32, g1 + 6144)
        gvT = at("gvT", [P, 2, 2, 2, NCMP], F32, g1 + 6144 + 256)
        posT = at("posT", [P, 16], F32, g1 + 7168)
        kc_s = at("kc_s", [2 * NCMP, HD], F32, g1 + 7168 + 64)
        kc_t = at("kc_t", [2 * NCMP, HD], F32, g1 + 7168 + 320)
        kc_r = at("kc_r", [2 * NCMP, HD], F32, g1 + 7168 + 576)
        w_c2 = at("w_c2", [P, 2, 2, HD], F32, g1 + 8192)
        spots = [proj_at + 4 * (t * MG + c) for t in range(NT) for c in (0, 512, 1024, 2048, 3328, 3840, 4864, 5376)]
        yT_hi = [at(f"yT_hi{g}", [P, 2, SEQ], F32R, spots[g]) for g in range(8)]
        yT_lo = [at(f"yT_lo{g}", [P, 2, SEQ], F32R, spots[8 + g]) for g in range(8)]
        part = at("part", [P, NT, CW], F32, qkT_at)
        t_raw = at("t_raw", [P, KD, TAIL], F32, qkT_at)
        t_hl = at("t_hl", [P, KD * 2 * TAIL + P - 2 * TAIL], F32R, qkT_at + 768)
        t_parts = t_hl[:, 0:KD * 2 * TAIL].rearrange("p (k s n) -> p k s n", k=KD, s=2)
        t_sum = at("t_sum", [2 * TAIL, SEQ], F32, qkT_at + 2688)
        t_cols = at("t_cols", [P, NT, TAIL], F32, qkT_at + 3712)

        acc = [ctx.enter_context(nc.psum_tensor(f"acc{i}", [P, CW], F32)) for i in range(4)]
        score = [ctx.enter_context(nc.psum_tensor(f"score{i}", [P, CW], F32)) for i in range(2)]
        tbank = ctx.enter_context(nc.psum_tensor("tbank", [P, CW], F32))
        obank = ctx.enter_context(nc.psum_tensor("obank", [P, CW], F32))
        xbank = [score[0], score[1], tbank, obank]

        s_x = [sem("s_x0"), sem("s_x1")]
        s_con = sem("s_con")
        s_mask = sem("s_mask")
        s_id = sem("s_id")
        s_g = sem("s_g")
        s_g_row = sem("s_g_row")
        s_tail = sem("s_tail")
        s_pos = sem("s_pos")
        s_c2 = sem("s_c2")
        s_out = sem("s_out")
        raw_full = [sem("raw_full0"), sem("raw_full1")]
        hi_done = sem("hi_done")
        hi_piece = sem("hi_piece")
        lo_done = sem("lo_done")
        w_used = sem("w_used")
        acc_act = sem("acc_act")
        acc_dve = sem("acc_dve")
        sq_done = sem("sq_done")
        g_T = sem("g_T")
        g_ready = sem("g_ready")
        half_rstd = sem("half_rstd")
        hi_quarter = sem("hi_quarter")
        lo_quarter = sem("lo_quarter")
        tail_hi = sem("tail_hi")
        tail_lo = sem("tail_lo")
        tail_done = sem("tail_done")
        tail_T = sem("tail_T")
        x_full = sem("x_full")
        x_hi = sem("x_hi")
        x_lo = sem("x_lo")
        setup_done = sem("setup_done")
        dve_step = sem("dve_step")
        pool_step = sem("pool_step")
        rstd_norm = sem("rstd_norm")
        var_norm = sem("var_norm")
        keys_roped = sem("keys_roped")
        keys_T = sem("keys_T")
        keys_out = sem("keys_out")
        dup_done = sem("dup_done")
        dup_T = sem("dup_T")
        blocks_done = sem("blocks_done")
        hid_sb = sem("hid_sb")
        hid_tanh = sem("hid_tanh")
        gelu_done = sem("gelu_done")
        gelu_T = sem("gelu_T")
        gelu_out = sem("gelu_out")
        cmp_kv = sem("cmp_kv")
        cmp_roped = sem("cmp_roped")
        kcT_full = sem("kcT_full")
        cmp_ready = sem("cmp_ready")
        tail_tanh = sem("tail_tanh")
        gates_nsa = sem("gates_nsa")
        q_roped = sem("q_roped")
        tq_done = sem("tq_done")
        t_full = sem("t_full")
        t_free = sem("t_free")
        s_full = sem("s_full")
        max_done = sem("max_done")
        exp_done = sem("exp_done")
        sink_exp = sem("sink_exp")
        s_dve = sem("s_dve")
        cmp_sub = sem("cmp_sub")
        cmp_exp = sem("cmp_exp")
        cmp_p = sem("cmp_p")
        o_full = sem("o_full")
        o_free = sem("o_free")
        z_tanh = sem("z_tanh")
        z_done = sem("z_done")
        y_done = sem("y_done")
        var_ret = sem("var_ret")
        rstd_ret = sem("rstd_ret")
        part_full = sem("part_full")
        part_added = sem("part_added")
        first_part = sem("first_part")
        y_final = sem("y_final")

        w_in_v = w_in.rearrange("l (h k p) n -> l h p k n", k=UNIT_K, p=P)
        w_br_v = w_branch.rearrange("l (i k p) n -> l i p k n", k=UNIT_K, p=P)
        w_out_v = w_out.rearrange("l (h k p) n -> l h p k n", k=UNIT_K, p=P)
        w_k1_v = w_ck1.rearrange("l (h k p) n -> l h p k n", k=8, p=P)
        w_v1_v = w_cv1.rearrange("l (h k p) n -> l h p k n", k=8, p=P)

        def slot4(buf, u):
            return buf[:, u % 2, :].rearrange("p (k n) -> p k n", k=UNIT_K)

        def slot8(buf, u):
            return buf[:, u % 2, :].rearrange("p (k n) -> p k n", k=8)

        def quarters(l, n, m):
            return l * (3 * len(QUARTERED)) + (3 * QUARTERED.index(n) + m + 1)

        ITEMS = [("ret", 0), ("moba", 0), ("swa", 0), ("cmp", 0), ("slc", 0), ("win", 0),
                 ("moba", 1), ("swa", 1), ("slc", 1), ("win", 1)]
        SOFT = {k: e for e, k in enumerate([1, 2, 4, 5, 6, 7, 8, 9])}
        SOFT_K = list(SOFT)
        S_AT, P_AT, O_AT, SLOTS = 3, 5, 6, 16
        PIECES = ((0, 1), (2, 3), (), ())
        KIND = {"moba": 1, "swa": 3, "slc": 4, "win": 4}
        VCOL = {"moba": MV, "swa": SV, "slc": VS, "win": VW}
        KEYS = {"swa": 0, "slc": 1, "win": 2}
        T_FILLS = 5 + 9

        def settle(eng):
            eng.nop(nofuse=True)

        block = ctx.enter_context(nc.Block())

        @block.sync
        def _(sp):
            sp.dma_start(ident, consts[:, C_ID:C_ID + P]).then_inc(s_id, 16)
            sp.dma_start(g_in[:, :], norm_g.rearrange("l (k p) -> (l k) p", p=P)).then_inc(s_g, 16)
            for half in range(2):
                cols = slice(half * CW, (half + 1) * CW)
                sp.dma_start(x_sb[:, :, cols], x[0].rearrange("(t p) d -> p t d", p=P)[:, :, cols]).then_inc(s_x[half], 16)

            def load(src, dst, u):
                sp.dma_start(dst, src).then_inc(raw_full[u % 2], 16)

            with sp.Fori(0, LAYERS) as l:
                for i in range(2):
                    sp.wait_ge(lo_done, l * UNITS + (i + 1))
                    load(w_in_v[l, i, :, :, FIRST * CW:(FIRST + 1) * CW], slot4(raw, i), i)
                sp.dma_start(pos_in[:, :], cmp_pos[l].rearrange("(k a) d -> k (a d)", a=2)).then_inc(s_pos, 16)
                with sp.Fori(0, LOOPED // 2) as c:
                    for i in range(4):
                        sp.wait_ge(lo_done, l * UNITS + c * 4 + (i + 3))
                        load(w_in_v[l, i % 2, :, :, bass.ds(c * 2 * CW + i // 2 * CW, CW)], slot4(raw, i), i)
                sp.wait_ge(x_lo, l * 16 + (4 + ONE))
                sp.dma_start(t_raw[:, :, :], w_in[l].rearrange("(k p) n -> p k n", p=P)[:, :, CHUNKS * CW:MG]
                             ).then_inc(s_tail, 16)
                for i, w2 in enumerate((w_ck2, w_cv2)):
                    sp.dma_start(w_c2[:, i, :, :], w2[l].rearrange("(k p) n -> p k n", p=P)).then_inc(s_c2, 16)
                for u, (chunk, half) in enumerate(LATE_UNITS, N_LATE):
                    sp.wait_ge(lo_done, l * UNITS + (u + 1))
                    if chunk is None:
                        load((w_k1_v, w_v1_v)[half // 2][l, half % 2], slot8(raw, u), u)
                    else:
                        load(w_in_v[l, half, :, :, chunk * CW:(chunk + 1) * CW], slot4(raw, u), u)
                settle(sp)
                with sp.Fori(0, 4) as j:
                    for i in range(4):
                        sp.wait_ge(lo_done, l * UNITS + j * 4 + (N_MERGE + i + 1))
                        load(w_in_v[l, i % 2, :, :, bass.ds(j * 2 * CW + (MG + i // 2 * CW), CW)], slot4(raw, i), i)
                for v in range(8):
                    sp.wait_ge(lo_done, l * UNITS + (N_BRANCH + v + 1))
                    c, i = divmod(v, 4)
                    load(w_br_v[l, i, :, :, c * CW:(c + 1) * CW], slot4(raw, v), v)
                for v in range(4):
                    sp.wait_ge(lo_done, l * UNITS + (N_OUT + v + 1))
                    kh, c = divmod(v, 2)
                    load(w_out_v[l, kh, :, :, c * CW:(c + 1) * CW], slot4(raw, v), v)
            sp.wait_ge(x_lo, LAYERS * 16 + ONE)
            sp.dma_start(g_row[:, :], final_norm_g.partition_broadcast(P)).then_inc(s_g_row, 16)
            for t in range(NT):
                sp.wait_ge(y_final, t + 1)
                sp.dma_start(out[0, t * P:(t + 1) * P, :], h[:, t, :]).then_inc(s_out, 16)
            sp.wait_ge(s_out, NT * 16)

        @block.gpsimd
        def _(pool):
            steps = Count()

            def rotate(dst, src):
                cos = con[:, C_COS:C_COS + 2 * P].rearrange("p (t n) -> p t n", t=NT)
                sin = con[:, C_SIN:C_SIN + 2 * P].rearrange("p (t a f n) -> p t a f n", t=NT, a=2, f=2)
                s = src.rearrange("p t (a f n) -> p t a f n", a=2, f=2)
                m = tmp_rope[:, :, :].rearrange("p t (a f n) -> p t a f n", a=2, f=2)
                nc.gpsimd.tensor_tensor(m[:, :, :, 0], s[:, :, :, 1], sin[:, :, :, 0], ALU.mult).then_inc(pool_step, 1)
                steps.next()
                nc.gpsimd.tensor_tensor(m[:, :, :, 1], s[:, :, :, 0], sin[:, :, :, 1], ALU.mult).then_inc(pool_step, 1)
                pool.wait_ge(pool_step, steps.next())
                settle(pool)
                nc.gpsimd.tensor_tensor(dst, src, cos, ALU.mult).then_inc(pool_step, 1)
                pool.wait_ge(pool_step, steps.next())
                return nc.gpsimd.tensor_tensor(dst, dst, tmp_rope[:, :, :], ALU.add)

            def norm_rstd(i):
                pool.wait_ge(var_norm, i + 1)
                nc.gpsimd.tensor_tensor(small[:, 4:6], small[:, 2:4], neg_half[:, :], ALU.pow).then_inc(rstd_norm, 1)

            pool.sem_inc(part_added, ONE)
            pool.wait_ge(raw_full[0], 16)
            pool.dma_start(mask_f[:, :], masks).then_inc(s_mask, 16)
            pool.dma_start(sink_in[:, :], swa_sink.rearrange("l h -> (l h)").partition_broadcast(P)).then_inc(s_mask, 16)
            nc.gpsimd.memset(neg_half[:, :], -0.5).then_inc(pool_step, 1)
            pool.wait_ge(s_id, 16)
            nc.gpsimd.tensor_copy(ident_b[:, :], ident)
            pool.wait_ge(s_mask, 32)
            nc.gpsimd.tensor_copy(mask_b[:, :, :], mask_f[:, :].rearrange("p (m n) -> p m n", m=2))
            for i in range(2):
                nc.gpsimd.tensor_copy(sink[:, :, i], sink_in[:, :])
                ins = nc.gpsimd.tensor_scalar(nsink[:, :, i], sink_in[:, :], -1.0, None, ALU.mult)
            ins.then_inc(setup_done, 1)
            pool.dma_start(con[:, P:N_CONST], consts[:, P:N_CONST]).then_inc(s_con, 16)
            pool.wait_ge(setup_done, 1)
            pool.wait_ge(pool_step, 1)
            per = POOL_PREP + 4 * POOL_TURN
            with pool.Fori(0, LAYERS) as l:
                norm_rstd(l)
                pool.wait_ge(s_con, 16)
                steps.at(l * per + 1)
                pool.wait_ge(acc_act, l * ACC_ACT + (2 + 11))
                pool.wait_ge(acc_dve, l * ACC_DVE + (2 + 11))
                for i, col in enumerate((SK, KS, KW)):
                    rotate(k_shared[:, :, i, :], proj[:, :, col:col + P]).then_inc(keys_roped, 1)
                    pool.wait_ge(keys_roped, l * 3 + (i + 1))
                settle(pool)
                assert steps.n == POOL_PREP, steps.n
                with pool.Fori(0, 4) as j:
                    steps.at(l * per + j * POOL_TURN + (1 + POOL_PREP))
                    pool.wait_ge(acc_act, l * ACC_ACT + (2 + 13))
                    pool.wait_ge(acc_dve, l * ACC_DVE + (2 + 12))
                    pool.wait_ge(tq_done, l * 4 + j + ONE)
                    rotate(roped[:, 1, :, :], proj[:, :, bass.ds(j * P + MQ, P)]).then_inc(q_roped, 1)
                    pool.wait_ge(q_roped, (l * 4 + j) * 5 + 1)
                    rotate(roped[:, 2, :, :], proj[:, :, bass.ds(j * P + MK, P)]).then_inc(q_roped, 1)
                    pool.wait_ge(q_roped, (l * 4 + j) * 5 + 2)
                    rotate(roped[:, 3, :, :], proj[:, :, bass.ds(j * P + SQ, P)]).then_inc(q_roped, 1)
                    pool.wait_ge(q_roped, (l * 4 + j) * 5 + 3)
                    rotate(roped[:, 4, :, :], proj[:, :, bass.ds(j * P + NQ, P)]).then_inc(q_roped, 1)
                    pool.wait_ge(q_roped, (l * 4 + j) * 5 + 4)
                    for f, col in ((0, RQ), (1, RK)):
                        nc.gpsimd.tensor_copy(roped[:, 0, :, f * HD:(f + 1) * HD],
                                              proj[:, :, bass.ds(j * HD + col, HD)]).then_inc(pool_step, 1)
                        v = steps.next()
                    pool.wait_ge(pool_step, v)
                    rotate(roped[:, 0, :, :], roped[:, 0, :, :]).then_inc(q_roped, 1)
                    pool.wait_ge(q_roped, (l * 4 + j) * 5 + 5)
                    for n, b in enumerate((2, 0, 1, 3)):
                        pool.wait_ge(z_tanh, (l * 4 + j) * 4 + n + 1)
                        settle(pool)
                        nc.gpsimd.tensor_scalar(zg[:, b, :, :], zg[:, b, :, :], 1.0, 0.25, ALU.add,
                                                ALU.mult).then_inc(pool_step, 1)
                        pool.wait_ge(pool_step, steps.next())
                        nc.gpsimd.tensor_tensor(zg[:, b, :, :], zg[:, b, :, :], proj[:, :, bass.ds(j * P + ZCOL[b], P)],
                                                ALU.mult).then_inc(z_done, 1)
                        if n == 1:
                            pool.wait_ge(var_ret, l * 4 + j + 1)
                            nc.gpsimd.tensor_tensor(ret_st[:, 18:20], ret_st[:, 16:18], neg_half[:, :], ALU.pow
                                                    ).then_inc(rstd_ret, 1)
                    assert steps.n == POOL_TURN, steps.n
                for v in range(8):
                    c, i = divmod(v, 4)
                    if i == 0:
                        continue
                    m = c * 6 + (i - 1) * 2
                    if i == 1:
                        pool.wait_ge(first_part, l * 4 + c * 2 + 2)
                    for t in range(NT):
                        pool.wait_ge(part_full, l * 12 + (m + t + 1))
                        if i > 1:
                            pool.wait_ge(part_added, l * 12 + (m + t - 1 + ONE))
                        nc.gpsimd.tensor_tensor(merged[:, t, c * CW:(c + 1) * CW], merged[:, t, c * CW:(c + 1) * CW],
                                                part[:, t, :], ALU.add).then_inc(part_added, 1)
            norm_rstd(LAYERS)

        @block.scalar
        def _(act):
            def split_hi(n, pair, slot, l):
                act.wait_ge(raw_full[slot], (l * (UNITS // 2) + pair) * 16 + 16)
                act.wait_ge(w_used, l * UNITS + n + 1)
                nc.scalar.activation(w_hi[:, slot, :], raw[:, slot, :], ACT.Copy).then_inc(hi_done, 1)

            def unit_hi(n, l):
                if n in QUARTERED:
                    act.wait_ge(raw_full[n % 2], (l * (UNITS // 2) + n // 2) * 16 + 16)
                    act.wait_ge(w_used, l * UNITS + (n + 1))
                    for m in range(UNIT_K):
                        cols = slice(m * CW, (m + 1) * CW)
                        nc.scalar.activation(w_hi[:, n % 2, cols], raw[:, n % 2, cols], ACT.Copy
                                             ).then_inc(hi_quarter if m < UNIT_K - 1 else hi_done, 1)
                    return
                split_hi(n, n // 2, n % 2, l)

            def xgroup_hi(g, dst, l):
                act.wait_ge(x_full, l * 16 + (g + 1))
                nc.scalar.activation(dst, xbank[g % 4][:, :], ACT.Copy).then_inc(x_hi, 1)

            def squares(count):
                act.wait_ge(acc_dve, count * ACC_DVE + 2)
                for t in range(NT):
                    nc.scalar.activation(h[:, t, :], x_sb[:, t, :], ACT.Square,
                                         accum_out=small[:, t:t + 1]).then_inc(sq_done, 1)

            def columns_out(count, bank, cols):
                act.wait_ge(w_used, count)
                nc.scalar.activation(proj[:, 0, cols], acc[bank][:, :], ACT.Copy, scale=small[:, 4:5]).then_inc(acc_act, 1)

            act.sem_inc(acc_act, 2)
            for first in (t_free, exp_done):
                act.sem_inc(first, ONE)
            act.wait_ge(s_id, 16)
            nc.scalar.activation(act_warm[:, :], ident[:, 0:1], ACT.Tanh)
            act.wait_ge(s_x[0], 16)
            act.wait_ge(s_x[1], 16)
            with act.Fori(0, LAYERS) as l:
                def xgain_hi(g):
                    act.wait_ge(x_full, l * 16 + (g + 1))
                    for k in range(2):
                        ins = nc.scalar.activation(hT_hi[:, 2 * g + k, :], xbank[g][:, k * SEQ:(k + 1) * SEQ], ACT.Copy,
                                                   scale=g_now[:, 2 * g + k:2 * g + k + 1])
                    ins.then_inc(x_hi, 1)

                act.wait_ge(g_ready, l + 1)
                for n in range(2):
                    for m in range(UNIT_K):
                        if n == 0 and m % 2 == 0:
                            xgain_hi(m // 2)
                        if m == 0:
                            if n == 1:
                                xgain_hi(2)
                                xgain_hi(3)
                            act.wait_ge(raw_full[n], l * (UNITS // 2 * 16) + 16)
                            act.wait_ge(w_used, l * UNITS + (n + 1))
                        cols = slice(m * CW, (m + 1) * CW)
                        nc.scalar.activation(w_hi[:, n, cols], raw[:, n, cols], ACT.Copy
                                             ).then_inc(hi_quarter if m < UNIT_K - 1 else hi_done, 1)
                squares(l)
                unit_hi(2, l)
                unit_hi(3, l)
                act.wait_ge(rstd_norm, l + 1)
                columns_out(l * UNITS + (2 + 2), 0, slice(FIRST * CW, (FIRST + 1) * CW))
                with act.Fori(0, LOOPED // 2) as c:
                    for i in range(2):
                        for m in range(2):
                            n = c * 4 + (2 * i + m + 4)
                            split_hi(n, c * 2 + (i + 2), m, l)
                        columns_out(l * UNITS + c * 4 + (2 * i + 4 + 2), 2 - 2 * i,
                                    bass.ds(c * 2 * CW + i * CW, CW))
                act.wait_ge(s_tail, l * 16 + 16)
                nc.scalar.activation(t_parts[:, :, 0, :], t_raw[:, :, :], ACT.Copy)
                nc.scalar.activation(t_hl[:, KD * 2 * TAIL:], t_raw[:, :, :].rearrange("p k n -> p (k n)")[:, 0:P - 2 * TAIL],
                                     ACT.Copy).then_inc(tail_hi, 1)

                def late_out(place):
                    chunk = dict(LATE)[place]
                    columns_out(l * UNITS + (late_unit(chunk, 1) + 1 + 2), 2 * (place % 2), slice(chunk * CW, (chunk + 1) * CW))

                unit_hi(N_LATE + 2, l)
                unit_hi(N_LATE + 3, l)
                late_out(9)
                unit_hi(N_LATE + 4, l)
                unit_hi(N_LATE + 5, l)
                late_out(10)
                act.wait_ge(tail_done, l + 1)
                nc.scalar.activation(t_sum[:, :], acc[2][0:2 * TAIL, 0:SEQ], ACT.Copy).then_inc(acc_act, 1)
                for n in range(N_LATE + 6, N_LATE + 10):
                    unit_hi(n, l)
                late_out(11)
                for i in range(3):
                    act.wait_ge(keys_T, l * 3 + (i + 1))
                    nc.scalar.activation(kT_shared[:, i, :, :], xbank[i + 1][0:HD, :], ACT.Copy).then_inc(keys_out, 1)
                unit_hi(N_LATE + 10, l)
                unit_hi(N_LATE + 11, l)
                act.wait_ge(hid_sb, l + 1)
                nc.scalar.activation(hid3[:, :], hid2[:, :], ACT.Tanh, scale=0.7978845608028654).then_inc(hid_tanh, 1)
                unit_hi(N_MERGE, l)
                late_out(12)
                act.wait_ge(acc_act, l * ACC_ACT + (2 + 14))
                act.wait_ge(acc_dve, l * ACC_DVE + (2 + 14))
                nc.scalar.activation(nsa_g[:, :, :], proj[:, :, NG:NG + 24], ACT.Tanh, scale=0.5).then_inc(tail_tanh, 1)
                act.wait_ge(half_rstd, l + 1)
                with act.Fori(0, 4) as j:
                    turn = l * 4 + j

                    def t_out(f, dst, src, scale=1.0):
                        act.wait_ge(t_full, turn * T_FILLS + (f + 1 + ONE))
                        nc.scalar.activation(dst, src, ACT.Copy, scale=scale).then_inc(t_free, 1)

                    def gate_out(i):
                        act.wait_ge(w_used, l * UNITS + j * 4 + (N_MERGE + 2 * i + 2 + 2))
                        for t in range(NT):
                            ins = nc.scalar.activation(gates[:, t, bass.ds(j * 2 * CW + i * CW, CW)],
                                                       acc[2 * i + t][:, :], ACT.Tanh, scale=small[:, 6 + t:7 + t])
                        ins.then_inc(acc_act, 1)

                    for s in range(SLOTS + 1):
                        i = s // 4 + 1
                        if s % 4 == 0 and s < SLOTS:
                            act.wait_ge(raw_full[i % 2], (l * (UNITS // 2) + j * 2 + (N_MERGE + i) // 2) * 16 + 16)
                            act.wait_ge(w_used, l * UNITS + j * 4 + (N_MERGE + i + 1))
                        for m in (PIECES[s % 4] if s < SLOTS else ()):
                            nc.scalar.activation(w_hi[:, i % 2, m * CW:(m + 1) * CW], raw[:, i % 2, m * CW:(m + 1) * CW],
                                                 ACT.Copy).then_inc(hi_piece, 1)
                        if s < 5:
                            if s == 0:
                                act.wait_ge(t_full, turn * T_FILLS + (1 + ONE))
                                nc.scalar.activation(qkT[:, 0, 0, :], tbank[0:HD, 0:SEQ], ACT.Copy, scale=0.125)
                                nc.scalar.activation(qkT[:, 0, 1, :], tbank[0:HD, SEQ:2 * SEQ],
                                                     ACT.Copy).then_inc(t_free, 1)
                            else:
                                t_out(s, qkT[:, s, :, :], tbank[0:HD, :], 1.0 if s == 2 else 0.125)
                        if s == 2:
                            act.wait_ge(y_done, turn + ONE)
                            for b in (2, 0, 1, 3):
                                nc.scalar.activation(zg[:, b, :, :], proj[:, :, bass.ds(j * P + ZCOL[b], P)],
                                                     ACT.Tanh, scale=0.5).then_inc(z_tanh, 1)
                        k = s - S_AT
                        if k in SOFT:
                            e = SOFT[k]
                            act.wait_ge(max_done, turn * 8 + (e + 1))
                            act.wait_ge(t_full, turn * T_FILLS + ((SOFT_K[e - 2] + 5 if e > 1 else 0) + ONE))
                            for t, (a, b) in enumerate(((0, P), (P, 384))):
                                ins = nc.scalar.activation(probs[:, e % 2, a:b], score[k % 2][:, a:b], ACT.Exp,
                                                           bias=stat[:, e % 4, t:t + 1],
                                                           accum_out=stat[:, e % 4, 2 + t:3 + t])
                            ins.then_inc(exp_done, 1)
                            if ITEMS[k][0] == "swa":
                                nc.scalar.activation(stat[:, e % 4, 6:8], stat[:, e % 4, 4:6],
                                                     ACT.Exp).then_inc(sink_exp, 1)
                        elif 0 <= k < 10 and ITEMS[k][0] == "cmp":
                            act.wait_ge(cmp_sub, turn + 1)
                            nc.scalar.activation(cmp_s[:, :, :], cmp_s[:, :, :], ACT.Exp).then_inc(cmp_exp, 1)
                        k = s - P_AT
                        if 1 <= k < 10:
                            if k in SOFT:
                                t_out(4 + k, probsT[:, SOFT[k] % 2, :], tbank[:, 0:384])
                            else:
                                t_out(4 + k, cmp_pT[:, :], tbank[0:2 * NCMP, 0:SEQ])
                        if s == 8:
                            gate_out(0)
                        if s == SLOTS:
                            gate_out(1)
                for g in range(4):
                    xgroup_hi(4 + g, yT_hi[g][:, :, :], l)
                for v in range(8):
                    unit_hi(N_BRANCH + v + 1, l)
                    if v < 2:
                        for g in (4 + 2 * v, 5 + 2 * v):
                            xgroup_hi(4 + g, yT_hi[g][:, :, :], l)
                    if v == 5:
                        for g in range(2):
                            xgroup_hi(12 + g, hT_hi[:, 2 * g:2 * g + 2, :], l)
                unit_hi(N_OUT + 1, l)
                for g in range(2, 4):
                    xgroup_hi(12 + g, hT_hi[:, 2 * g:2 * g + 2, :], l)
                unit_hi(N_OUT + 2, l)
                unit_hi(N_OUT + 3, l)
            squares(LAYERS)

        @block.vector
        def _(dve):
            steps = Count()

            def chain(ins):
                ins.then_inc(dve_step, 1)
                return steps.next()

            def split_lo(parity, done):
                dve.wait_ge(hi_done, done)
                nc.vector.tensor_tensor(w_lo[:, parity, :], raw[:, parity, :], w_hi[:, parity, :].bitcast(F32),
                                        ALU.subtract).then_inc(lo_done, 1)

            def xgroup_lo(g, hi, lo, l):
                dve.wait_ge(x_hi, l * 16 + (g + 1))
                bank = xbank[g % 4][:, :].rearrange("p (k n) -> p k n", k=2)
                nc.vector.tensor_tensor(lo, bank, hi.bitcast(F32), ALU.subtract).then_inc(x_lo, 1)

            def mean_square(i):
                dve.wait_ge(sq_done, i * 2 + 2)
                nc.vector.tensor_scalar(small[:, 2:4], small[:, 0:2], 1.0 / D, EPS, ALU.mult,
                                        ALU.add).then_inc(var_norm, 1)
                dve.wait_ge(rstd_norm, i + 1)

            def columns_out(count, bank, cols):
                dve.wait_ge(w_used, count)
                nc.vector.tensor_scalar(proj[:, 1, cols], acc[bank][:, :], small[:, 5:6], None, ALU.mult).then_inc(acc_dve, 1)

            dve.sem_inc(lo_done, 2)
            for first in (x_lo, y_done, o_free):
                dve.sem_inc(first, ONE)
            dve.sem_inc(acc_dve, 2)
            dve.wait_ge(g_T, 1)
            nc.vector.tensor_copy(g_col[:, :], score[0][:, 0:LAYERS * KD]).then_inc(dve_step, 1)
            dve.wait_ge(dve_step, 1)
            per = DVE_PREP + 4 * DVE_TURN
            with dve.Fori(0, LAYERS) as l:
                def unit_lo(n):
                    if n not in QUARTERED:
                        split_lo(n % 2, l * WHOLE + (n + 1))
                        return
                    for m in range(UNIT_K):
                        if m < UNIT_K - 1:
                            dve.wait_ge(hi_quarter, quarters(l, n, m))
                        else:
                            dve.wait_ge(hi_done, l * WHOLE + (n + 1))
                        cols = slice(m * CW, (m + 1) * CW)
                        nc.vector.tensor_tensor(w_lo[:, n % 2, cols], raw[:, n % 2, cols],
                                                w_hi[:, n % 2, cols].bitcast(F32), ALU.subtract
                                                ).then_inc(lo_quarter if m < UNIT_K - 1 else lo_done, 1)

                nc.vector.tensor_copy(g_now[:, :], g_col[:, bass.ds(l * KD, KD)]).then_inc(g_ready, 1)
                dve.wait_ge(g_ready, l + 1)

                def xgain_lo(g):
                    dve.wait_ge(x_hi, l * 16 + (g + 1))
                    for k in range(2 * g, 2 * g + 2):
                        ins = nc.vector.scalar_tensor_tensor(hT_lo[:, k, :], xbank[g][:, k % 2 * SEQ:(k % 2 + 1) * SEQ],
                                                             g_now[:, k:k + 1], hT_hi[:, k, :].bitcast(F32), ALU.mult,
                                                             ALU.subtract)
                    ins.then_inc(x_lo, 1)

                for n in range(2):
                    for m in range(UNIT_K):
                        if n == 0 and m % 2 == 0:
                            xgain_lo(m // 2)
                        if n == 1 and m == 0:
                            xgain_lo(2)
                            xgain_lo(3)
                        if m < UNIT_K - 1:
                            dve.wait_ge(hi_quarter, quarters(l, n, m))
                        else:
                            dve.wait_ge(hi_done, l * WHOLE + (n + 1))
                        cols = slice(m * CW, (m + 1) * CW)
                        nc.vector.tensor_tensor(w_lo[:, n, cols], raw[:, n, cols], w_hi[:, n, cols].bitcast(F32),
                                                ALU.subtract).then_inc(lo_quarter if m < UNIT_K - 1 else lo_done, 1)
                mean_square(l)
                nc.vector.tensor_scalar(small[:, 6:8], small[:, 4:6], 0.5, None, ALU.mult).then_inc(half_rstd, 1)
                for n in (2, 3):
                    unit_lo(n)
                columns_out(l * UNITS + (2 + 2), 1, slice(FIRST * CW, (FIRST + 1) * CW))
                with dve.Fori(0, LOOPED // 2) as c:
                    for i in range(2):
                        for m in range(2):
                            split_lo(m, l * WHOLE + c * 4 + (2 * i + m + 5))
                        columns_out(l * UNITS + c * 4 + (2 * i + 4 + 2), 3 - 2 * i, bass.ds(c * 2 * CW + i * CW, CW))

                def late_out(place):
                    chunk = dict(LATE)[place]
                    columns_out(l * UNITS + (late_unit(chunk, 1) + 1 + 2), 2 * (place % 2) + 1,
                                slice(chunk * CW, (chunk + 1) * CW))

                steps.at(l * per + 1)
                dve.wait_ge(s_con, 16)
                dve.wait_ge(acc_act, l * ACC_ACT + (2 + 9))
                dve.wait_ge(acc_dve, l * ACC_DVE + (2 + 9))
                for a in range(2):
                    for t in range(NT):
                        ins = nc.vector.tensor_copy(dup[:, t, :, a, :],
                                                    proj[:, t, KC:KC + 2 * P].rearrange("p (s n) -> p s n", n=HD))
                ins.then_inc(dup_done, 1)
                for t, bank in enumerate((obank, tbank)):
                    dve.wait_ge(dup_T, l * 3 + (t + 1))
                    for odd in range(2):
                        rows = slice(odd * HD, (odd + 1) * HD)
                        v = chain(nc.vector.tensor_copy(
                            pairT[rows, :, t * HD:(t + 1) * HD],
                            bank[rows, :].rearrange("p (s n two) -> p s n two", s=4, two=2)[:, :, :, odd]))
                dve.wait_ge(dup_T, l * 3 + 3)
                v = chain(nc.vector.tensor_copy(posT[:, :], score[1][:, 0:16]))
                unit_lo(N_LATE + 2)
                dve.wait_ge(dve_step, v)
                for s in range(2):
                    for half in range(2):
                        src = pairT[:, 2 * s:2 * s + 2, :].rearrange("p v (n k) -> p k v n", k=8)[:, :, :, half:half + NCMP]
                        k0 = (2 * s + half) * 8
                        dst = blocksT[:, k0:k0 + 8, :].rearrange("p k (v n) -> p k v n", v=2)
                        pos = posT[:, half * 8:half * 8 + 8].unsqueeze(2).unsqueeze(3).to_broadcast([P, 8, 2, NCMP])
                        v = chain(nc.vector.tensor_tensor(dst, src, pos, ALU.add))
                parts = b_parts[:, 0:32 * 64].rearrange("p (k s n) -> p k s n", k=32, s=2)
                nc.vector.memset(b_parts[:, 32 * 64:33 * 64].bitcast(F32), 0.0)
                nc.vector.memset(parts[:, :, :, 2 * NCMP:32].bitcast(F32), 0.0)
                dve.wait_ge(dve_step, v)
                v = chain(nc.vector.tensor_copy(parts[:, :, 0, 0:2 * NCMP], blocksT[:, :, :]))
                dve.wait_ge(dve_step, v)
                nc.vector.tensor_tensor(parts[:, :, 1, 0:2 * NCMP], blocksT[:, :, :], parts[:, :, 0, 0:2 * NCMP].bitcast(F32),
                                        ALU.subtract).then_inc(blocks_done, 1)
                unit_lo(N_LATE + 3)
                late_out(9)
                dve.wait_ge(tail_hi, l + 1)
                nc.vector.tensor_tensor(t_parts[:, :, 1, :], t_raw[:, :, :], t_parts[:, :, 0, :].bitcast(F32),
                                        ALU.subtract).then_inc(tail_lo, 1)
                unit_lo(N_LATE + 4)
                unit_lo(N_LATE + 5)
                late_out(10)
                for n in range(N_LATE + 6, N_LATE + 10):
                    unit_lo(n)
                late_out(11)
                unit_lo(N_LATE + 10)
                dve.wait_ge(w_used, l * UNITS + (late_unit(None, 3) + 1 + 2))
                v = chain(nc.vector.tensor_copy(hid[:, :], score[0][0:2 * NCMP, :]))
                dve.wait_ge(dve_step, v)
                v = chain(nc.vector.tensor_tensor(hid[:, :], hid[:, :], score[0][32:32 + 2 * NCMP, :], ALU.add))
                dve.wait_ge(dve_step, v)
                v = chain(nc.vector.tensor_tensor(hid2[:, :], hid[:, :], hid[:, :], ALU.mult))
                dve.wait_ge(dve_step, v)
                v = chain(nc.vector.tensor_scalar(hid2[:, :], hid2[:, :], 0.044715, 1.0, ALU.mult, ALU.add))
                dve.wait_ge(dve_step, v)
                nc.vector.tensor_tensor(hid2[:, :], hid2[:, :], hid[:, :], ALU.mult).then_inc(hid_sb, 1)
                unit_lo(N_LATE + 11)
                dve.wait_ge(hid_tanh, l + 1)
                nc.vector.scalar_tensor_tensor(hid2[:, :], hid3[:, :], 1.0, hid[:, :], ALU.add,
                                               ALU.mult).then_inc(gelu_done, 1)
                dve.wait_ge(gelu_T, l + 1)
                gT = obank[:, :].rearrange("p (f n) -> p f n", f=4)
                nc.vector.tensor_copy(gkT[:, :, :], gT[:, 0:2, 0:2 * NCMP])
                for a in range(2):
                    ins = nc.vector.tensor_copy(gvT[:, :, :, a, :],
                                                gT[:, 2:4, 0:2 * NCMP].rearrange("p f (v n) -> p f v n", v=2))
                ins.then_inc(gelu_out, 1)
                unit_lo(N_MERGE)
                late_out(12)
                dve.wait_ge(cmp_kv, l + 1)
                v = chain(nc.vector.tensor_scalar(kc_s[:, :], score[0][0:2 * NCMP, 0:HD], 0.5, None, ALU.mult))
                for kv in range(2):
                    blk = con[0:2 * NCMP, C_BLK:C_BLK + 2].unsqueeze(2).to_broadcast([2 * NCMP, 2, HD])
                    val = score[1][0:2 * NCMP, kv * HD:(kv + 1) * HD].unsqueeze(1).to_broadcast([2 * NCMP, 2, HD])
                    last = chain(nc.vector.tensor_tensor(v_blk[:, kv, :].rearrange("p (a n) -> p a n", a=2), val, blk,
                                                         ALU.mult))
                dve.wait_ge(dve_step, v)
                sin = con[0:2 * NCMP, C_SINK:C_SINK + HD]
                chain(nc.vector.tensor_tensor(kc_t[:, 0:32], kc_s[:, 32:64], sin[:, 0:32], ALU.mult))
                chain(nc.vector.tensor_tensor(kc_t[:, 32:64], kc_s[:, 0:32], sin[:, 32:64], ALU.mult))
                v = chain(nc.vector.tensor_tensor(kc_r[:, :], kc_s[:, :], con[0:2 * NCMP, C_COSK:C_COSK + HD], ALU.mult))
                dve.wait_ge(dve_step, v)
                nc.vector.tensor_tensor(kc_r[:, :], kc_r[:, :], kc_t[:, :], ALU.add).then_inc(cmp_roped, 1)
                dve.wait_ge(tail_T, l + 1)
                parts = acc[3][:, 0:NT * 2 * TAIL].rearrange("p (t s n) -> p t s n", t=NT, s=2)
                v = chain(nc.vector.tensor_copy(t_cols[:, :, :], parts[:, :, 0, :]))
                dve.wait_ge(dve_step, v)
                v = chain(nc.vector.tensor_tensor(t_cols[:, :, :], t_cols[:, :, :], parts[:, :, 1, :], ALU.add))
                dve.wait_ge(dve_step, v)
                for t in range(NT):
                    ins = nc.vector.tensor_scalar(proj[:, t, CHUNKS * CW:MG], t_cols[:, t, :], small[:, 4 + t:5 + t], None,
                                                  ALU.mult)
                ins.then_inc(acc_dve, 1)
                dve.wait_ge(tail_tanh, l + 1)
                nc.vector.tensor_scalar(nsa_g[:, :, :], nsa_g[:, :, :], 1.0, 0.5, ALU.add, ALU.mult).then_inc(gates_nsa, 1)
                dve.wait_ge(kcT_full, l + 1)
                nc.vector.tensor_copy(kcT[:, :, :], score[1][0:HD, 0:2 * NCMP].rearrange("p (v n) -> p v n", v=2)
                                      ).then_inc(cmp_ready, 1)
                prep_n = steps.n
                dve.wait_ge(setup_done, 1)
                dve.wait_ge(gates_nsa, l + 1)
                with dve.Fori(0, 4) as j:
                    turn = l * 4 + j
                    steps.at(l * per + j * DVE_TURN + (1 + DVE_PREP))

                    def per_tile(col):
                        return con[:, col:col + 2 * NCMP].rearrange("p (t n) -> p t n", t=NT).unsqueeze(2
                            ).to_broadcast([P, NT, 2, NCMP])

                    def cmp_rest():
                        cs = cmp_s[:, :, :].rearrange("p (t a) n -> p t a n", t=NT)
                        dve.wait_ge(cmp_exp, turn + 1)
                        nc.vector.tensor_tensor(cs, cs, per_tile(C_C01), ALU.mult).then_inc(cmp_p, 1)
                        dve.wait_ge(cmp_p, turn + 1)
                        v = chain(nc.vector.tensor_reduce(cmp_st[:, :, 1], cmp_s[:, :, :], AX.X, ALU.add))
                        dve.wait_ge(dve_step, v)
                        v = chain(nc.vector.tensor_scalar(cmp_st[:, :, 2], cmp_st[:, :, 1], TINY, None, ALU.max))
                        dve.wait_ge(dve_step, v)
                        v = chain(nc.vector.reciprocal(cmp_st[:, :, 3], cmp_st[:, :, 2]))
                        dve.wait_ge(dve_step, v)
                        chain(nc.vector.tensor_tensor(
                            cmp_st[:, :, 2].rearrange("p (t a) -> p t a", t=NT),
                            cmp_st[:, :, 3].rearrange("p (t a) -> p t a", t=NT),
                            nsa_g[:, :, bass.ds(j * 2, 2)], ALU.mult))

                    def ret_rest():
                        dve.wait_ge(rstd_ret, turn + 1)
                        for t in range(NT):
                            v = chain(nc.vector.tensor_scalar(nsa_sum[:, t, :], nsa_sum[:, t, :],
                                                              ret_st[:, 12 + 2 * t:13 + 2 * t],
                                                              ret_st[:, 18 + t:19 + t], ALU.subtract, ALU.mult))
                        dve.wait_ge(dve_step, v)
                        dve.wait_ge(z_done, turn * 4 + 1)
                        chain(nc.vector.tensor_tensor(proj[:, :, bass.ds(j * P + RZ, P)], nsa_sum[:, :, :],
                                                      zg[:, 2, :, :], ALU.mult))

                    def scores_in(k):
                        kind, a = ITEMS[k]
                        bank = score[k % 2]
                        dve.wait_ge(s_full, turn * 10 + (k + 1))
                        if kind == "ret":
                            dve.wait_ge(o_full, turn * 10 + ONE)
                            nc.vector.tensor_tensor(attT[:, :], bank[:, 0:384],
                                                    con[:, bass.ds(j * 384 + C_DECAY, 384)], ALU.mult
                                                    ).then_inc(s_dve, 1)
                            return
                        if kind == "cmp":
                            sc = bank[:, 0:64].rearrange("p (t a n) -> p t a n", t=NT, a=2)[:, :, :, 0:NCMP]
                            cs = cmp_s[:, :, :].rearrange("p (t a) n -> p t a n", t=NT)
                            nc.vector.tensor_tensor(cs, sc, per_tile(C_CADD), ALU.add).then_inc(s_dve, 1)
                            dve.wait_ge(s_dve, turn * 2 + 2)
                            v = chain(nc.vector.tensor_reduce(cmp_st[:, :, 0], cmp_s[:, :, :], AX.X, ALU.max))
                            dve.wait_ge(dve_step, v)
                            nc.vector.tensor_tensor(cmp_s[:, :, :], cmp_s[:, :, :],
                                                    cmp_st[:, :, 0:1].to_broadcast([P, 4, NCMP]), ALU.subtract
                                                    ).then_inc(cmp_sub, 1)
                            return
                        e = SOFT[k]
                        st = stat[:, e % 4, :]
                        n_max = chain(nc.vector.tensor_reduce(st[:, 0:1], bank[:, 0:P], AX.X, ALU.max, negate=True))
                        if kind != "swa":
                            nc.vector.tensor_reduce(st[:, 1:2], bank[:, P:384], AX.X, ALU.max, negate=True
                                                    ).then_inc(max_done, 1)
                            return
                        v = chain(nc.vector.tensor_reduce(st[:, 1:2], bank[:, P:384], AX.X, ALU.max, negate=True))
                        dve.wait_ge(dve_step, v)
                        v = chain(nc.vector.tensor_tensor(st[:, 0:2], st[:, 0:2],
                                                          nsink[:, bass.ds(l * HEADS + j * 2 + a, 1), :].squeeze(1),
                                                          ALU.min))
                        dve.wait_ge(dve_step, v)
                        nc.vector.tensor_tensor(st[:, 4:6], st[:, 0:2],
                                                sink[:, bass.ds(l * HEADS + j * 2 + a, 1), :].squeeze(1), ALU.add
                                                ).then_inc(max_done, 1)

                    def outputs_in(k):
                        kind, a = ITEMS[k]
                        o = obank[:, 0:2 * P].rearrange("p (t n) -> p t n", t=NT)
                        hcols = slice(a * HD, (a + 1) * HD)
                        if kind == "ret":
                            dve.wait_ge(o_full, turn * 10 + (k + 1 + ONE))
                            nc.vector.tensor_copy(nsa_sum[:, :, :], o).then_inc(o_free, 1)
                            dve.wait_ge(o_free, turn * 10 + (k + 1 + ONE))
                            for t in range(NT):
                                v = chain(nc.vector.bn_stats(ret_st[:, 6 * t:6 * t + 6], nsa_sum[:, t, :]))
                            dve.wait_ge(dve_step, v)
                            settle(dve)
                            for t in range(NT):
                                v = chain(nc.vector.bn_aggr(ret_st[:, 12 + 2 * t:14 + 2 * t], ret_st[:, 6 * t:6 * t + 6]))
                            dve.wait_ge(dve_step, v)
                            nc.vector.tensor_scalar(ret_st[:, 16:18],
                                                    ret_st[:, 12:16].rearrange("p (t m) -> p t m", m=2)[:, :, 1],
                                                    EPS, None, ALU.add).then_inc(var_ret, 1)
                            return
                        if kind == "cmp":
                            dve.wait_ge(dve_step, steps.base + steps.n)
                            dve.wait_ge(o_full, turn * 10 + (k + 1 + ONE))
                            nc.vector.tensor_tensor(
                                nsa_sum[:, :, :].rearrange("p t (a n) -> p (t a) n", a=2),
                                obank[:, 0:2 * P].rearrange("p (t n) -> p t n", n=HD),
                                cmp_st[:, :, 2:3].to_broadcast([P, 4, HD]), ALU.mult).then_inc(o_free, 1)
                            return
                        e = SOFT[k]
                        st = stat[:, e % 4, :]
                        dve.wait_ge(exp_done, turn * 8 + (e + 1 + ONE))
                        if kind == "swa":
                            dve.wait_ge(sink_exp, turn * 2 + (a + 1))
                            v = chain(nc.vector.tensor_tensor(st[:, 2:4], st[:, 2:4], st[:, 6:8], ALU.add))
                            dve.wait_ge(dve_step, v)
                        v = chain(nc.vector.reciprocal(st[:, 8:10], st[:, 2:4]))
                        dve.wait_ge(dve_step, v)
                        if kind in ("moba", "swa"):
                            b = 0 if kind == "moba" else 1
                            dve.wait_ge(z_done, turn * 4 + (b + 2))
                            dve.wait_ge(o_full, turn * 10 + (k + 1 + ONE))
                            for t in range(NT):
                                ins = nc.vector.scalar_tensor_tensor(
                                    proj[:, t, bass.ds(j * P + (ZCOL[b] + a * HD), HD)], o[:, t, 0:HD], st[:, 8 + t:9 + t],
                                    zg[:, b, t, hcols], ALU.mult, ALU.mult)
                            ins.then_inc(o_free, 1)
                            return
                        g = 1 if kind == "slc" else 2
                        v = chain(nc.vector.tensor_tensor(st[:, 10:12], st[:, 8:10],
                                                          nsa_g[:, :, bass.ds(j * 2 + (g * HEADS + a), 1)].squeeze(2),
                                                          ALU.mult))
                        dve.wait_ge(dve_step, v)
                        dve.wait_ge(o_full, turn * 10 + (k + 1 + ONE))
                        dve.wait_ge(o_free, turn * 10 + (k + ONE))
                        for t in range(NT):
                            ins = nc.vector.scalar_tensor_tensor(nsa_sum[:, t, hcols], o[:, t, 0:HD], st[:, 10 + t:11 + t],
                                                                 nsa_sum[:, t, hcols], ALU.mult, ALU.add)
                        ins.then_inc(o_free, 1)
                        if kind == "win":
                            dve.wait_ge(o_free, turn * 10 + (k + 1 + ONE))
                            dve.wait_ge(z_done, turn * 4 + 4)
                            ins = nc.vector.tensor_tensor(proj[:, :, bass.ds(j * P + (NZ + a * HD), HD)],
                                                          nsa_sum[:, :, hcols], zg[:, 3, :, hcols], ALU.mult)
                            if a == 1:
                                ins.then_inc(y_done, 1)
                            else:
                                chain(ins)

                    for s in range(SLOTS):
                        if 0 <= s - S_AT < 10:
                            scores_in(s - S_AT)
                        if 0 <= s - O_AT < 10:
                            outputs_in(s - O_AT)
                        if s == S_AT + 3:
                            cmp_rest()
                        if s == O_AT + 1:
                            ret_rest()
                        i = s // 4 + 1
                        for m in PIECES[s % 4]:
                            dve.wait_ge(hi_piece, turn * SLOTS + (i - 1) * 4 + m + 1)
                            cols = slice(m * CW, (m + 1) * CW)
                            ins = nc.vector.tensor_tensor(w_lo[:, i % 2, cols], raw[:, i % 2, cols],
                                                          w_hi[:, i % 2, cols].bitcast(F32), ALU.subtract)
                            if m == UNIT_K - 1:
                                ins.then_inc(lo_done, 1)
                    turn_n = steps.n
                assert (prep_n, turn_n) == (DVE_PREP, DVE_TURN), (prep_n, turn_n)
                for g in range(4):
                    xgroup_lo(4 + g, yT_hi[g][:, :, :], yT_lo[g][:, :, :], l)
                for v in range(8):
                    c, i = divmod(v, 4)
                    split_lo((v + 1) % 2, l * WHOLE + (N_BRANCH + v + 2 - MIX_UNITS))
                    if v < 2:
                        for g in (4 + 2 * v, 5 + 2 * v):
                            xgroup_lo(4 + g, yT_hi[g][:, :, :], yT_lo[g][:, :, :], l)
                    dve.wait_ge(w_used, l * UNITS + (N_BRANCH + v + 1 + 2))
                    if i == 0:
                        dve.wait_ge(acc_act, l * ACC_ACT + (22 + 2))
                    for t in range(NT):
                        gate = gates[:, t, i * D + c * CW:i * D + (c + 1) * CW]
                        if i == 0:
                            ins = nc.vector.scalar_tensor_tensor(gate, gate, 1.0, acc[(v % 2) * 2 + t][:, :], ALU.add,
                                                                 ALU.mult)
                            ins.then_inc(first_part, 1)
                        else:
                            m = c * 6 + (i - 1) * 2 + t
                            dve.wait_ge(part_added, l * 12 + (max(m - 1, 0) + ONE))
                            nc.vector.scalar_tensor_tensor(part[:, t, :], gate, 1.0, acc[(v % 2) * 2 + t][:, :],
                                                           ALU.add, ALU.mult).then_inc(part_full, 1)
                    if v == 5:
                        for g in range(2):
                            xgroup_lo(12 + g, hT_hi[:, 2 * g:2 * g + 2, :], hT_lo[:, 2 * g:2 * g + 2, :], l)
                split_lo(1, l * WHOLE + (N_OUT + 2 - MIX_UNITS))
                for g in range(2, 4):
                    xgroup_lo(12 + g, hT_hi[:, 2 * g:2 * g + 2, :], hT_lo[:, 2 * g:2 * g + 2, :], l)
                split_lo(0, l * WHOLE + (N_OUT + 3 - MIX_UNITS))
                split_lo(1, l * WHOLE + (N_OUT + 4 - MIX_UNITS))
                for c in range(2):
                    dve.wait_ge(w_used, l * UNITS + (N_OUT + 2 + c + 1 + 2))
                    for t in range(NT):
                        cols = slice(c * CW, (c + 1) * CW)
                        ins = nc.vector.tensor_tensor(x_sb[:, t, cols], x_sb[:, t, cols], acc[2 * c + t][:, :], ALU.add)
                    ins.then_inc(acc_dve, 1)
            mean_square(LAYERS)
            dve.wait_ge(s_g_row, 16)
            for t in range(NT):
                nc.vector.scalar_tensor_tensor(h[:, t, :], x_sb[:, t, :], small[:, 4 + t:5 + t], g_row[:, :], ALU.mult,
                                               ALU.mult).then_inc(y_final, 1)

        @block.tensor
        def _(pe):
            def steps_of(hi, lo, k, unit, uk, banks, first, last):
                wh, wl = slot4(w_hi, unit)[:, uk, :], slot4(w_lo, unit)[:, uk, :]
                for t in range(NT):
                    o = acc[banks + t][:, :]
                    a, b = hi[:, k, t * P:(t + 1) * P], lo[:, k, t * P:(t + 1) * P]
                    nc.tensor.matmul(o, a, wl, start=first, stop=False)
                    nc.tensor.matmul(o, a, wh, start=False, stop=False)
                    ins = nc.tensor.matmul(o, b, wh, start=False, stop=last)
                return ins

            def unit_of(kh, unit, banks, done):
                pe.wait_ge(lo_done, done)
                for uk in range(UNIT_K):
                    ins = steps_of(hT_hi, hT_lo, kh * UNIT_K + uk, unit, uk, banks, kh == 0 and uk == 0,
                                   kh == 1 and uk == UNIT_K - 1)
                ins.then_inc(w_used, 1)

            def transposes(g, src):
                for k in range(2):
                    for t in range(NT):
                        ins = nc.tensor.transpose(xbank[g % 4][:, k * SEQ + t * P:k * SEQ + (t + 1) * P],
                                                  src(t, k), ident)
                ins.then_inc(x_full, 1)

            pe.sem_inc(w_used, 2)
            for first in (tq_done, t_full, o_full):
                pe.sem_inc(first, ONE)
            pe.wait_ge(s_id, 16)
            pe.wait_ge(s_g, 16)
            nc.tensor.transpose(score[0][:, 0:LAYERS * KD], g_in[:, :], ident[0:LAYERS * KD, 0:LAYERS * KD]).then_inc(g_T, 1)
            pe.wait_ge(g_ready, 1)
            pe.wait_ge(s_x[0], 16)
            pe.wait_ge(s_x[1], 16)
            with pe.Fori(0, LAYERS) as l:
                pe.wait_ge(x_lo, l * 16 + ONE)
                for g in range(4):
                    pe.wait_ge(acc_dve, l * ACC_DVE + (1 + g // 2))
                    transposes(g, lambda t, k: x_sb[:, t, (2 * g + k) * P:(2 * g + k + 1) * P])

                def wait_banks(q):
                    pe.wait_ge(acc_act, l * ACC_ACT + (q + 1))
                    pe.wait_ge(acc_dve, l * ACC_DVE + (q + 1))

                wait_banks(0)
                for n in range(2):
                    for uk in range(UNIT_K):
                        if uk < UNIT_K - 1:
                            pe.wait_ge(lo_quarter, quarters(l, n, uk))
                        else:
                            pe.wait_ge(lo_done, l * UNITS + (n + 1 + 2))
                        if uk % 2 == 0:
                            pe.wait_ge(x_lo, l * 16 + (2 * n + uk // 2 + 1 + ONE))
                        ins = steps_of(hT_hi, hT_lo, n * UNIT_K + uk, n, uk, 0, n == 0 and uk == 0,
                                       n == 1 and uk == UNIT_K - 1)
                    ins.then_inc(w_used, 1)
                settle(pe)
                with pe.Fori(0, LOOPED // 2) as c:
                    for i in range(2):
                        pe.wait_ge(acc_act, l * ACC_ACT + c * 2 + (i + 2))
                        pe.wait_ge(acc_dve, l * ACC_DVE + c * 2 + (i + 2))
                        for kh in range(2):
                            unit_of(kh, kh, 2 - 2 * i, l * UNITS + c * 4 + (2 * i + kh + 2 + 1 + 2))

                def late(chunk, half, from_=0, to=UNIT_K):
                    u, place = late_unit(chunk, half), {c: q for q, c in LATE}[chunk]
                    if half == 0 and from_ == 0:
                        wait_banks(place)
                    for uk in range(from_, to):
                        if u in QUARTERED and uk < UNIT_K - 1:
                            pe.wait_ge(lo_quarter, quarters(l, u, uk))
                        elif uk == 0 or u in QUARTERED:
                            pe.wait_ge(lo_done, l * UNITS + (u + 1 + 2))
                        ins = steps_of(hT_hi, hT_lo, half * UNIT_K + uk, u % 2, uk, 2 * (place % 2),
                                       half == 0 and uk == 0, half == 1 and uk == UNIT_K - 1)
                    if to == UNIT_K:
                        ins.then_inc(w_used, 1)

                def hidden(i):
                    u = late_unit(None, i)
                    pe.wait_ge(lo_done, l * UNITS + (u + 1 + 2))
                    out_ = score[0][:, i // 2 * 256:i // 2 * 256 + 256]
                    for k in range(8):
                        c0 = (i * 8 + k) * 64
                        for weights in (w_hi, w_lo):
                            ins = nc.tensor.matmul(out_, b_parts[:, c0:c0 + P], slot8(weights, u)[:, k, :],
                                                   start=(i % 2 == 0 and k == 0 and weights is w_hi),
                                                   stop=(i % 2 == 1 and k == 7 and weights is w_lo))
                    ins.then_inc(w_used, 1)

                late(8, 0)
                late(8, 1, 0, 1)
                pe.wait_ge(dup_done, l + 1)
                for t, bank in enumerate((obank, tbank)):
                    for s in range(4):
                        ins = nc.tensor.transpose(bank[:, s * P:(s + 1) * P],
                                                  dup[:, t, s, :, :].rearrange("p a n -> p (a n)"), ident)
                    ins.then_inc(dup_T, 1)
                pe.wait_ge(s_pos, l * 16 + 16)
                settle(pe)
                nc.tensor.transpose(score[1][:, 0:16], pos_in[:, :], ident[0:16, 0:16]).then_inc(dup_T, 1)
                late(8, 1, 1, 4)
                late(11, 0)
                pe.wait_ge(blocks_done, l + 1)
                hidden(0)
                late(11, 1)
                pe.wait_ge(acc_act, l * ACC_ACT + (2 + 10))
                pe.wait_ge(acc_dve, l * ACC_DVE + (2 + 10))
                pe.wait_ge(tail_lo, l + 1)
                for k in range(KD):
                    weights = t_hl[:, k * 2 * TAIL:k * 2 * TAIL + P]
                    nc.tensor.matmul(acc[2][:, 0:SEQ], weights, hT_hi[:, k, :], start=(k == 0), stop=False)
                    ins = nc.tensor.matmul(acc[2][:, 0:SEQ], weights, hT_lo[:, k, :], start=False, stop=(k == KD - 1))
                ins.then_inc(tail_done, 1)
                hidden(1)
                pe.wait_ge(acc_act, l * ACC_ACT + (2 + 12))
                late(9, 0)
                hidden(2)
                late(9, 1)
                pe.wait_ge(keys_roped, l * 3 + 3)
                settle(pe)
                for i in range(3):
                    for kv in range(2):
                        for t in range(NT):
                            ins = nc.tensor.transpose(xbank[i + 1][0:HD, kv * SEQ + t * P:kv * SEQ + (t + 1) * P],
                                                      k_shared[:, t, i, kv * HD:(kv + 1) * HD], ident)
                    ins.then_inc(keys_T, 1)
                hidden(3)
                late(12, 0)
                late(12, 1, 0, 2)
                pe.wait_ge(keys_out, l * 3 + 3)
                pe.wait_ge(gelu_done, l + 1)
                settle(pe)
                for f in range(4):
                    ins = nc.tensor.transpose(obank[:, f * P:f * P + 2 * NCMP], hid2[:, f * P:(f + 1) * P],
                                              ident[0:2 * NCMP, 0:2 * NCMP])
                ins.then_inc(gelu_T, 1)
                late(12, 1, 2, 4)
                pe.wait_ge(gelu_out, l + 1)
                pe.wait_ge(s_c2, l * 32 + 32)
                for f in range(2):
                    nc.tensor.matmul(score[0][0:2 * NCMP, 0:HD], gkT[:, f, :], w_c2[:, 0, f, :], start=(f == 0),
                                     stop=(f == 1))
                for kv in range(2):
                    for f in range(2):
                        ins = nc.tensor.matmul(score[1][0:2 * NCMP, kv * HD:(kv + 1) * HD],
                                               gvT[:, f, kv, :, :].rearrange("p a n -> p (a n)"), w_c2[:, 1, f, :],
                                               start=(f == 0), stop=(f == 1))
                ins.then_inc(cmp_kv, 1)
                pe.wait_ge(acc_act, l * ACC_ACT + (2 + 13))
                pe.wait_ge(acc_dve, l * ACC_DVE + (2 + 12))
                settle(pe)
                for t in range(NT):
                    ins = nc.tensor.transpose(acc[3][:, t * 2 * TAIL:(t + 1) * 2 * TAIL], t_sum[:, t * P:(t + 1) * P],
                                              ident[0:2 * TAIL, 0:2 * TAIL])
                ins.then_inc(tail_T, 1)
                pe.wait_ge(cmp_roped, l + 1)
                settle(pe)
                nc.tensor.transpose(score[1][0:HD, 0:2 * NCMP], kc_r[:, :], ident[0:2 * NCMP, 0:2 * NCMP]).then_inc(kcT_full, 1)
                pe.wait_ge(acc_act, l * ACC_ACT + (2 + 14))
                pe.wait_ge(setup_done, 1)
                settle(pe)
                with pe.Fori(0, 4) as j:
                    turn = l * 4 + j

                    def heads_T(f):
                        pe.wait_ge(t_free, turn * T_FILLS + (f + ONE))
                        settle(pe)
                        for a in range(2):
                            for t in range(NT):
                                ins = nc.tensor.transpose(tbank[0:HD, a * SEQ + t * P:a * SEQ + (t + 1) * P],
                                                          roped[:, f, t, a * HD:(a + 1) * HD], ident)
                        ins.then_inc(t_full, 1)

                    def scores_of(k):
                        kind, a = ITEMS[k]
                        bank = score[k % 2]
                        if k < 2:
                            pe.wait_ge(exp_done, turn * 8 + ONE)
                            if k == 1:
                                pe.wait_ge(cmp_ready, l + 1)
                        elif k - 2 in SOFT:
                            pe.wait_ge(exp_done, turn * 8 + (SOFT[k - 2] + 1 + ONE))
                        else:
                            pe.wait_ge(s_dve, turn * 2 + (1 if k == 2 else 2))
                        if kind == "ret":
                            pe.wait_ge(t_free, turn * T_FILLS + (1 + ONE))
                            nc.tensor.matmul(bank[:, 0:SEQ], qkT[:, 0, 1, 0:P], qkT[:, 0, 0, :], start=True, stop=True)
                            nc.tensor.matmul(bank[:, SEQ:384], qkT[:, 0, 1, P:SEQ], qkT[:, 0, 0, P:SEQ], start=True,
                                             stop=True).then_inc(s_full, 1)
                            return
                        if kind == "cmp":
                            pe.wait_ge(t_free, turn * T_FILLS + (5 + ONE))
                            for t in range(NT):
                                for b in range(2):
                                    o = (t * 2 + b) * 16
                                    ins = nc.tensor.matmul(bank[:, o:o + NCMP], qkT[:, 4, b, t * P:(t + 1) * P],
                                                           kcT[:, bass.ds(j // 2, 1), :].squeeze(1), start=True, stop=True)
                            ins.then_inc(s_full, 1)
                            return
                        pe.wait_ge(t_free, turn * T_FILLS + ((3 if kind == "moba" else KIND[kind] + 1) + ONE))
                        ins = nc.tensor.matmul(bank[:, 0:384], ident_b[:, :], mask_b[:, int(kind == "swa"), :],
                                               start=True, stop=False)
                        if k == 1:
                            ins.then_inc(tq_done, 1)
                        for t, (c0, c1, n) in enumerate(((0, P, P), (P, 384, SEQ))):
                            keys = qkT[:, 2, a, 0:n] if kind == "moba" else \
                                kT_shared[:, KEYS[kind], bass.ds(j // 2, 1), 0:n].squeeze(1)
                            ins = nc.tensor.matmul(bank[:, c0:c1], qkT[:, KIND[kind], a, t * P:(t + 1) * P], keys,
                                                   start=False, stop=(t == 1))
                        ins.then_inc(s_full, 1)

                    def probs_T(k):
                        pe.wait_ge(t_free, turn * T_FILLS + (4 + k + ONE))
                        if k in SOFT:
                            e = SOFT[k]
                            pe.wait_ge(exp_done, turn * 8 + (e + 1 + ONE))
                            for i in range(3):
                                ins = nc.tensor.transpose(tbank[:, i * P:(i + 1) * P], probs[:, e % 2, i * P:(i + 1) * P],
                                                          ident)
                            ins.then_inc(t_full, 1)
                            return
                        pe.wait_ge(cmp_p, turn + 1)
                        for t in range(NT):
                            ins = nc.tensor.transpose(tbank[0:2 * NCMP, t * P:(t + 1) * P],
                                                      cmp_s[:, 2 * t:2 * t + 2, :].rearrange("p a n -> p (a n)"), ident)
                        ins.then_inc(t_full, 1)

                    def outputs_of(k):
                        kind, a = ITEMS[k]
                        pe.wait_ge(o_free, turn * 10 + (k + ONE))
                        if kind == "cmp":
                            pe.wait_ge(t_free, turn * T_FILLS + (5 + k + ONE))
                            for t in range(NT):
                                ins = nc.tensor.matmul(obank[:, t * P:(t + 1) * P], cmp_pT[:, t * P:(t + 1) * P],
                                                       v_blk[:, bass.ds(j // 2, 1), :].squeeze(1), start=True, stop=True)
                            ins.then_inc(o_full, 1)
                            return
                        if kind == "ret":
                            pe.wait_ge(s_dve, turn * 2 + 1)
                            left, n = attT[:, :], P
                            vcol = bass.ds(j * P + RV, P)
                        else:
                            pe.wait_ge(t_free, turn * T_FILLS + (5 + k + ONE))
                            left, n = probsT[:, SOFT[k] % 2, :], HD
                            vcol = bass.ds(j * P + (MV + a * HD), HD) if kind == "moba" else \
                                bass.ds(j // 2 * HD + VCOL[kind], HD)
                        nc.tensor.matmul(obank[:, 0:n], left[:, 0:P], proj[:, 0, vcol], start=True, stop=True)
                        nc.tensor.matmul(obank[:, P:P + n], left[:, P:2 * P], proj[:, 0, vcol], start=True, stop=False)
                        nc.tensor.matmul(obank[:, P:P + n], left[:, 2 * P:3 * P], proj[:, 1, vcol], start=False,
                                         stop=True).then_inc(o_full, 1)

                    for s in range(SLOTS):
                        i, uk = divmod(s, UNIT_K)
                        if s % 8 == 0:
                            pe.wait_ge(acc_act, l * ACC_ACT + j * 2 + (14 + s // 8 + 1))
                            pe.wait_ge(acc_dve, l * ACC_DVE + (2 + 13 + s // 8))
                        if uk == 0:
                            pe.wait_ge(lo_done, l * UNITS + j * 4 + (N_MERGE + i + 1 + 2))
                        ins = steps_of(hT_hi, hT_lo, s % 8, i % 2, uk, 2 * (s // 8), s % 8 == 0, s % 8 == 7)
                        if uk == UNIT_K - 1:
                            ins.then_inc(w_used, 1)
                        if s == 0:
                            pe.wait_ge(q_roped, turn * 5 + 5)
                        if s < 5:
                            heads_T(s)
                        if 0 <= s - S_AT < 10:
                            scores_of(s - S_AT)
                        if 1 <= s - P_AT < 10:
                            probs_T(s - P_AT)
                        if 0 <= s - O_AT < 10:
                            outputs_of(s - O_AT)
                def outputs_T(g):
                    b, pair = divmod(g, 2)
                    if g >= 4:
                        pe.wait_ge(x_lo, l * 16 + (g + 1 + ONE))
                    transposes(4 + g, lambda t, k: proj[:, t, ZCOL[b] + (2 * pair + k) * P:ZCOL[b] + (2 * pair + k + 1) * P])

                def merged_T(g):
                    pe.wait_ge(x_lo, l * 16 + (12 + ONE))
                    transposes(12 + g, lambda t, k: merged[:, t, (2 * g + k) * P:(2 * g + k + 1) * P])

                pe.wait_ge(exp_done, l * 32 + (32 + ONE))
                outputs_T(0)
                outputs_T(1)
                pe.wait_ge(y_done, l * 4 + (4 + ONE))
                pe.wait_ge(t_free, l * 4 * T_FILLS + (4 * T_FILLS + ONE))
                outputs_T(2)
                outputs_T(3)
                for v in range(8):
                    c, i = divmod(v, 4)
                    pe.wait_ge(x_lo, l * 16 + (4 + min(2 * v + 2, 8) + ONE))
                    if v < 2:
                        pe.wait_ge(acc_act, l * ACC_ACT + (23 + v))
                    elif (v - 2) % 4 == 0:
                        pe.wait_ge(first_part, l * 4 + ((v - 2) // 4 * 2 + 2))
                    else:
                        pe.wait_ge(part_full, l * 12 + ((v - 2) // 4 * 6 + (v - 2) % 4 * 2))
                    pe.wait_ge(lo_done, l * UNITS + (N_BRANCH + v + 1 + 2))
                    for uk in range(UNIT_K):
                        g = 2 * i + uk // 2
                        ins = steps_of(yT_hi[g], yT_lo[g], uk % 2, v % 2, uk, (v % 2) * 2, uk == 0, uk == UNIT_K - 1)
                    ins.then_inc(w_used, 1)
                    if v < 2:
                        outputs_T(4 + 2 * v)
                        outputs_T(5 + 2 * v)
                    if v == 4:
                        pe.wait_ge(part_added, l * 12 + (6 + ONE))
                        merged_T(0)
                        merged_T(1)
                for v in range(4):
                    kh, c = divmod(v, 2)
                    pe.wait_ge(x_lo, l * 16 + ((14 if kh == 0 else 16) + ONE))
                    pe.wait_ge(lo_done, l * UNITS + (N_OUT + v + 1 + 2))
                    for uk in range(UNIT_K):
                        k = kh * UNIT_K + uk
                        ins = steps_of(hT_hi, hT_lo, k, v % 2, uk, 2 * c, k == 0, k == KD - 1)
                    ins.then_inc(w_used, 1)
                    if v == 0:
                        pe.wait_ge(part_added, l * 12 + (12 + ONE))
                        merged_T(2)
                        merged_T(3)


_INS = ["x", "norm_g", "w_in", "w_branch", "w_out", "swa_sink", "nsa_cmp_pos", "nsa_w_ck1", "nsa_w_ck2",
        "nsa_w_cv1", "nsa_w_cv2", "final_norm_g"]


def constant_arrays():
    import numpy as np
    f = np.float32
    inv = (f(1.0) / f(10000.0) ** (np.arange(0, HD, 2, dtype=f) / f(HD))).astype(f)
    ang = np.arange(SEQ, dtype=f)[:, None] * inv[None, :]
    cos, sin = np.cos(ang).astype(f), np.sin(ang).astype(f)
    cos2, sin2 = np.concatenate([cos, cos], 1), np.concatenate([-sin, sin], 1)
    c = np.zeros((P, N_CONST), f)
    c[:, C_ID:C_ID + P] = np.eye(P, dtype=f)
    for t in range(NT):
        for a in range(2):
            o = t * P + a * HD
            c[:, C_COS + o:C_COS + o + HD] = cos2[t * P:(t + 1) * P]
            c[:, C_SIN + o:C_SIN + o + HD] = sin2[t * P:(t + 1) * P]
    row = np.arange(P)
    for h in range(4):
        log_g = np.log(f(1.0) - f(2.0) ** f(-5.0 - h)).astype(f)
        for i, (k0, q0, n) in enumerate(((0, 0, 2 * P), (P, P, P))):
            diff = (q0 + np.arange(n))[None, :] - (k0 + row)[:, None]
            o = C_DECAY + h * 384 + i * 2 * P
            c[:, o:o + n] = np.where(diff >= 0, np.exp(np.maximum(diff, 0).astype(f) * log_g), 0.0)
    end = np.arange(NCMP) * 16 + 31
    for t in range(NT):
        ok = end[None, :] <= (t * P + row)[:, None]
        c[:, C_CADD + t * NCMP:C_CADD + (t + 1) * NCMP] = np.where(ok, 0.0, -1e30)
        c[:, C_C01 + t * NCMP:C_C01 + (t + 1) * NCMP] = ok
    for a in range(2):
        c[a * NCMP:(a + 1) * NCMP, C_BLK + a] = 0.5
        c[a * NCMP:(a + 1) * NCMP, C_COSK:C_COSK + HD] = cos2[end]
        c[a * NCMP:(a + 1) * NCMP, C_SINK:C_SINK + HD] = sin2[end]
    m = np.zeros((P, 2, 384), f)
    for i, (q0, k0) in enumerate(((0, 0), (P, 0), (P, P))):
        dist = (q0 + row)[:, None] - (k0 + row)[None, :]
        m[:, 0, i * P:(i + 1) * P] = np.where(dist >= 0, 0.0, -1e30)
        m[:, 1, i * P:(i + 1) * P] = np.where((dist >= 0) & (dist < 128), 0.0, -1e30)
    return c, m.reshape(P, 768)


def kernel(**inputs):
    import numpy as np
    import concourse.bacc as bacc
    from concourse.bass_utils import run_bass_kernel_spmd

    nc = bacc.Bacc("TRN2", target_bir_lowering=False, num_devices=1)
    consts, masks = constant_arrays()
    arrays, args = {}, []
    for name, a in [(n, np.ascontiguousarray(inputs[n])) for n in _INS] + [("consts", consts), ("masks", masks)]:
        arrays[f"in_{name}_dram"] = a
        args.append(nc.dram_tensor(f"in_{name}_dram", a.shape, mybir.dt.from_np(a.dtype), kind="ExternalInput").ap())
    args.append(nc.dram_tensor("out_dram", (1, SEQ, D), F32, kind="ExternalOutput").ap())
    hybrid_trunk(nc, *args)
    r = run_bass_kernel_spmd(nc, [arrays], core_ids=[0])
    return r.results[0]["out_dram"]
```
